# Optimizing a Trainium2 kernel written in Bass

```python
import jax, jax.numpy as jnp
from jax import lax
import numpy as np
import math

D_MODEL = 1024
BATCH = 1
SEQ = 256
DEPTH = 1

ML_HEADS = 4
ML_HEAD_DIM = 256
ML_W = ML_HEADS * ML_HEAD_DIM
ML_CHUNK = 64
SC_W = D_MODEL
CONV_K = 3
SB_HEADS = 16
SB_HEAD_DIM = 64
SB_W = SB_HEADS * SB_HEAD_DIM
SB_BLOCK = 128
N_BRANCH = 3
D_FF = 4 * D_MODEL
EPS = 1e-6
SPLIT_SIZES = (ML_W, ML_W, ML_W, ML_W, ML_HEADS, ML_HEADS,
               SC_W, SC_W, SC_W,
               SB_W, SB_W, SB_W,
               D_MODEL, D_MODEL, D_MODEL)
N_IN = sum(SPLIT_SIZES)


def rmsnorm(x, g):
    xf = x.astype(jnp.float32)
    y = xf * lax.rsqrt(jnp.mean(xf * xf, axis=-1, keepdims=True) + EPS)
    return (y * g.astype(jnp.float32)).astype(x.dtype)

def _to_chunks(a, nc, L):
    a = a.reshape((a.shape[0], nc, L) + a.shape[2:])
    return jnp.swapaxes(jnp.moveaxis(a, 1, 0), 2, 3)

def mlstm(q, k, v, i_pre, f_pre):
    B_, S_, H, dh = q.shape
    L = ML_CHUNK
    nc = S_ // L
    f32 = jnp.float32
    qc = _to_chunks(q.astype(f32), nc, L)
    kc = _to_chunks(k.astype(f32) * (dh ** -0.5), nc, L)
    vc = _to_chunks(v.astype(f32), nc, L)
    ic = _to_chunks(i_pre.astype(f32), nc, L)
    lfc = _to_chunks(jax.nn.log_sigmoid(f_pre.astype(f32)), nc, L)
    causal = jnp.tril(jnp.ones((L, L), dtype=bool))

    def step(carry, xs):
        C, n, m = carry
        qb, kb, vb, ib, lfb = xs
        b = jnp.cumsum(lfb, axis=-1)
        dmat = b[..., :, None] - b[..., None, :] + ib[..., None, :]
        dmat = jnp.where(causal, dmat, -jnp.inf)
        inter = b + m[..., None]
        m_t = jnp.maximum(inter, jnp.max(dmat, axis=-1))
        w_intra = jnp.exp(dmat - m_t[..., None])
        a_inter = jnp.exp(inter - m_t)
        s = jnp.einsum('bhtd,bhsd->bhts', qb, kb) * w_intra
        num = (jnp.einsum('bhts,bhsd->bhtd', s, vb)
               + a_inter[..., None] * jnp.einsum('bhvk,bhtk->bhtv', C, qb))
        den = jnp.sum(s, axis=-1) + a_inter * jnp.einsum('bhk,bhtk->bht', n, qb)
        h = num / jnp.maximum(jnp.abs(den), jnp.exp(-m_t))[..., None]
        b_last = b[..., -1]
        g = b_last[..., None] - b + ib
        m_new = jnp.maximum(b_last + m, jnp.max(g, axis=-1))
        decay = jnp.exp(b_last + m - m_new)
        w_state = jnp.exp(g - m_new[..., None])
        C_new = decay[..., None, None] * C + jnp.einsum('bhs,bhsv,bhsk->bhvk', w_state, vb, kb)
        n_new = decay[..., None] * n + jnp.einsum('bhs,bhsk->bhk', w_state, kb)
        return (C_new, n_new, m_new), h

    init = (jnp.zeros((B_, H, dh, dh), f32), jnp.zeros((B_, H, dh), f32), jnp.zeros((B_, H), f32))
    _, hs = lax.scan(step, init, (qc, kc, vc, ic, lfc))
    hs = jnp.moveaxis(jnp.swapaxes(hs, 2, 3), 0, 1)
    return hs.reshape(B_, S_, H, dh)

def short_conv(gate_b, gate_c, u, w):
    z = gate_c * u
    y = lax.conv_general_dilated(
        z, w[:, None, :].astype(z.dtype), window_strides=(1,),
        padding=[(CONV_K - 1, 0)], dimension_numbers=('NWC', 'WIO', 'NWC'),
        feature_group_count=z.shape[-1])
    return gate_b * y

def stick_breaking(q, k, v):
    B_, S_, H, d = q.shape
    nb = S_ // SB_BLOCK
    f32 = jnp.float32
    qf = q.astype(f32) * (d ** -0.5)
    kf = k.astype(f32)
    vf = v.astype(f32)
    q_blocks = jnp.transpose(qf.reshape(B_, nb, SB_BLOCK, H, d), (1, 0, 3, 2, 4))
    starts = jnp.arange(nb, dtype=jnp.int32) * SB_BLOCK
    key_pos = jnp.arange(S_, dtype=jnp.int32)

    def block(args):
        qblk, start = args
        q_pos = start + jnp.arange(SB_BLOCK, dtype=jnp.int32)
        mask = key_pos[None, :] < q_pos[:, None]
        z = jnp.einsum('bhqd,bshd->bhqs', qblk, kf)
        log_beta = jax.nn.log_sigmoid(z)
        log_1m = jnp.where(mask, log_beta - z, 0.0)
        cum = jnp.cumsum(log_1m, axis=-1)
        log_a = log_beta + cum[..., -1:] - cum
        a = jnp.where(mask, jnp.exp(log_a), 0.0)
        return jnp.einsum('bhqs,bshd->bqhd', a, vf)

    out = lax.map(block, (q_blocks, starts))
    return jnp.moveaxis(out, 0, 1).reshape(B_, S_, H * d)

def head_rmsnorm(h, g, n_heads):
    B_, S_, W = h.shape
    hh = h.reshape(B_, S_, n_heads, W // n_heads)
    hh = hh * lax.rsqrt(jnp.mean(hh * hh, axis=-1, keepdims=True) + EPS)
    return hh.reshape(B_, S_, W) * g.astype(jnp.float32)

def first_inputs(seed: int = 0) -> dict:
    key = jax.random.key(seed)
    ks = jax.random.split(key, 16)
    nrm = jax.random.normal
    x = nrm(ks[0], (BATCH, SEQ, D_MODEL), jnp.float32)
    norm_mix_g = 1.0 + 0.02 * nrm(ks[1], (DEPTH, D_MODEL), jnp.float32)
    w_in = nrm(ks[2], (DEPTH, D_MODEL, N_IN), jnp.float32) * D_MODEL ** -0.5
    b_if = jnp.concatenate([
        0.1 * nrm(ks[3], (DEPTH, ML_HEADS), jnp.float32),
        jnp.linspace(3.0, 6.0, ML_HEADS, dtype=jnp.float32)[None, :]
        + 0.1 * nrm(ks[4], (DEPTH, ML_HEADS), jnp.float32)], axis=-1)
    ml_norm_g = 1.0 + 0.02 * nrm(ks[5], (DEPTH, ML_W), jnp.float32)
    conv_w = nrm(ks[6], (DEPTH, CONV_K, SC_W), jnp.float32) * CONV_K ** -0.5
    w_ml_proj = nrm(ks[7], (DEPTH, ML_W, D_MODEL), jnp.float32) * ML_W ** -0.5
    w_sc_proj = nrm(ks[8], (DEPTH, SC_W, D_MODEL), jnp.float32) * SC_W ** -0.5
    w_sb_proj = nrm(ks[9], (DEPTH, SB_W, D_MODEL), jnp.float32) * SB_W ** -0.5
    w_out = nrm(ks[10], (DEPTH, D_MODEL, D_MODEL), jnp.float32) * D_MODEL ** -0.5
    norm_mlp_g = 1.0 + 0.02 * nrm(ks[11], (DEPTH, D_MODEL), jnp.float32)
    w_up = nrm(ks[12], (DEPTH, D_MODEL, D_FF), jnp.float32) * D_MODEL ** -0.5
    w_down = nrm(ks[13], (DEPTH, D_FF, D_MODEL), jnp.float32) * D_FF ** -0.5
    norm_final_g = 1.0 + 0.02 * nrm(ks[14], (D_MODEL,), jnp.float32)
    return {"x": x, "norm_mix_g": norm_mix_g, "w_in": w_in, "b_if": b_if,
            "ml_norm_g": ml_norm_g, "conv_w": conv_w, "w_ml_proj": w_ml_proj,
            "w_sc_proj": w_sc_proj, "w_sb_proj": w_sb_proj, "w_out": w_out,
            "norm_mlp_g": norm_mlp_g, "w_up": w_up, "w_down": w_down,
            "norm_final_g": norm_final_g}

def first_block(x, norm_mix_g, w_in, b_if, ml_norm_g, conv_w, w_ml_proj, w_sc_proj,
              w_sb_proj, w_out, norm_mlp_g, w_up, w_down, norm_final_g):
    B_, S_, _ = x.shape
    offsets = []
    acc = 0
    for sz in SPLIT_SIZES[:-1]:
        acc += sz
        offsets.append(acc)
    for l in range(DEPTH):
        h = rmsnorm(x, norm_mix_g[l])
        proj = h @ w_in[l]
        (ml_q, ml_k, ml_v, ml_o, ml_i, ml_f,
         sc_b, sc_c, sc_u,
         sb_q, sb_k, sb_v,
         g_ml, g_sc, g_sb) = jnp.split(proj, offsets, axis=-1)
        i_pre = ml_i + b_if[l, :ML_HEADS]
        f_pre = ml_f + b_if[l, ML_HEADS:]
        h_tilde = mlstm(ml_q.reshape(B_, S_, ML_HEADS, ML_HEAD_DIM),
                        ml_k.reshape(B_, S_, ML_HEADS, ML_HEAD_DIM),
                        ml_v.reshape(B_, S_, ML_HEADS, ML_HEAD_DIM),
                        i_pre, f_pre).reshape(B_, S_, ML_W)
        y_ml = head_rmsnorm(jax.nn.sigmoid(ml_o.astype(jnp.float32)) * h_tilde,
                            ml_norm_g[l], ML_HEADS).astype(x.dtype)
        y_sc = short_conv(sc_b, sc_c, sc_u, conv_w[l])
        y_sb = stick_breaking(sb_q.reshape(B_, S_, SB_HEADS, SB_HEAD_DIM),
                              sb_k.reshape(B_, S_, SB_HEADS, SB_HEAD_DIM),
                              sb_v.reshape(B_, S_, SB_HEADS, SB_HEAD_DIM)).astype(x.dtype)
        merged = (jax.nn.sigmoid(g_ml) * (y_ml @ w_ml_proj[l])
                  + jax.nn.sigmoid(g_sc) * (y_sc @ w_sc_proj[l])
                  + jax.nn.sigmoid(g_sb) * (y_sb @ w_sb_proj[l]))
        x = x + merged @ w_out[l]
        h2 = rmsnorm(x, norm_mlp_g[l])
        x = x + jnp.square(jax.nn.relu(h2 @ w_up[l])) @ w_down[l]
    return rmsnorm(x, norm_final_g)


LRU_WIDTH = D_MODEL // 4
LRU_BLOCKS = 4
LRU_BLOCK_W = LRU_WIDTH // LRU_BLOCKS
LRU_CONV = 4
LRU_C = 8.0
GLA_HEADS = 4
GLA_DV = (D_MODEL // 4) // GLA_HEADS
GLA_DK = GLA_DV // 2
GLA_GATE_RANK = 16
GLA_TAU = 16.0
GLA_CHUNK = 64
MOBA_HEADS = 8
MOBA_DH = (D_MODEL // 2) // MOBA_HEADS
MOBA_BLOCK = 256
MOBA_TOPK = 3
MOBA_Q_CHUNK = 128
REL_BUCKETS = 32
REL_MAX_DIST = 128
D_FF_2 = -(-8 * D_MODEL // (3 * 256)) * 256

GLA_QK_W = GLA_HEADS * GLA_DK
GLA_V_W = GLA_HEADS * GLA_DV
MOBA_W = MOBA_HEADS * MOBA_DH
D_MIX = LRU_WIDTH + GLA_V_W + MOBA_W
IN_SPLITS = (LRU_WIDTH, LRU_WIDTH, GLA_QK_W, GLA_QK_W, GLA_V_W, GLA_GATE_RANK, GLA_V_W, MOBA_W, MOBA_W, MOBA_W)
D_IN = sum(IN_SPLITS)
RMS_EPS = 1e-6
NEG_INF = -1e30


def rms_norm(x, g):
    xf = x.astype(jnp.float32)
    y = xf * lax.rsqrt(jnp.mean(xf * xf, axis=-1, keepdims=True) + RMS_EPS)
    return (y * g.astype(jnp.float32)).astype(x.dtype)

def split_heads(t, n):
    b, s, w = t.shape
    return t.astype(jnp.float32).reshape(b, s, n, w // n).transpose(0, 2, 1, 3)

def t5_bucket(rel):
    n = jnp.maximum(rel, 0)
    max_exact = REL_BUCKETS // 2
    nf = jnp.maximum(n, 1).astype(jnp.float32)
    large = max_exact + (jnp.log(nf / max_exact) / math.log(REL_MAX_DIST / max_exact)
                         * (REL_BUCKETS - max_exact)).astype(jnp.int32)
    large = jnp.minimum(large, REL_BUCKETS - 1)
    return jnp.where(n < max_exact, n, large)

def rg_lru_branch(xb, gb, conv_w, conv_b, wa, ba, wx, bx, lam):
    b, s, c = xb.shape
    xc = lax.conv_general_dilated(xb, conv_w[:, None, :].astype(xb.dtype), window_strides=(1,),
                                  padding=[(LRU_CONV - 1, 0)],
                                  dimension_numbers=('NWC', 'WIO', 'NWC'),
                                  feature_group_count=c)
    xc = xc.astype(jnp.float32) + conv_b.astype(jnp.float32)
    xg = xc.reshape(b, s, LRU_BLOCKS, LRU_BLOCK_W)
    r = jax.nn.sigmoid(jnp.einsum('bsgi,gij->bsgj', xg, wa.astype(jnp.float32)).reshape(b, s, c)
                       + ba.astype(jnp.float32))
    i = jax.nn.sigmoid(jnp.einsum('bsgi,gij->bsgj', xg, wx.astype(jnp.float32)).reshape(b, s, c)
                       + bx.astype(jnp.float32))
    log_a = -LRU_C * r * jax.nn.softplus(-lam.astype(jnp.float32))
    a = jnp.exp(log_a)
    mult = jnp.sqrt(-jnp.expm1(2.0 * log_a))
    mult = mult.at[:, 0].set(1.0)
    u = mult * (i * xc)

    def combine(left, right):
        a1, b1 = left
        a2, b2 = right
        return a1 * a2, a2 * b1 + b2

    _, h = lax.associative_scan(combine, (a, u), axis=1)
    return h * jax.nn.gelu(gb.astype(jnp.float32))

def gla_chunked(q, k, v, g):
    b, h, s, dk = q.shape
    dv = v.shape[-1]
    c = GLA_CHUNK
    n = s // c
    q = q.reshape(b, h, n, c, dk) * (dk ** -0.5)
    k = k.reshape(b, h, n, c, dk)
    v = v.reshape(b, h, n, c, dv)
    cum = jnp.cumsum(g.reshape(b, h, n, c, dk), axis=3)
    last = cum[:, :, :, -1:, :]
    q_d = q * jnp.exp(cum)
    k_d = k * jnp.exp(-cum)
    causal = jnp.tril(jnp.ones((c, c), dtype=bool))
    attn = jnp.where(causal, jnp.einsum('bhncd,bhned->bhnce', q_d, k_d), 0.0)
    intra = jnp.einsum('bhnce,bhnev->bhncv', attn, v)
    kv = jnp.einsum('bhncd,bhncv->bhndv', k * jnp.exp(last - cum), v)
    decay = jnp.exp(last[:, :, :, 0, :])

    def step(state, inp):
        kv_n, d_n = inp
        return d_n[..., None] * state + kv_n, state

    init = jnp.zeros((b, h, dk, dv), jnp.float32)
    _, s_prev = lax.scan(step, init, (kv.transpose(2, 0, 1, 3, 4), decay.transpose(2, 0, 1, 3)))
    s_prev = s_prev.transpose(1, 2, 0, 3, 4)
    inter = jnp.einsum('bhncd,bhndv->bhncv', q_d, s_prev)
    return (intra + inter).reshape(b, h, s, dv)

def moba_attention(q, k, v, rel_bias):
    b, h, s, d = q.shape
    nb = -(-s // MOBA_BLOCK)
    pad = nb * MOBA_BLOCK - s
    k_blk = jnp.pad(k, ((0, 0), (0, 0), (0, pad), (0, 0))).reshape(b, h, nb, MOBA_BLOCK, d)
    v_blk = jnp.pad(v, ((0, 0), (0, 0), (0, pad), (0, 0))).reshape(b, h, nb, MOBA_BLOCK, d)
    k_mean = jnp.mean(k_blk, axis=3)
    topk = min(MOBA_TOPK, nb)
    scale = d ** -0.5
    bias_h = rel_bias.T.astype(jnp.float32)
    bi = jnp.arange(b)[:, None, None]
    hi = jnp.arange(h)[None, :, None]
    blk_ids = jnp.arange(nb)
    offs = jnp.arange(MOBA_BLOCK)

    def chunk(ci):
        q0 = ci * MOBA_Q_CHUNK
        qc = lax.dynamic_slice_in_dim(q, q0, MOBA_Q_CHUNK, axis=2)
        qpos = q0 + jnp.arange(MOBA_Q_CHUNK)
        n_past = q0 // MOBA_BLOCK
        gate = jnp.einsum('bhqd,bhnd->bhqn', qc, k_mean)
        gate = jnp.where(blk_ids < n_past, gate, -jnp.inf)
        _, sel = lax.top_k(gate, topk)
        k_own = lax.dynamic_index_in_dim(k_blk, n_past, axis=2, keepdims=False)
        v_own = lax.dynamic_index_in_dim(v_blk, n_past, axis=2, keepdims=False)
        rel_own = qpos[:, None] - (n_past * MOBA_BLOCK + offs)[None, :]
        logit_own = (jnp.einsum('bhqd,bhkd->bhqk', qc, k_own) * scale
                     + bias_h[:, t5_bucket(rel_own)])
        logit_own = jnp.where(rel_own >= 0, logit_own, NEG_INF)
        logits = []
        for j in range(topk):
            idx = sel[..., j]
            kj = k_blk[bi, hi, idx]
            rel = qpos[:, None] - (idx[..., None] * MOBA_BLOCK + offs)
            bias = bias_h[hi[..., None], t5_bucket(rel)]
            lj = jnp.einsum('bhqd,bhqkd->bhqk', qc, kj) * scale + bias
            logits.append(jnp.where(j < n_past, lj, NEG_INF))
        logits.append(logit_own)
        p = jax.nn.softmax(jnp.concatenate(logits, axis=-1), axis=-1)
        p = p.reshape(b, h, MOBA_Q_CHUNK, topk + 1, MOBA_BLOCK)
        out = jnp.einsum('bhqk,bhkd->bhqd', p[..., topk, :], v_own)
        for j in range(topk):
            vj = v_blk[bi, hi, sel[..., j]]
            out = out + jnp.einsum('bhqk,bhqkd->bhqd', p[..., j, :], vj)
        return out

    out = lax.map(chunk, jnp.arange(s // MOBA_Q_CHUNK))
    return out.transpose(1, 2, 0, 3, 4).reshape(b, h, s, d)

def hybrid_mixer(h, w_in, conv_w, conv_b, wa, ba, wx, bx, lam, gate_w2, gate_b, gla_gain, rel_bias):
    bsz, s, _ = h.shape
    proj = h @ w_in
    split_points = [int(p) for p in np.cumsum(IN_SPLITS)[:-1]]
    lru_x, lru_g, gq, gk, gv, g_lr, g_out, mq, mk, mv = jnp.split(proj, split_points, axis=-1)
    y_lru = rg_lru_branch(lru_x, lru_g, conv_w, conv_b, wa, ba, wx, bx, lam)
    log_alpha = jax.nn.log_sigmoid((g_lr @ gate_w2 + gate_b).astype(jnp.float32)) / GLA_TAU
    o = gla_chunked(split_heads(gq, GLA_HEADS), split_heads(gk, GLA_HEADS),
                    split_heads(gv, GLA_HEADS), split_heads(log_alpha, GLA_HEADS))
    o = o.transpose(0, 2, 1, 3)
    o = o * lax.rsqrt(jnp.mean(o * o, axis=-1, keepdims=True) + RMS_EPS)
    y_gla = (o.reshape(bsz, s, GLA_V_W) * gla_gain.astype(jnp.float32)
             * jax.nn.silu(g_out.astype(jnp.float32)))
    y_moba = moba_attention(split_heads(mq, MOBA_HEADS), split_heads(mk, MOBA_HEADS),
                            split_heads(mv, MOBA_HEADS), rel_bias)
    y_moba = y_moba.transpose(0, 2, 1, 3).reshape(bsz, s, MOBA_W)
    return jnp.concatenate([y_lru, y_gla, y_moba], axis=-1).astype(h.dtype)

def second_inputs(seed: int = 0) -> dict:
    key = jax.random.key(seed)
    ks = jax.random.split(key, 24)
    f32 = jnp.float32
    L = DEPTH

    def nrm(k, shape, scale):
        return jax.random.normal(k, shape, f32) * scale

    u = jax.random.uniform(ks[12], (L, LRU_WIDTH), f32, 0.9, 0.999) ** (1.0 / LRU_C)
    return {
        'x': nrm(ks[0], (BATCH, SEQ, D_MODEL), 1.0),
        'pre_mix_norm': 1.0 + nrm(ks[1], (L, D_MODEL), 0.02),
        'post_mix_norm': 1.0 + nrm(ks[2], (L, D_MODEL), 0.02),
        'pre_ffn_norm': 1.0 + nrm(ks[3], (L, D_MODEL), 0.02),
        'post_ffn_norm': 1.0 + nrm(ks[4], (L, D_MODEL), 0.02),
        'w_in': nrm(ks[5], (L, D_MODEL, D_IN), D_MODEL ** -0.5),
        'w_out': nrm(ks[6], (L, D_MIX, D_MODEL), D_MIX ** -0.5),
        'lru_conv_w': nrm(ks[7], (L, LRU_CONV, LRU_WIDTH), LRU_CONV ** -0.5),
        'lru_conv_b': nrm(ks[8], (L, LRU_WIDTH), 0.01),
        'lru_wa': nrm(ks[9], (L, LRU_BLOCKS, LRU_BLOCK_W, LRU_BLOCK_W), LRU_BLOCK_W ** -0.5),
        'lru_ba': nrm(ks[10], (L, LRU_WIDTH), 0.01),
        'lru_wx': nrm(ks[11], (L, LRU_BLOCKS, LRU_BLOCK_W, LRU_BLOCK_W), LRU_BLOCK_W ** -0.5),
        'lru_bx': nrm(ks[13], (L, LRU_WIDTH), 0.01),
        'lru_lambda': jnp.log(u) - jnp.log1p(-u),
        'gla_gate_w2': nrm(ks[14], (L, GLA_GATE_RANK, GLA_QK_W), GLA_GATE_RANK ** -0.5),
        'gla_gate_b': nrm(ks[15], (L, GLA_QK_W), 0.01),
        'gla_norm': 1.0 + nrm(ks[16], (L, GLA_V_W), 0.02),
        'rel_bias': nrm(ks[17], (REL_BUCKETS, MOBA_HEADS), 0.2),
        'w_ffn_gate': nrm(ks[18], (L, D_MODEL, D_FF_2), D_MODEL ** -0.5),
        'w_ffn_up': nrm(ks[19], (L, D_MODEL, D_FF_2), D_MODEL ** -0.5),
        'w_ffn_down': nrm(ks[20], (L, D_FF_2, D_MODEL), D_FF_2 ** -0.5),
    }

def second_block(x, pre_mix_norm, post_mix_norm, pre_ffn_norm, post_ffn_norm, w_in, w_out,
              lru_conv_w, lru_conv_b, lru_wa, lru_ba, lru_wx, lru_bx, lru_lambda,
              gla_gate_w2, gla_gate_b, gla_norm, rel_bias, w_ffn_gate, w_ffn_up, w_ffn_down):
    for l in range(DEPTH):
        h = rms_norm(x, pre_mix_norm[l])
        mix = hybrid_mixer(h, w_in[l], lru_conv_w[l], lru_conv_b[l], lru_wa[l], lru_ba[l],
                           lru_wx[l], lru_bx[l], lru_lambda[l], gla_gate_w2[l], gla_gate_b[l],
                           gla_norm[l], rel_bias)
        x = x + rms_norm(mix @ w_out[l], post_mix_norm[l])
        h = rms_norm(x, pre_ffn_norm[l])
        f = (jax.nn.silu(h @ w_ffn_gate[l]) * (h @ w_ffn_up[l])) @ w_ffn_down[l]
        x = x + rms_norm(f, post_ffn_norm[l])
    return x


def setup_inputs(seed=0):
    out = dict(first_inputs(seed))
    for name, value in second_inputs(seed + 1).items():
        if name != "x":
            out[name + "_2"] = value
    return out


def reference(
    x, norm_mix_g, w_in, b_if, ml_norm_g, conv_w, w_ml_proj, w_sc_proj, w_sb_proj, w_out,
    norm_mlp_g, w_up, w_down, norm_final_g, pre_mix_norm_2, post_mix_norm_2, pre_ffn_norm_2,
    post_ffn_norm_2, w_in_2, w_out_2, lru_conv_w_2, lru_conv_b_2, lru_wa_2, lru_ba_2, lru_wx_2,
    lru_bx_2, lru_lambda_2, gla_gate_w2_2, gla_gate_b_2, gla_norm_2, rel_bias_2, w_ffn_gate_2,
    w_ffn_up_2, w_ffn_down_2,
):
    x = first_block(
        x, norm_mix_g, w_in, b_if, ml_norm_g, conv_w, w_ml_proj, w_sc_proj, w_sb_proj, w_out,
        norm_mlp_g, w_up, w_down, norm_final_g,
    )
    return second_block(
        x, pre_mix_norm_2, post_mix_norm_2, pre_ffn_norm_2, post_ffn_norm_2, w_in_2, w_out_2,
        lru_conv_w_2, lru_conv_b_2, lru_wa_2, lru_ba_2, lru_wx_2, lru_bx_2, lru_lambda_2,
        gla_gate_w2_2, gla_gate_b_2, gla_norm_2, rel_bias_2, w_ffn_gate_2, w_ffn_up_2,
        w_ffn_down_2,
    )


_drawn_inputs = setup_inputs


def setup_inputs(seed=0):
    import zlib

    import numpy as np

    out = dict(_drawn_inputs(seed))
    spreads = {}
    factors = {'ml_norm_g': 4.042,
     'post_mix_norm_2': 3.472,
     'pre_ffn_norm_2': 3.398,
     'post_ffn_norm_2': 17.692,
     'lru_conv_b_2': 2.773,
     'lru_ba_2': 64.0,
     'lru_bx_2': 58.444,
     'gla_gate_b_2': 8.0,
     'gla_norm_2': 5.184,
     'rel_bias_2': 2.998}
    for name, (base, spread) in spreads.items():
        noise = np.random.default_rng([zlib.crc32(name.encode()), seed]).standard_normal(out[name].shape)
        drawn = base * np.exp(spread * noise) if base else spread * noise
        out[name] = __import__('jax').numpy.asarray(drawn.astype(out[name].dtype))
    for name, factor in factors.items():
        out[name] = (out[name] * factor).astype(out[name].dtype)
    return out
```

```python
from contextlib import ExitStack

import concourse.bass as bass
import concourse.mybir as mybir

F32 = mybir.dt.float32
F32R = mybir.dt.float32r
ALU = mybir.AluOpType
ACT = mybir.ActivationFunctionType
AX = mybir.AxisListType

P = 128
T = 256
TT = T // P
D = 1024
KD = D // P
NG = 512
UK = 4
EPS = 1e-6
MASKED = -1e30

ML_H, ML_D = 4, 256
SB_H, SB_D = 16, 64
CONV_K = 3
D_FF = 4 * D
KF = D_FF // P
C_MLQ, C_MLK, C_MLV, C_MLO = 0, D, 2 * D, 3 * D
C_IF = 4 * D
C_SCB = C_IF + 2 * ML_H
C_SCC, C_SCU = C_SCB + D, C_SCB + 2 * D
C_SBQ, C_SBK, C_SBV = C_SCB + 3 * D, C_SCB + 4 * D, C_SCB + 5 * D
C_GML, C_GSC, C_GSB = C_SCB + 6 * D, C_SCB + 7 * D, C_SCB + 8 * D

LRU_W, LRU_TAPS, LRU_C = 256, 4, 8.0
GLA_H, GLA_DK, GLA_DV, GLA_RANK, GLA_CHUNK, GLA_TAU = 4, 32, 64, 16, 64, 16.0
MB_H, MB_D = 8, 64
D_FF2 = 2816
KF2 = D_FF2 // P
GU = 256
C2_LRU = 0
C2_GQ = 2 * LRU_W
C2_GV = C2_GQ + 2 * GLA_H * GLA_DK
C2_GOUT = C2_GV + GLA_H * GLA_DV + GLA_RANK
C2_MQ = C2_GOUT + GLA_H * GLA_DV
C2_MK, C2_MV = C2_MQ + MB_H * MB_D, C2_MQ + 2 * MB_H * MB_D
BUCKETS = 32
ROOT_FLOOR = 2.0 ** -100
GELU_C = 2.0 * (2.0 / 3.141592653589793) ** 0.5

LANDS, PARTS = 3, 3

K_ID, K_TRI, K_ONES, K_END = 0, P, 2 * P, 3 * P

VECS = [("norm_mix_g", 8), ("norm_mlp_g", 8), ("pre_mix_norm_2", 8), ("pre_ffn_norm_2", 8),
        ("ml_norm_g", 8), ("conv_w", 24), ("lru_conv_w_2", 8), ("lru_conv_b_2", 2),
        ("lru_ba_2", 2), ("lru_bx_2", 2), ("lru_lambda_2", 2), ("gla_gate_b_2", 1),
        ("gla_norm_2", 2)]
V_AT = {}
V_ROWS = 0
for _name, _rows in VECS:
    V_AT[_name] = V_ROWS
    V_ROWS += _rows


def plan_groups():
    g = []

    def halves(name, weight, col, act, form, k=KD):
        for j in range(2):
            g.append((f"{name}{j}", weight, [(col + j * NG, NG)], k, act, form))

    halves("sbq", "w_in", C_SBQ, "xT", "feat")
    halves("sbk", "w_in", C_SBK, "xT", "feat")
    halves("sbv", "w_in", C_SBV, "xT", "tok")
    halves("mlq", "w_in", C_MLQ, "xT", "feat")
    halves("mlk", "w_in", C_MLK, "xT", "feat")
    halves("mlv", "w_in", C_MLV, "xT", "tok")
    halves("mlo", "w_in", C_MLO, "xT", "tok")
    halves("scc", "w_in", C_SCC, "xT", "feat")
    halves("scu", "w_in", C_SCU, "xT", "feat")
    halves("scb", "w_in", C_SCB, "xT", "feat")
    for b, col in (("sb", C_GSB), ("ml", C_GML), ("sc", C_GSC)):
        for j in range(2):
            g.append((f"g{b}{j}", "w_in", [(col + j * NG, NG)], KD, "xT", "tok"))
            g.append((f"p{b}{j}", f"w_{b}_proj", [(j * NG, NG)], KD, f"y{b}T", "tok"))
    halves("out", "w_out", 0, "xT", "tok")
    for j in range(D_FF // NG):
        g.append((f"up{j}", "w_up", [(j * NG, NG)], KD, "xT", "feat"))
    halves("down", "w_down", 0, "aT", "tok", KF)
    w2 = "w_in_2"
    g.append(("mq", w2, [(C2_MQ, NG)], KD, "xT", "feat"))
    g.append(("mk", w2, [(C2_MK, NG)], KD, "xT", "feat"))
    g.append(("mv", w2, [(C2_MV, NG)], KD, "xT", "tok"))
    g.append(("gv", w2, [(C2_GV, GLA_H * GLA_DV + GLA_RANK)], KD, "xT", "tok"))
    g.append(("gqk", w2, [(C2_GQ, 2 * P)], KD, "xT", "feat"))
    g.append(("gout", w2, [(C2_GOUT, GLA_H * GLA_DV)], KD, "xT", "tok"))
    g.append(("lru", w2, [(C2_LRU, 2 * LRU_W)], KD, "xT", "feat"))
    halves("mix", "w_out_2", 0, "y2T", "tok")
    for j in range(D_FF2 // GU):
        g.append((f"gu{j}", ("w_ffn_gate_2", "w_ffn_up_2"), [(j * GU, GU), (j * GU, GU)], KD, "xT", "feat"))
    halves("dn", "w_ffn_down_2", 0, "a2T", "tok", KF2)
    return g


GROUPS = plan_groups()
G_AT = {grp[0]: n for n, grp in enumerate(GROUPS)}
UNITS = [(n, k, min(UK, grp[3] - k)) for n, grp in enumerate(GROUPS) for k in range(0, grp[3], UK)]
FIRST_U, LAST_U = {}, {}
for _u, (_n, _k, _m) in enumerate(UNITS):
    FIRST_U.setdefault(GROUPS[_n][0], _u)
    LAST_U[GROUPS[_n][0]] = _u
NU = len(UNITS)


def width(n):
    return sum(w for _, w in GROUPS[n][2])


def readers(name):
    if name[:3] == "mlo" or name[0:3] in ("gsb", "gml", "gsc"):
        return ("act",)
    if name[:2] in ("up", "gu"):
        return ("dve",)
    if name == "gout":
        return ("dve",)
    return ("dve",)


def reads_before(n, eng):
    return sum(eng in readers(GROUPS[m][0]) for m in range(n + 1))


TURNS = [("x", KD, "norm_mix_g"), ("ysb", KD, None), ("yml", KD, "ml_norm_g"), ("merged", KD, None),
         ("h2", KD, "norm_mlp_g"), ("h3", KD, "pre_mix_norm_2"), ("gla", 2, "gla_norm_2"),
         ("moba", 4, None), ("h4", KD, "pre_ffn_norm_2")]
TURN_AT = {}
_b = 0
for _name, _k, _ in TURNS:
    TURN_AT[_name] = _b
    _b += _k // 2

SB0 = LAST_U["sbv1"] + 1
ML0 = SB0 + SB_H + 2
U_IF = 1
TURN_SB = ML0 + 6
TURN_ML = TURN_SB + 2
MB0 = FIRST_U["gv"]


def build(nc, dram, out):
    ctx = ExitStack()

    def sb(name, shape, dt=F32, stack=None):
        return (stack or ctx).enter_context(nc.sbuf_tensor(name, shape, dt))

    def sem(name):
        return ctx.enter_context(nc.semaphore(name))

    land = sb("land", [P, LANDS, UK, NG])
    whi = sb("whi", [P, PARTS, UK, NG], F32R)
    wlo = sb("wlo", [P, PARTS, UK, NG], F32R)
    xT_hi = sb("xT_hi", [P, KD, T], F32R)
    xT_lo = sb("xT_lo", [P, KD, T], F32R)
    x_tok = sb("x_tok", [P, TT, D])
    tok = sb("tok", [P, TT, D])
    con = sb("con", [P, K_END])
    rows = sb("rows", [P, P])
    vecs = sb("vecs", [P, V_ROWS])
    squares = sb("squares", [P, 7, TT])
    mean_sq = sb("mean_sq", [P, 7, TT])
    rstd = sb("rstd", [P, 7, TT])
    mhalf = sb("mhalf", [P, 1])
    ident = con[:, K_ID:K_ID + P]
    negtri = con[:, K_TRI:K_TRI + P]
    negones = con[:, K_ONES:K_ONES + P]

    mix, area = ExitStack(), ExitStack()
    sbqT = sb("sbqT", [P, KD, T], stack=area)
    sbkT = sb("sbkT", [P, KD, T], stack=area)
    sbv = sb("sbv", [P, TT, D], stack=area)
    area.close()
    cT = sb("cT", [P, KD, T], stack=mix)
    zT = sb("zT", [P, KD, T + CONV_K - 1], stack=mix)
    conv = sb("conv", [P, 4, T], stack=mix)
    sb("pad0", [P, KD * T - KD * (CONV_K - 1) - 4 * T], stack=mix)
    mlqT = sb("mlqT", [P, KD, T], stack=area)
    mlkT = sb("mlkT", [P, KD, T], stack=area)
    mlv = sb("mlv", [P, TT, D], stack=area)
    area.close()
    ymlT_hi = sb("ymlT_hi", [P, KD, T], F32R, stack=mix)
    ymlT_lo = sb("ymlT_lo", [P, KD, T], F32R, stack=mix)
    gate = sb("gate", [P, TT, NG], stack=mix)
    gated = sb("gated", [P, TT, NG], stack=mix)
    mlo = sb("mlo", [P, TT, D], stack=mix)
    ysbT_hi = sb("ysbT_hi", [P, KD, T], F32R, stack=mix)
    ysbT_lo = sb("ysbT_lo", [P, KD, T], F32R, stack=mix)
    sel = sb("sel", [ML_H, ML_H * P], stack=area)
    i_row = sb("i_row", [ML_H, T], stack=area)
    f_row = sb("f_row", [ML_H, T], stack=area)
    e_row = sb("e_row", [ML_H, T], stack=area)
    one_row = sb("one_row", [ML_H, T], stack=area)
    negm_row = sb("negm_row", [ML_H, T], stack=area)
    bm_row = sb("bm_row", [ML_H, T], stack=area)
    hot = sb("hot", [BUCKETS + 1, 2 * T], stack=area)
    tab = sb("tab", [MB_H, 2 * T], stack=area)
    rel33 = sb("rel33", [BUCKETS + 1, MB_H], stack=area)
    w_if = sb("w_if", [P, KD, 2 * ML_H], stack=area)
    w_if_hi = sb("w_if_hi", [P, KD, 2 * ML_H], F32R, stack=area)
    w_if_lo = sb("w_if_lo", [P, KD, 2 * ML_H], F32R, stack=area)
    area.close()
    yscT_hi = sb("yscT_hi", [P, KD, T], F32R, stack=mix)
    yscT_lo = sb("yscT_lo", [P, KD, T], F32R, stack=mix)
    sbw = sb("sbw", [P, 2, 3 * P], stack=mix)
    sba = sb("sba", [P, 2, 3 * P], stack=mix)
    if_tok = sb("if_tok", [P, TT, 2 * ML_H], stack=mix)
    b_if = sb("b_if", [P, 2 * ML_H], stack=mix)
    c_col = sb("c_col", [P, TT, ML_H], stack=mix)
    floor_col = sb("floor_col", [P, TT, ML_H], stack=mix)
    ml_den = sb("ml_den", [P, 4, TT], stack=mix)
    ml_sq = sb("ml_sq", [P, TT, ML_H], stack=mix)
    ml_ms = sb("ml_ms", [P, TT, ML_H], stack=mix)
    ml_rstd = sb("ml_rstd", [P, TT, ML_H], stack=mix)
    mix.close()

    ffn = ExitStack()
    aT_hi = sb("aT_hi", [P, KF, T], F32R, stack=ffn)
    aT_lo = sb("aT_lo", [P, KF, T], F32R, stack=ffn)
    relu = sb("relu", [P, 2, 2 * NG], stack=ffn)
    relu2 = sb("relu2", [P, 2, 2 * NG], stack=ffn)
    gain_a = sb("gain_a", [P, D], stack=ffn)
    ffn.close()

    two = ExitStack()
    y2T_hi = sb("y2T_hi", [P, KD, T], F32R, stack=two)
    y2T_lo = sb("y2T_lo", [P, KD, T], F32R, stack=two)
    mixed = sb("mixed", [P, TT, D], stack=two)
    gain_b = sb("gain_b", [P, D], stack=two)
    gain_c = sb("gain_c", [P, D], stack=two)
    a2T_hi = sb("a2T_hi", [P, KF2, T], F32R, stack=area)
    a2T_lo = sb("a2T_lo", [P, KF2, T], F32R, stack=area)
    sig2 = sb("sig2", [P, 2, 2 * T], stack=area)
    act2 = sb("act2", [P, 2, 2 * T], stack=area)
    area.close()
    LC = LRU_W // P
    mbq = sb("mbq", [P, 4, T], stack=area)
    mbk = sb("mbk", [P, 4, T], stack=area)
    mbv = sb("mbv", [P, TT, MB_H * MB_D], stack=area)
    bias = sb("bias", [P, MB_H, 3 * P], stack=area)
    area.close()
    lw = sb("lw", [P, 10, LC, T], stack=two)
    sb("pad1", [P, (12 + 2 * MB_H - MB_H // 2) * T - 10 * LC * T], stack=two)
    mbs = sb("mbs", [P, 2, 3 * P], stack=two)
    mbp = sb("mbp", [P, 2, 3 * P], stack=two)
    mb_max = sb("mb_max", [P, MB_H, TT], stack=two)
    mb_sum = sb("mb_sum", [P, MB_H, TT], stack=two)
    mb_inv = sb("mb_inv", [P, MB_H, TT], stack=two)
    GD = GLA_H * GLA_DV
    gv = sb("gv", [P, TT, GD + GLA_RANK], stack=two)
    gqk = sb("gqk", [P, 2, T], stack=two)
    gout = sb("gout", [P, TT, GD], stack=two)
    gsig = sb("gsig", [P, TT, GD], stack=two)
    glrT = sb("glrT", [GLA_RANK, T], stack=two)
    gw2 = sb("gw2", [GLA_RANK, P], stack=two)
    gla = sb("gla", [P, 6, T], stack=two)
    gdec = sb("gdec", [P, 4], stack=two)
    gnew = sb("gnew", [P, T], stack=two)
    qd = sb("qd", [P, T], stack=two)
    kd = sb("kd", [P, T], stack=two)
    kl = sb("kl", [P, T], stack=two)
    kl_tok = sb("kl_tok", [P, TT, P], stack=two)
    gattn = sb("gattn", [P, GLA_H, TT, P], stack=two)
    gstate = sb("gstate", [P, 4, GD], stack=two)
    gsq = sb("gsq", [P, TT * GLA_H, GLA_DV], stack=two)
    gss = sb("gss", [P, 3, TT * GLA_H], stack=two)
    lruT = sb("lruT", [P, 2 * LC, T + LRU_TAPS - 1], stack=two)
    wab = sb("wab", [P, 2, LC, 64], stack=two)
    lamb = sb("lamb", [P, 8, LC], stack=two)
    two.close()

    acc = ctx.enter_context(nc.psum_tensor("acc", [P, 2, 2, NG], F32))
    M = [ctx.enter_context(nc.psum_tensor(f"m{i}", [P, NG], F32)) for i in range(4)]

    landed = [sem(f"landed{i}") for i in range(LANDS)]
    x_in, rows_in, con_in, small_in, gain_in, late_in = (
        sem(n) for n in ("x_in", "rows_in", "con_in", "small_in", "gain_in", "late_in"))
    tab_out, copies_out, bias_in, stored = (sem(n) for n in ("tab_out", "copies_out", "bias_in", "stored"))
    hi_ready, lo_ready, units_done = sem("hi_ready"), sem("lo_ready"), sem("units_done")
    read_act, read_dve = sem("read_act"), sem("read_dve")
    turned, turn_hi, turn_lo = sem("turned"), sem("turn_hi"), sem("turn_lo")
    sq_act, sq_dve, rstd_ready = sem("sq_act"), sem("sq_dve"), sem("rstd_ready")
    norm_act, norm_dve = sem("norm_act"), sem("norm_dve")
    act_step, dve_step, pool_step = sem("act_step"), sem("dve_step"), sem("pool_step")
    vecs_turned, vecs_ready, tab_done, tab_ready = (
        sem(n) for n in ("vecs_turned", "vecs_ready", "tab_done", "tab_ready"))
    pool_set = sem("pool_set")
    if_hi, if_lo, if_done, if_ready = sem("if_hi"), sem("if_lo"), sem("if_done"), sem("if_ready")
    rows_turned, rows_ready, e_ready, scans_ready = (
        sem(n) for n in ("rows_turned", "rows_ready", "e_ready", "scans_ready"))
    cols_turned, c_ready, floor_ready = sem("cols_turned"), sem("c_ready"), sem("floor_ready")
    sb_z, sb_log, sb_t, sb_tm, sb_r, sb_a, sb_am, sb_av, sb_y = (
        sem(n) for n in ("sb_z", "sb_log", "sb_t", "sb_tm", "sb_r", "sb_a", "sb_am", "sb_av", "sb_y"))
    sig_o = sem("sig_o")
    ml_s, ml_w, ml_wm, ml_p, ml_num, ml_y, ml_ss, ml_rs, yml_ready = (
        sem(n) for n in ("ml_s", "ml_w", "ml_wm", "ml_p", "ml_num", "ml_y", "ml_ss", "ml_rs", "yml_ready"))
    ysc_hi, ysc_lo = sem("ysc_hi"), sem("ysc_lo")
    relu_ready, a_hi, a_lo = sem("relu_ready"), sem("a_hi"), sem("a_lo")
    x_done = sem("x_done")
    mb_s, mb_logit, mb_max_ready, mb_e, mb_pt, mb_p, mb_av, mb_y = (
        sem(n) for n in ("mb_s", "mb_logit", "mb_max_ready", "mb_e", "mb_pt", "mb_p", "mb_av", "mb_y"))
    g_sets, glr_turned, glr_ready, g_gate, g_ln, g_min, g_cum, g_exp, g_qk, g_at, g_atc, g_atm = (
        sem(n) for n in ("g_sets", "glr_turned", "glr_ready", "g_gate", "g_ln", "g_min", "g_cum", "g_exp",
                         "g_qk", "g_at", "g_atc", "g_atm"))
    kl_turned, kl_ready, g_kv, g_state, g_o, g_osq, g_oss, g_rs, g_y, g_sig = (
        sem(n) for n in ("kl_turned", "kl_ready", "g_kv", "g_state", "g_o", "g_osq", "g_oss", "g_rs", "g_y",
                         "g_sig"))
    l_conv, l_gates, l_sig, l_exp, l_m2, l_mult, l_y, l_hi, l_lo, l_gin, l_gel, l_lam, l_sp, l_spn = (
        sem(n) for n in ("l_conv", "l_gates", "l_sig", "l_exp", "l_m2", "l_mult", "l_y", "l_hi", "l_lo",
                         "l_gin", "l_gel", "l_lam", "l_sp", "l_spn"))
    sig2_ready, act2_hi, act2_lo = sem("sig2_ready"), sem("act2_hi"), sem("act2_lo")

    weights = {n: dram[n] for n in dram}
    by_distance = nc.dram_tensor("by_distance", (1, MB_H * 2 * T), F32, kind="Internal").ap()
    by_query = nc.dram_tensor("by_query", (P, MB_H * 2 * T), F32, kind="Internal").ap()

    def land_count(u):
        return 16 * sum(len(GROUPS[UNITS[v][0]][2]) for v in range(u % LANDS, u + 1, LANDS))

    block = ctx.enter_context(nc.Block())

    @block.sync
    def _(sp):
        sp.dma_start(x_tok[:, 0, :], dram["x"][0:P, :]).then_inc(x_in, 16)
        sp.dma_start(x_tok[:, 1, :], dram["x"][P:T, :]).then_inc(x_in, 16)
        sp.dma_start(con[:], dram["con"]).then_inc(con_in, 16)
        for name, n in VECS:
            sp.dma_start(rows[V_AT[name]:V_AT[name] + n, :], dram[name]).then_inc(rows_in, 16)

        def load(u):
            n, k, m = UNITS[u]
            _, weight, segs, *_ = GROUPS[n]
            if u >= LANDS:
                sp.wait_ge(lo_ready, u - LANDS + 1)
            at = 0
            for i, (col, w) in enumerate(segs):
                src = weights[weight if len(segs) == 1 else weight[i]]
                sp.dma_start(land[:, u % LANDS, 0:m, at:at + w],
                             src[k * P:(k + m) * P, col:col + w].rearrange("(k p) n -> p k n", p=P)
                             ).then_inc(landed[u % LANDS], 16)
                at += w

        for u in range(NU):
            load(u)
            if u == 0:
                sp.dma_start(w_if[:], dram["w_in"][:, C_IF:C_IF + 2 * ML_H].rearrange(
                    "(k p) n -> p k n", p=P)).then_inc(small_in, 16)
                sp.dma_start(b_if[:], dram["b_if"].to_broadcast([P, 2 * ML_H])).then_inc(small_in, 16)
                sp.dma_start(hot[:], dram["hot"]).then_inc(small_in, 16)
                sp.dma_start(sel[:], dram["sel"]).then_inc(small_in, 16)
                sp.dma_start(rel33[0:BUCKETS, :], dram["rel_bias_2"]).then_inc(small_in, 16)
            if u == 2:
                sp.wait_ge(tab_ready, 1)
                sp.dma_start(by_distance.rearrange("a (h j) -> (a h) j", h=MB_H), tab[:]).then_inc(tab_out, 16)
            if u == SB0:
                sp.wait_ge(tab_out, 16)
                sp.dma_start(by_query, by_distance.to_broadcast([P, MB_H * 2 * T])).then_inc(copies_out, 16)
            if u == FIRST_U["up1"]:
                sp.wait_ge(turn_lo, TURN_AT["merged"] + 4)
                sp.wait_ge(turn_hi, TURN_AT["merged"] + 4)
                sp.dma_start(gain_a[:], dram["norm_final_g"].to_broadcast([P, D])).then_inc(gain_in, 16)
            if u == FIRST_U["mq"] + 2:
                sp.wait_ge(x_done, 1)
                sp.wait_ge(copies_out, 16)
                row = MB_H * 2 * T - 1
                sp.dma_start(bias[:, :, 0:P], bass.AP(by_query.tensor, T - 1, [[row, P], [2 * T, MB_H], [1, P]])
                             ).then_inc(bias_in, 16)
                sp.dma_start(bias[:, :, P:3 * P],
                             bass.AP(by_query.tensor, T - 1 - P, [[row, P], [2 * T, MB_H], [1, T]])
                             ).then_inc(bias_in, 16)
                sp.dma_start(gw2[:], dram["gla_gate_w2_2"]).then_inc(late_in, 16)
                for i, name in enumerate(("lru_wa_2", "lru_wx_2")):
                    for c in range(LC):
                        sp.dma_start(wab[:, i, c, :], dram[name][2 * c:2 * c + 2].rearrange("b i j -> (b i) j")
                                     ).then_inc(late_in, 16)
                sp.dma_start(gain_b[:], dram["post_mix_norm_2"].to_broadcast([P, D])).then_inc(late_in, 16)
                sp.dma_start(gain_c[:], dram["post_ffn_norm_2"].to_broadcast([P, D])).then_inc(late_in, 16)
        for t in range(TT):
            sp.wait_ge(x_done, 3 + t)
            sp.dma_start(out[t * P:(t + 1) * P, :], x_tok[:, t, :]).then_inc(stored, 16)
        sp.wait_ge(stored, 16 * TT)

    LATE = 16 * (1 + 2 * LC + 2)

    @block.tensor
    def _(pe):
        mm = nc.tensor.matmul

        def lhs_of(act):
            return {"xT": (xT_hi, xT_lo), "ysbT": (ysbT_hi, ysbT_lo), "ymlT": (ymlT_hi, ymlT_lo),
                    "yscT": (yscT_hi, yscT_lo), "aT": (aT_hi, aT_lo), "y2T": (y2T_hi, y2T_lo),
                    "a2T": (a2T_hi, a2T_lo)}[act]

        def turned_ready(stage, tiles):
            pe.wait_ge(turn_hi, TURN_AT[stage] + (tiles + 1) // 2)
            pe.wait_ge(turn_lo, TURN_AT[stage] + (tiles + 1) // 2)

        def wait_operand(name, act, k1):
            if act == "xT":
                turned_ready("merged" if name[:3] == "out" else "h2" if name[:2] == "up" else
                             "h4" if name[:2] == "gu" else
                             "h3" if name in ("mq", "mk", "mv", "gv", "gqk", "gout", "lru") else "x", k1)
            elif act == "ysbT":
                turned_ready("ysb", k1)
            elif act == "ymlT":
                turned_ready("yml", k1)
            elif act == "yscT":
                pe.wait_ge(ysc_hi, k1 // 4)
                pe.wait_ge(ysc_lo, k1 // 4)
            elif act == "aT":
                pe.wait_ge(a_hi, k1 // 4)
                pe.wait_ge(a_lo, k1 // 4)
            elif act == "a2T":
                pe.wait_ge(act2_hi, k1 // 2)
                pe.wait_ge(act2_lo, k1 // 2)
            else:
                pe.wait_ge(l_hi, 1)
                pe.wait_ge(l_lo, 1)
                turned_ready("moba", 4)

        def product(u):
            n, k0, m = UNITS[u]
            name, _, _, kk, act, form = GROUPS[n]
            xh, xl = lhs_of(act)
            w, s = width(n), u % PARTS
            wait_operand(name, act, k0 + m)
            if k0 == 0 and n >= 2:
                for eng, seen in (("act", read_act), ("dve", read_dve)):
                    if eng in readers(GROUPS[n - 2][0]):
                        pe.wait_ge(seen, reads_before(n - 2, eng))
            pe.wait_ge(hi_ready, u + 1)
            pe.wait_ge(lo_ready, u + 1)
            for k in range(m):
                first, end = k0 + k == 0, k0 + k == kk - 1
                if form == "tok":
                    for t in range(TT):
                        to = acc[:, n % 2, t, 0:w]
                        ts = slice(t * P, (t + 1) * P)
                        mm(to, xh[:, k0 + k, ts], whi[:, s, k, 0:w], start=first, stop=False)
                        mm(to, xh[:, k0 + k, ts], wlo[:, s, k, 0:w], start=False, stop=False)
                        last = mm(to, xl[:, k0 + k, ts], whi[:, s, k, 0:w], start=False, stop=end)
                else:
                    for c in range(w // P):
                        to = acc[:, n % 2, c // 2, (c % 2) * T:(c % 2 + 1) * T]
                        cs = slice(c * P, (c + 1) * P)
                        mm(to, whi[:, s, k, cs], xh[:, k0 + k, :], start=first and c % 2 == 0, stop=False,
                           skip_group_check=True)
                        mm(to, whi[:, s, k, cs], xl[:, k0 + k, :], start=False, stop=False,
                           skip_group_check=True)
                        last = mm(to, wlo[:, s, k, cs], xh[:, k0 + k, :], start=False, stop=end,
                                  skip_group_check=True)
            last.then_inc(units_done, 1)

        def turn(stage, src, col0=0):
            _, kk, _ = [s for s in TURNS if s[0] == stage][0]
            if TURN_AT[stage]:
                pe.wait_ge(turn_hi, TURN_AT[stage])
                pe.wait_ge(turn_lo, TURN_AT[stage])
            for b in range(kk // 2):
                for i in range(2):
                    for t in range(TT):
                        k = 2 * b + i
                        last = nc.tensor.transpose(M[b][:, (i * TT + t) * P:(i * TT + t + 1) * P],
                                                   src[:, t, col0 + k * P:col0 + (k + 1) * P], ident)
                last.then_inc(turned, 1)

        def norm_turn(stage, count):
            pe.wait_ge(norm_act, count)
            pe.wait_ge(norm_dve, count)
            turn(stage, tok)

        def sb_scores(h):
            if h == 0:
                pe.wait_ge(read_dve, reads_before(G_AT["sbv1"], "dve"))
            if h >= 2:
                pe.wait_ge(sb_a, h - 1)
            c, o = h // 2, SB_D * (h % 2)
            z = M[h % 2]
            mm(z[:, 0:T], sbkT[o:o + SB_D, c, 0:P], sbqT[o:o + SB_D, c, :], start=True, stop=True)
            mm(z[:, T:T + P], sbkT[o:o + SB_D, c, P:T], sbqT[o:o + SB_D, c, P:T], start=False, stop=True,
               skip_group_check=True).then_inc(sb_z, 1)

        def sb_remain(h):
            pe.wait_ge(sb_tm, h + 1)
            z, w = M[h % 2], sbw[:, h % 2]
            mm(z[:, 0:T], negtri, w[:, 0:T], start=False, stop=True, skip_group_check=True)
            mm(z[:, T:T + P], negtri, w[:, T:T + P], start=False, stop=True, skip_group_check=True)
            mm(z[:, P:T], negones, w[:, T:T + P], start=False, stop=True,
               skip_group_check=True).then_inc(sb_r, 1)

        def sb_values(h):
            pe.wait_ge(sb_am, h + 1)
            if h < 2:
                pe.wait_ge(c_ready, 1)
                pe.wait_ge(floor_ready, 1)
                pe.wait_ge(if_ready, 1)
            else:
                pe.wait_ge(sb_y, h - 1)
            o, a = M[2 + h % 2], sba[:, h % 2]
            v = slice(h * SB_D, (h + 1) * SB_D)
            mm(o[:, 0:SB_D], a[:, 0:P], sbv[:, 0, v], start=True, stop=True)
            mm(o[:, SB_D:2 * SB_D], a[:, P:T], sbv[:, 0, v], start=True, stop=False)
            mm(o[:, SB_D:2 * SB_D], a[:, T:T + P], sbv[:, 1, v], start=False, stop=True).then_inc(sb_av, 1)

        def if_gates():
            pe.wait_ge(if_hi, 1)
            pe.wait_ge(if_lo, 1)
            for t in range(TT):
                to, ts = M[3][:, t * 8:(t + 1) * 8], slice(t * P, (t + 1) * P)
                for k in range(KD):
                    mm(to, xT_hi[:, k, ts], w_if_hi[:, k, :], start=k == 0, stop=False)
                    mm(to, xT_hi[:, k, ts], w_if_lo[:, k, :], start=False, stop=False)
                    last = mm(to, xT_lo[:, k, ts], w_if_hi[:, k, :], start=False, stop=k == KD - 1)
            last.then_inc(if_done, 1)

        def if_rows():
            pe.wait_ge(if_ready, 1)
            for i in range(2):
                for t in range(TT):
                    last = nc.tensor.transpose(M[2][0:ML_H, (i * TT + t) * P:(i * TT + t + 1) * P],
                                               if_tok[:, t, i * ML_H:(i + 1) * ML_H], ident)
            last.then_inc(rows_turned, 1)

        def if_cols():
            pe.wait_ge(scans_ready, 1)
            for i, row in enumerate((i_row, bm_row)):
                for t in range(TT):
                    at = (i * TT + t) * ML_H
                    last = nc.tensor.transpose(M[2][:, at:at + ML_H], row[:, t * P:(t + 1) * P],
                                               ident[0:ML_H, 0:ML_H])
            last.then_inc(cols_turned, 1)

        def ml_scores(h):
            s, b = M[2 * (h % 2)], M[2 * (h % 2) + 1]
            if h < 2:
                pe.wait_ge(sb_a, SB_H)
                pe.wait_ge(sb_y, SB_H)
                pe.wait_ge(read_dve, reads_before(G_AT["mlv1"], "dve"))
            else:
                pe.wait_ge(ml_y, h - 1)
            for i in range(2):
                c = 2 * h + i
                mm(s[:, 0:T], mlkT[:, c, 0:P], mlqT[:, c, :], start=i == 0, stop=i == 1, skip_group_check=True)
                mm(s[:, T:T + P], mlkT[:, c, P:T], mlqT[:, c, P:T], start=False, stop=i == 1,
                   skip_group_check=True)
            mm(b[:, 0:T], sel[:, h * P:(h + 1) * P], negm_row[:, :], start=True, stop=True).then_inc(ml_s, 1)

        def ml_values(h):
            pe.wait_ge(ml_p, h + 1)
            o, b, w = M[2 * (h % 2)], M[2 * (h % 2) + 1], sba[:, h % 2]
            v = slice(h * ML_D, (h + 1) * ML_D)
            ones = con[:, K_ONES:K_ONES + 1]
            mm(o[:, 0:ML_D], w[:, 0:P], mlv[:, 0, v], start=True, stop=True)
            mm(o[:, ML_D:], w[:, P:T], mlv[:, 0, v], start=True, stop=False)
            mm(o[:, ML_D:], w[:, T:T + P], mlv[:, 1, v], start=False, stop=True)
            mm(b[:, T:T + 1], w[:, 0:P], ones, start=True, stop=True)
            mm(b[:, T + 1:T + 2], w[:, P:T], ones, start=True, stop=False)
            mm(b[:, T + 1:T + 2], w[:, T:T + P], ones, start=False, stop=True).then_inc(ml_num, 1)

        def mb_scores(h):
            if h == 0:
                pe.wait_ge(read_dve, reads_before(G_AT["mv"], "dve"))
                pe.wait_ge(turn_hi, TURN_AT["h3"] + 4)
                pe.wait_ge(turn_lo, TURN_AT["h3"] + 4)
            if h >= 2:
                pe.wait_ge(mb_y, h - 1)
            c, o = h // 2, MB_D * (h % 2)
            s = M[h % 2]
            mm(s[:, 0:P], mbq[o:o + MB_D, c, 0:P], mbk[o:o + MB_D, c, 0:P], start=True, stop=True)
            mm(s[:, P:3 * P], mbq[o:o + MB_D, c, P:T], mbk[o:o + MB_D, c, :], start=True,
               stop=True).then_inc(mb_s, 1)

        def mb_turn(h):
            pe.wait_ge(mb_e, h + 1)
            if h >= 2:
                pe.wait_ge(mb_p, h - 1)
            for i in range(3):
                last = nc.tensor.transpose(M[2 + h % 2][:, i * P:(i + 1) * P], mbs[:, h % 2, i * P:(i + 1) * P],
                                           ident)
            last.then_inc(mb_pt, 1)

        def mb_values(h):
            pe.wait_ge(mb_p, h + 1)
            o, p = M[h % 2], mbp[:, h % 2]
            v = slice(h * MB_D, (h + 1) * MB_D)
            mm(o[:, 0:MB_D], p[:, 0:P], mbv[:, 0, v], start=True, stop=True)
            mm(o[:, MB_D:2 * MB_D], p[:, P:T], mbv[:, 0, v], start=True, stop=False)
            mm(o[:, MB_D:2 * MB_D], p[:, T:3 * P], mbv[:, 1, v], start=False, stop=True).then_inc(mb_av, 1)

        def gla_products():
            pe.wait_ge(read_dve, reads_before(G_AT["gout"], "dve"))
            pe.wait_ge(late_in, LATE)
            for t in range(TT):
                last = nc.tensor.transpose(M[0][0:GLA_RANK, t * P:(t + 1) * P], gv[:, t, GD:GD + GLA_RANK], ident)
            last.then_inc(glr_turned, 1)
            pe.wait_ge(glr_ready, 1)
            mm(M[1][:, 0:T], gw2[:, :], glrT[:, :], start=True, stop=True).then_inc(g_gate, 1)
            pe.wait_ge(g_qk, 3)
            for t in range(TT):
                ts = slice(t * P, (t + 1) * P)
                for h in range(GLA_H):
                    hs = slice(h * GLA_DK, (h + 1) * GLA_DK)
                    last = mm(M[h][:, ts], kd[hs, ts], qd[hs, ts], start=True, stop=True)
            last.then_inc(g_at, 1)
            pe.wait_ge(g_atc, 1)
            for t in range(TT):
                last = nc.tensor.transpose(M[3][:, t * P:(t + 1) * P], kl[:, t * P:(t + 1) * P], ident)
            last.then_inc(kl_turned, 1)
            pe.wait_ge(kl_ready, 1)
            for n in range(3):
                o, t = GLA_CHUNK * (n % 2), n // 2
                last = mm(M[n][:, 0:GD], kl_tok[o:o + GLA_CHUNK, t, :], gv[o:o + GLA_CHUNK, t, 0:GD],
                          start=True, stop=True)
            last.then_inc(g_kv, 1)
            pe.wait_ge(g_state, 1)
            pe.wait_ge(g_atm, 1)
            for t in range(TT):
                to = M[3][:, t * GD:(t + 1) * GD]
                for i in range(2):
                    n = 2 * t + i
                    o = GLA_CHUNK * i
                    mm(to[o:o + GLA_CHUNK, :], qd[:, n * GLA_CHUNK:(n + 1) * GLA_CHUNK], gstate[:, n, :],
                       start=True, stop=False, skip_group_check=True)
                for h in range(GLA_H):
                    hs = slice(h * GLA_DV, (h + 1) * GLA_DV)
                    last = mm(to[:, hs], gattn[:, h, t, :], gv[:, t, hs], start=False, stop=True,
                              skip_group_check=True)
            last.then_inc(g_o, 1)

        def lru_gates():
            pe.wait_ge(l_conv, 1)
            pe.wait_ge(g_y, 1)
            pe.wait_ge(turn_hi, TURN_AT["moba"])
            pe.wait_ge(turn_lo, TURN_AT["moba"])
            for i in range(2):
                for c in range(LC):
                    for b in range(2):
                        bs = slice(64 * b, 64 * b + 64)
                        last = mm(M[2 * i + b][bs, c * T:(c + 1) * T], wab[bs, i, c, :], lw[bs, 0, c, :],
                                  start=True, stop=True)
            last.then_inc(l_gates, 1)

        pe.wait_ge(con_in, 16)
        pe.wait_ge(rows_in, 16 * len(VECS))
        nc.tensor.transpose(M[0][:, 0:V_ROWS], rows[0:V_ROWS, :], ident[0:V_ROWS, 0:V_ROWS]).then_inc(vecs_turned, 1)
        pe.wait_ge(small_in, 80)
        pe.wait_ge(pool_set, 1)
        mm(M[1][0:MB_H, :], rel33[:, :], hot[:, :], start=True, stop=True).then_inc(tab_done, 1)
        pe.wait_ge(vecs_ready, 1)
        pe.wait_ge(tab_ready, 1)
        norm_turn("x", 1)

        for u in range(NU):
            name = GROUPS[UNITS[u][0]][0]
            first_k = UNITS[u][1] == 0
            if name == "out0" and first_k:
                pe.wait_ge(read_dve, reads_before(G_AT["psc1"], "dve"))
                turn("merged", tok)
            if name == "up0" and first_k:
                norm_turn("h2", 2)
            if name == "mq" and first_k:
                norm_turn("h3", 3)
            if name == "mix0" and first_k:
                for i in range(LAST_U["lru"] - MB0, MB_H + 2):
                    if i >= 2:
                        mb_values(i - 2)
                    if 1 <= i <= MB_H:
                        mb_turn(i - 1)
                    if i < MB_H:
                        mb_scores(i)
                pe.wait_ge(mb_y, MB_H)
                gla_products()
                pe.wait_ge(g_y, 1)
                turn("gla", tok)
                turn("moba", tok, 2 * P)
                pe.wait_ge(turn_hi, TURN_AT["moba"] + 2)
                pe.wait_ge(turn_lo, TURN_AT["moba"] + 2)
                lru_gates()
            if name == "gu0" and first_k:
                norm_turn("h4", 4)
            product(u)
            if u == U_IF:
                if_gates()
            if u == U_IF + 2:
                if_rows()
            if u == U_IF + 6:
                if_cols()
            i = u - SB0
            if 1 <= i <= SB_H:
                sb_remain(i - 1)
            if 0 <= i < SB_H:
                sb_scores(i)
            if 2 <= i < SB_H + 2:
                sb_values(i - 2)
            i = u - ML0
            if 0 <= i < ML_H:
                ml_scores(i)
            if 1 <= i <= ML_H:
                ml_values(i - 1)
            if u == TURN_SB:
                pe.wait_ge(sb_y, SB_H)
                pe.wait_ge(ml_y, ML_H)
                turn("ysb", tok)
            if u == TURN_ML:
                pe.wait_ge(yml_ready, 1)
                turn("yml", mlo)
            i = u - MB0
            if 0 <= i < LAST_U["lru"] - MB0:
                if i >= 2:
                    mb_values(i - 2)
                if 1 <= i <= MB_H:
                    mb_turn(i - 1)
                if i < MB_H:
                    mb_scores(i)

    @block.scalar
    def _(act):
        steps = [0]
        activate = nc.scalar.activation

        def link(ins):
            steps[0] += 1
            ins.then_inc(act_step, 1)
            act.wait_ge(act_step, steps[0])

        def split(u):
            if u >= NU:
                return
            n, k, m = UNITS[u]
            w = width(n)
            act.wait_ge(landed[u % LANDS], land_count(u))
            if u >= PARTS:
                act.wait_ge(units_done, u - PARTS + 1)
            activate(whi[:, u % PARTS, 0:m, 0:w], land[:, u % LANDS, 0:m, 0:w], ACT.Copy).then_inc(hi_ready, 1)

        def square(j, src):
            activate(tok[:, 0, :], src[:, 0, :], ACT.Square, accum_out=squares[:, j, 0:1]).then_inc(sq_act, 1)

        def scale(j, src, count):
            act.wait_ge(rstd_ready, j + 1)
            activate(tok[:, 0, :], src[:, 0, :], ACT.Copy, scale=rstd[:, j, 0:1]).then_inc(norm_act, 1)

        def turn_split(stage, hi, k_to=0):
            _, kk, gain = [s for s in TURNS if s[0] == stage][0]
            for b in range(kk // 2):
                act.wait_ge(turned, TURN_AT[stage] + b + 1)
                if gain is None:
                    last = activate(hi[:, k_to + 2 * b:k_to + 2 * b + 2, :],
                                    M[b][:, :].rearrange("p (k t) -> p k t", k=2), ACT.Copy)
                else:
                    for i in range(2):
                        g = V_AT[gain] + 2 * b + i
                        last = activate(hi[:, k_to + 2 * b + i, :], M[b][:, i * T:(i + 1) * T], ACT.Copy,
                                        scale=vecs[:, g:g + 1])
                last.then_inc(turn_hi, 1)

        def product_done(name):
            act.wait_ge(units_done, LAST_U[name] + 1)

        def sb_logs(h):
            act.wait_ge(sb_z, h + 1)
            w = sbw[:, h % 2]
            if h >= 2:
                act.wait_ge(sb_r, h - 1)
            link(activate(w, M[h % 2][:, 0:3 * P], ACT.Abs))
            link(activate(w, w, ACT.Exp, scale=-1.0))
            activate(w, w, ACT.Ln, bias=1.0).then_inc(sb_log, 1)

        def sb_weights(h):
            act.wait_ge(sb_r, h + 1)
            if h >= 2:
                act.wait_ge(sb_av, h - 1)
            activate(sba[:, h % 2], M[h % 2][:, 0:3 * P], ACT.Exp).then_inc(sb_a, 1)

        def ml_weights(h):
            act.wait_ge(ml_s, h + 1)
            act.wait_ge(c_ready, 1)
            b, w = M[2 * (h % 2) + 1], sba[:, h % 2]
            activate(w[:, 0:T], b[:, 0:T], ACT.Exp, bias=c_col[:, 0, h:h + 1])
            activate(w[:, T:3 * P], b[:, P:T], ACT.Exp, bias=c_col[:, 1, h:h + 1]).then_inc(ml_w, 1)

        def ml_squares(h):
            act.wait_ge(ml_y, h + 1)
            for t in range(TT):
                last = activate(sbw[:, t, 0:T], mlo[:, t, h * ML_D:(h + 1) * ML_D], ACT.Square,
                                accum_out=ml_sq[:, t, h:h + 1])
            last.then_inc(ml_ss, 1)
            act.wait_ge(ml_ss, h + 1)

        def mb_exps(h):
            act.wait_ge(mb_max_ready, h + 1)
            s = mbs[:, h % 2]
            activate(s[:, 0:P], s[:, 0:P], ACT.Exp, bias=mb_max[:, h, 0:1], accum_out=mb_sum[:, h, 0:1])
            activate(s[:, P:3 * P], s[:, P:3 * P], ACT.Exp, bias=mb_max[:, h, 1:2],
                     accum_out=mb_sum[:, h, 1:2]).then_inc(mb_e, 1)

        def mb_weights(h):
            act.wait_ge(mb_pt, h + 1)
            if h >= 2:
                act.wait_ge(mb_av, h - 1)
            activate(mbp[:, h % 2], M[2 + h % 2][:, 0:3 * P], ACT.Copy).then_inc(mb_p, 1)

        def gla_exps():
            b = vecs[:, V_AT["gla_gate_b_2"]:V_AT["gla_gate_b_2"] + 1]
            act.wait_ge(g_gate, 1)
            link(activate(gla[:, 0], M[1][:, 0:T], ACT.Abs, bias=b))
            link(activate(gla[:, 0], gla[:, 0], ACT.Exp, scale=-1.0))
            activate(gla[:, 0], gla[:, 0], ACT.Ln, bias=1.0).then_inc(g_ln, 1)
            act.wait_ge(g_cum, 1)
            activate(gla[:, 3], gla[:, 1], ACT.Exp).then_inc(g_exp, 1)
            activate(gla[:, 4], gla[:, 1], ACT.Exp, scale=-1.0).then_inc(g_exp, 1)
            activate(gla[:, 5], gla[:, 2], ACT.Exp).then_inc(g_exp, 1)
            last = gla[:, 1].rearrange("p (n c) -> p n c", c=GLA_CHUNK)[:, :, GLA_CHUNK - 1]
            activate(gdec[:, :], last, ACT.Exp).then_inc(g_exp, 1)
            act.wait_ge(g_at, 1)
            for h in range(GLA_H):
                last = activate(gattn[:, h].rearrange("p t c -> p (t c)"), M[h][:, 0:T], ACT.Copy)
            last.then_inc(g_atc, 1)
            act.wait_ge(g_o, 1)
            activate(gsq[:].rearrange("p a b -> p (a b)"), M[3][:, :], ACT.Square).then_inc(g_osq, 1)

        def lru_log():
            lam = vecs[:, V_AT["lru_lambda_2"]:V_AT["lru_lambda_2"] + LC]
            link(activate(lamb[:, 0], lam, ACT.Abs))
            activate(lamb[:, 1], lamb[:, 0], ACT.Exp, scale=-1.0).then_inc(l_lam, 1)

        def lru_activations():
            act.wait_ge(l_gates, 1)
            for i, (at, name) in enumerate(((1, "lru_ba_2"), (2, "lru_bx_2"))):
                for c in range(LC):
                    for b in range(2):
                        bs = slice(64 * b, 64 * b + 64)
                        last = activate(lw[bs, at, c, :], M[2 * i + b][bs, c * T:(c + 1) * T], ACT.Sigmoid,
                                        bias=vecs[bs, V_AT[name] + c:V_AT[name] + c + 1])
            link(last)
            act.wait_ge(l_gin, 1)
            activate(lw[:, 9], lw[:, 8], ACT.Sigmoid, scale=GELU_C).then_inc(l_gel, 1)
            act.wait_ge(l_spn, 1)
            for c in range(LC):
                last = activate(lw[:, 3, c, :], lw[:, 1, c, :], ACT.Exp, scale=lamb[:, 6, c:c + 1])
            link(last)
            for c in range(LC):
                last = activate(lw[:, 4, c, :], lw[:, 1, c, :], ACT.Tanh, scale=lamb[:, 7, c:c + 1])
            last.then_inc(l_exp, 1)
            act.wait_ge(l_m2, 1)
            activate(lw[:, 4], lw[:, 6], ACT.Sqrt).then_inc(l_mult, 1)
            act.wait_ge(l_y, 1)
            activate(y2T_hi[:, 0:LC, :], lw[:, 7], ACT.Copy).then_inc(l_hi, 1)

        def moba_step(i):
            if 1 <= i <= MB_H:
                mb_weights(i - 1)
            if i < MB_H:
                mb_exps(i)

        act.wait_ge(x_in, 32)
        square(0, x_tok)
        act.wait_ge(small_in, 80)
        activate(w_if_hi[:], w_if[:], ACT.Copy).then_inc(if_hi, 1)
        scale(0, x_tok, 1)
        act.wait_ge(tab_done, 1)
        activate(tab[:, :], M[1][0:MB_H, :], ACT.Copy).then_inc(tab_ready, 1)
        split(0)
        act.wait_ge(vecs_ready, 1)
        turn_split("x", xT_hi)
        split(1)

        for u in range(NU):
            n = UNITS[u][0]
            name = GROUPS[n][0]
            ends = u == LAST_U[name]
            split(u + 2)
            if u == U_IF + 2:
                act.wait_ge(rows_ready, 1)
                link(activate(e_row[:, :], f_row[:, :], ACT.Abs))
                link(activate(e_row[:, :], e_row[:, :], ACT.Exp, scale=-1.0))
                activate(e_row[:, :], e_row[:, :], ACT.Ln, bias=1.0).then_inc(e_ready, 1)
            if u == U_IF + 6:
                act.wait_ge(cols_turned, 1)
                act.wait_ge(c_ready, 1)
                activate(floor_col[:].rearrange("p t h -> p (t h)"), M[2][:, TT * ML_H:2 * TT * ML_H], ACT.Exp,
                         scale=-1.0).then_inc(floor_ready, 1)
            i = u - SB0
            if 1 <= i <= SB_H:
                sb_weights(i - 1)
            if 0 <= i < SB_H:
                sb_logs(i)
            i = u - ML0
            if 0 <= i < ML_H:
                ml_weights(i)
            if 2 <= i < ML_H + 2:
                ml_squares(i - 2)
            if ends and name[:3] == "mlo":
                j = int(name[3])
                product_done(name)
                activate(mlo[:, :, j * NG:(j + 1) * NG], acc[:, n % 2], ACT.Exp, scale=-1.0).then_inc(read_act, 1)
            if ends and name[:3] in ("gsb", "gml", "gsc"):
                product_done(name)
                if name != "gsb0":
                    act.wait_ge(read_dve, reads_before(n - 1, "dve"))
                activate(gate[:], acc[:, n % 2], ACT.Sigmoid).then_inc(read_act, 1)
            if u == TURN_SB:
                turn_split("ysb", ysbT_hi)
            if u == TURN_ML:
                turn_split("yml", ymlT_hi)
            if ends and name[:3] == "scb":
                j = int(name[3])
                act.wait_ge(read_dve, reads_before(n, "dve"))
                activate(yscT_hi[:, 4 * j:4 * j + 4, :], conv[:], ACT.Copy).then_inc(ysc_hi, 1)
            if ends and name == "psc1":
                turn_split("merged", xT_hi)
            if ends and name == "out1":
                act.wait_ge(read_dve, reads_before(n, "dve"))
                square(1, x_tok)
                scale(1, x_tok, 2)
                turn_split("h2", xT_hi)
            if ends and name[:2] == "up":
                j = int(name[2:])
                product_done(name)
                activate(relu[:, j % 2, :], acc[:, n % 2].rearrange("p a b -> p (a b)"),
                         ACT.Relu).then_inc(relu_ready, 1)
                act.wait_ge(relu_ready, j + 1)
                activate(aT_hi[:, 4 * j:4 * j + 4, :].rearrange("p a b -> p (a b)"), relu[:, j % 2, :],
                         ACT.Square).then_inc(a_hi, 1)
            if ends and name == "down1":
                act.wait_ge(read_dve, reads_before(n, "dve"))
                square(2, x_tok)
                act.wait_ge(x_done, 1)
                square(3, x_tok)
                scale(3, x_tok, 3)
                turn_split("h3", xT_hi)
                lru_log()
            i = u - MB0
            if 0 <= i < LAST_U["lru"] - MB0:
                moba_step(i)
            if ends and name == "lru":
                for i in range(LAST_U["lru"] - MB0, MB_H + 2):
                    moba_step(i)
                act.wait_ge(read_dve, reads_before(G_AT["gout"], "dve"))
                activate(gsig[:], gout[:], ACT.Sigmoid).then_inc(g_sig, 1)
                gla_exps()
                turn_split("gla", y2T_hi, LC)
                turn_split("moba", y2T_hi, LC + 2)
                lru_activations()
            if ends and name == "mix1":
                act.wait_ge(read_dve, reads_before(n, "dve"))
                square(4, mixed)
                act.wait_ge(x_done, 2)
                square(5, x_tok)
                scale(5, x_tok, 4)
                turn_split("h4", xT_hi)
            if ends and name[:2] == "gu":
                j = int(name[2:])
                product_done(name)
                activate(sig2[:, j % 2, :], acc[:, n % 2, 0, :], ACT.Sigmoid).then_inc(sig2_ready, 1)
                act.wait_ge(read_dve, reads_before(n, "dve"))
                activate(a2T_hi[:, 2 * j:2 * j + 2, :].rearrange("p a b -> p (a b)"), act2[:, j % 2, :],
                         ACT.Copy).then_inc(act2_hi, 1)
            if ends and name == "dn1":
                act.wait_ge(read_dve, reads_before(n, "dve"))
                square(6, mixed)

    @block.vector
    def _(dve):
        v = nc.vector
        steps = [0]

        def link(ins):
            steps[0] += 1
            ins.then_inc(dve_step, 1)
            dve.wait_ge(dve_step, steps[0])

        def split(u):
            if u >= NU:
                return
            n, k, m = UNITS[u]
            w = width(n)
            dve.wait_ge(hi_ready, u + 1)
            dve.wait_ge(landed[u % LANDS], land_count(u))
            v.tensor_tensor(wlo[:, u % PARTS, 0:m, 0:w], land[:, u % LANDS, 0:m, 0:w],
                            whi[:, u % PARTS, 0:m, 0:w].bitcast(F32), ALU.subtract).then_inc(lo_ready, 1)

        def square(j, src):
            v.tensor_tensor_reduce(tok[:, 1, :], src[:, 1, :], src[:, 1, :], 1.0, 0.0, ALU.mult, ALU.add,
                                   squares[:, j, 1:2]).then_inc(sq_dve, 1)

        def scale(j, src):
            dve.wait_ge(rstd_ready, j + 1)
            v.tensor_scalar(tok[:, 1, :], src[:, 1, :], rstd[:, j, 1:2], None, ALU.mult).then_inc(norm_dve, 1)

        def turn_split(stage, hi, lo, k_to=0):
            _, kk, gain = [s for s in TURNS if s[0] == stage][0]
            for b in range(kk // 2):
                dve.wait_ge(turn_hi, TURN_AT[stage] + b + 1)
                ks = slice(k_to + 2 * b, k_to + 2 * b + 2)
                if gain is None:
                    last = v.tensor_tensor(lo[:, ks, :], M[b][:, :].rearrange("p (k t) -> p k t", k=2),
                                           hi[:, ks, :].bitcast(F32), ALU.subtract)
                else:
                    for i in range(2):
                        g, k = V_AT[gain] + 2 * b + i, k_to + 2 * b + i
                        last = v.scalar_tensor_tensor(out=lo[:, k, :], in0=M[b][:, i * T:(i + 1) * T],
                                                      scalar=vecs[:, g:g + 1], in1=hi[:, k, :].bitcast(F32),
                                                      op0=ALU.mult, op1=ALU.subtract)
                last.then_inc(turn_lo, 1)

        def product_done(name):
            dve.wait_ge(units_done, LAST_U[name] + 1)

        def sb_softplus(h):
            dve.wait_ge(sb_log, h + 1)
            w = sbw[:, h % 2]
            v.scalar_tensor_tensor(out=w, in0=M[h % 2][:, 0:3 * P], scalar=0.0, in1=w, op0=ALU.max,
                                   op1=ALU.add).then_inc(sb_t, 1)

        def sb_result(h):
            dve.wait_ge(sb_av, h + 1)
            v.tensor_copy(tok[:, :, h * SB_D:(h + 1) * SB_D],
                          M[2 + h % 2][:, 0:2 * SB_D].rearrange("p (t d) -> p t d", t=TT)).then_inc(sb_y, 1)

        def ml_products(h):
            dve.wait_ge(ml_wm, h + 1)
            w = sba[:, h % 2]
            v.tensor_tensor(w, M[2 * (h % 2)][:, 0:3 * P], w, ALU.mult).then_inc(ml_p, 1)

        def ml_result(h):
            dve.wait_ge(ml_num, h + 1)
            if h == 0:
                dve.wait_ge(floor_ready, 1)
            o, b = M[2 * (h % 2)], M[2 * (h % 2) + 1]
            link(v.tensor_copy(ml_den[:, 0], b[:, T:T + TT]))
            link(v.scalar_tensor_tensor(out=ml_den[:, 1], in0=ml_den[:, 0], scalar=-1.0, in1=ml_den[:, 0],
                                        op0=ALU.mult, op1=ALU.max))
            link(v.tensor_tensor(ml_den[:, 2], ml_den[:, 1], floor_col[:, :, h], ALU.max))
            link(v.reciprocal(ml_den[:, 3], ml_den[:, 2]))
            for t in range(TT):
                y = mlo[:, t, h * ML_D:(h + 1) * ML_D]
                last = v.scalar_tensor_tensor(out=y, in0=o[:, t * ML_D:(t + 1) * ML_D],
                                              scalar=ml_den[:, 3, t:t + 1], in1=y, op0=ALU.mult, op1=ALU.mult)
            last.then_inc(ml_y, 1)

        def conv_taps(j):
            for tap in reversed(range(CONV_K)):
                for i in range(4):
                    k = 4 * j + i
                    w = vecs[:, V_AT["conv_w"] + tap * KD + k:V_AT["conv_w"] + tap * KD + k + 1]
                    z = zT[:, k, tap:tap + T]
                    if tap == CONV_K - 1:
                        last = v.tensor_scalar(conv[:, i, :], z, w, None, ALU.mult)
                    else:
                        last = v.scalar_tensor_tensor(out=conv[:, i, :], in0=z, scalar=w, in1=conv[:, i, :],
                                                      op0=ALU.mult, op1=ALU.add)
                link(last)

        def mb_logits(h):
            dve.wait_ge(mb_s, h + 1)
            if h == 0:
                dve.wait_ge(bias_in, 32)
            if h >= 2:
                dve.wait_ge(mb_pt, h - 1)
            s = mbs[:, h % 2]
            link(v.tensor_tensor(s, M[h % 2][:, 0:3 * P], bias[:, h, :], ALU.add))
            v.tensor_reduce(mb_max[:, h, 0:1], s[:, 0:P], AX.X, ALU.max)
            link(v.tensor_reduce(mb_max[:, h, 1:2], s[:, P:3 * P], AX.X, ALU.max))
            v.tensor_scalar(mb_max[:, h, :], mb_max[:, h, :], -1.0, None, ALU.mult).then_inc(mb_max_ready, 1)

        def mb_result(h):
            dve.wait_ge(mb_av, h + 1)
            link(v.reciprocal(mb_inv[:, h, :], mb_sum[:, h, :]))
            for t in range(TT):
                last = v.tensor_scalar(tok[:, t, 2 * P + h * MB_D:2 * P + (h + 1) * MB_D],
                                       M[h % 2][:, t * MB_D:(t + 1) * MB_D], mb_inv[:, h, t:t + 1], None, ALU.mult)
            last.then_inc(mb_y, 1)

        def gla_steps():
            b = vecs[:, V_AT["gla_gate_b_2"]:V_AT["gla_gate_b_2"] + 1]
            dve.wait_ge(glr_turned, 1)
            v.tensor_copy(glrT[:, :], M[0][0:GLA_RANK, 0:T]).then_inc(glr_ready, 1)
            dve.wait_ge(g_ln, 1)
            link(v.tensor_scalar(gla[:, 1], M[1][:, 0:T], b, 0.0, ALU.add, ALU.min))
            link(v.tensor_tensor(gla[:, 1], gla[:, 1], gla[:, 0], ALU.subtract))
            link(v.tensor_scalar(gla[:, 2], gla[:, 1], 1.0 / GLA_TAU, None, ALU.mult))
            dve.wait_ge(g_sets, 1)
            link(v.tensor_tensor_scan(gla[:, 1], gnew[:, :], gla[:, 2], 0.0, ALU.mult, ALU.add))
            cum = gla[:, 1].rearrange("p (n c) -> p n c", c=GLA_CHUNK)
            last = cum[:, :, GLA_CHUNK - 1:GLA_CHUNK].to_broadcast([P, T // GLA_CHUNK, GLA_CHUNK])
            v.tensor_tensor(gla[:, 2].rearrange("p (n c) -> p n c", c=GLA_CHUNK), last, cum,
                            ALU.subtract).then_inc(g_cum, 1)
            dve.wait_ge(g_exp, 4)
            v.scalar_tensor_tensor(out=qd[:, :], in0=gqk[:, 0, :], scalar=float(GLA_DK) ** -0.5, in1=gla[:, 3],
                                   op0=ALU.mult, op1=ALU.mult).then_inc(g_qk, 1)
            v.tensor_tensor(kd[:, :], gqk[:, 1, :], gla[:, 4], ALU.mult).then_inc(g_qk, 1)
            v.tensor_tensor(kl[:, :], gqk[:, 1, :], gla[:, 5], ALU.mult).then_inc(g_qk, 1)
            dve.wait_ge(kl_turned, 1)
            v.tensor_copy(kl_tok[:].rearrange("p t c -> p (t c)"), M[3][:, 0:T]).then_inc(kl_ready, 1)
            dve.wait_ge(g_kv, 1)
            for n in range(3):
                for h in range(GLA_H):
                    ps = slice(h * GLA_DK, (h + 1) * GLA_DK)
                    vs = slice(h * GLA_DV, (h + 1) * GLA_DV)
                    last = v.scalar_tensor_tensor(out=gstate[ps, n + 1, vs], in0=gstate[ps, n, vs],
                                                  scalar=gdec[ps, n:n + 1], in1=M[n][ps, vs], op0=ALU.mult,
                                                  op1=ALU.add)
                if n < 2:
                    link(last)
                else:
                    last.then_inc(g_state, 1)
            dve.wait_ge(g_sig, 1)
            link(v.tensor_tensor(gsig[:], gsig[:], gout[:], ALU.mult))
            dve.wait_ge(g_osq, 1)
            v.tensor_reduce(gss[:, 0, :], gsq[:], AX.X, ALU.add).then_inc(g_oss, 1)
            dve.wait_ge(g_rs, 1)
            link(v.tensor_tensor(gsq[:], M[3][:, :].rearrange("p (a b) -> p a b", b=GLA_DV),
                                 gss[:, 2, :].unsqueeze(2).to_broadcast([P, TT * GLA_H, GLA_DV]), ALU.mult))
            v.tensor_tensor(tok[:, :, 0:GD], gsq[:].rearrange("p (t h) b -> p t (h b)", t=TT), gsig[:],
                            ALU.mult).then_inc(g_y, 1)

        def lru_decay():
            dve.wait_ge(l_lam, 1)
            e, w, w2, s = lamb[:, 1], lamb[:, 2], lamb[:, 3], lamb[:, 4]
            link(v.tensor_scalar(w, e, 2.0, None, ALU.add))
            link(v.reciprocal(w2, w))
            link(v.tensor_tensor(w, e, w2, ALU.mult))
            link(v.tensor_tensor(w2, w, w, ALU.mult))
            link(v.tensor_scalar(s, w2, 1.0 / 17, 1.0 / 15, ALU.mult, ALU.add))
            for odd in (13, 11, 9, 7, 5, 3, 1):
                link(v.tensor_tensor(s, s, w2, ALU.mult))
                link(v.tensor_scalar(s, s, 1.0 / odd, None, ALU.add))
            link(v.tensor_tensor(s, s, w, ALU.mult))
            lam = vecs[:, V_AT["lru_lambda_2"]:V_AT["lru_lambda_2"] + LC]
            link(v.tensor_scalar(lamb[:, 5], lam, -1.0, 0.0, ALU.mult, ALU.max))
            link(v.scalar_tensor_tensor(out=s, in0=s, scalar=2.0, in1=lamb[:, 5], op0=ALU.mult, op1=ALU.add))
            v.tensor_scalar(lamb[:, 6], s, -LRU_C, None, ALU.mult)
            v.tensor_scalar(lamb[:, 7], s, LRU_C, None, ALU.mult).then_inc(l_spn, 1)

        def lru_conv():
            dve.wait_ge(g_sets, 1)
            for tap in reversed(range(LRU_TAPS)):
                for c in range(LC):
                    r = V_AT["lru_conv_w_2"] + tap * LC + c
                    w, x = vecs[:, r:r + 1], lruT[:, c, tap:tap + T]
                    if tap == LRU_TAPS - 1:
                        last = v.tensor_scalar(lw[:, 0, c, :], x, w, None, ALU.mult)
                    else:
                        last = v.scalar_tensor_tensor(out=lw[:, 0, c, :], in0=x, scalar=w, in1=lw[:, 0, c, :],
                                                      op0=ALU.mult, op1=ALU.add)
                link(last)
            for c in range(LC):
                r = V_AT["lru_conv_b_2"] + c
                last = v.tensor_scalar(lw[:, 0, c, :], lw[:, 0, c, :], vecs[:, r:r + 1], None, ALU.add)
            last.then_inc(l_conv, 1)
            g = lruT[:, LC:2 * LC, LRU_TAPS - 1:]
            link(v.tensor_tensor(lw[:, 8], g, g, ALU.mult))
            link(v.tensor_scalar(lw[:, 8], lw[:, 8], 0.044715, 1.0, ALU.mult, ALU.add))
            v.tensor_tensor(lw[:, 8], lw[:, 8], g, ALU.mult).then_inc(l_gin, 1)

        def lru_scan():
            dve.wait_ge(l_exp, 1)
            p, q, m2 = lw[:, 4], lw[:, 5], lw[:, 6]
            link(v.tensor_scalar(q, p, 1.0, None, ALU.add))
            link(v.reciprocal(q, q))
            link(v.scalar_tensor_tensor(out=m2, in0=p, scalar=2.0, in1=q, op0=ALU.mult, op1=ALU.mult))
            v.tensor_scalar(m2, m2, ROOT_FLOOR, None, ALU.max).then_inc(l_m2, 1)
            link(v.tensor_tensor(lw[:, 7], lw[:, 2], lw[:, 0], ALU.mult))
            link(v.tensor_tensor(lw[:, 9], lw[:, 9], lruT[:, LC:2 * LC, LRU_TAPS - 1:], ALU.mult))
            dve.wait_ge(l_mult, 1)
            link(v.memset(lw[:, 4, :, 0:1], 1.0))
            link(v.tensor_tensor(lw[:, 5], lw[:, 7], lw[:, 4], ALU.mult))
            for c in range(LC):
                last = v.tensor_tensor_scan(lw[:, 6, c, :], lw[:, 3, c, :], lw[:, 5, c, :], 0.0, ALU.mult, ALU.add)
            link(last)
            v.tensor_tensor(lw[:, 7], lw[:, 6], lw[:, 9], ALU.mult).then_inc(l_y, 1)
            dve.wait_ge(l_hi, 1)
            dve.wait_ge(l_y, 1)
            v.tensor_tensor(y2T_lo[:, 0:LC, :], lw[:, 7], y2T_hi[:, 0:LC, :].bitcast(F32),
                            ALU.subtract).then_inc(l_lo, 1)

        def moba_step(i):
            if i >= 2:
                mb_result(i - 2)
            if i < MB_H:
                mb_logits(i)

        def residual(j, gain, done):
            dve.wait_ge(rstd_ready, j + 1)
            for t in range(TT):
                link(v.scalar_tensor_tensor(out=mixed[:, t, :], in0=mixed[:, t, :], scalar=rstd[:, j, t:t + 1],
                                            in1=gain[:, :], op0=ALU.mult, op1=ALU.mult))
                last = v.tensor_tensor(x_tok[:, t, :], x_tok[:, t, :], mixed[:, t, :], ALU.add)
                if done > 1 or t == TT - 1:
                    last.then_inc(x_done, 1)

        dve.wait_ge(x_in, 32)
        square(0, x_tok)
        link(v.memset(one_row[:, :], 1.0))
        dve.wait_ge(vecs_turned, 1)
        v.tensor_copy(vecs[:, :], M[0][:, 0:V_ROWS]).then_inc(vecs_ready, 1)
        scale(0, x_tok)
        dve.wait_ge(if_hi, 1)
        v.tensor_tensor(w_if_lo[:], w_if[:], w_if_hi[:].bitcast(F32), ALU.subtract).then_inc(if_lo, 1)
        split(0)
        dve.wait_ge(vecs_ready, 1)
        turn_split("x", xT_hi, xT_lo)
        split(1)

        for u in range(NU):
            n = UNITS[u][0]
            name = GROUPS[n][0]
            ends = u == LAST_U[name]
            flat = acc[:, n % 2].rearrange("p a b -> p (a b)")
            split(u + 2)
            if u == U_IF:
                dve.wait_ge(if_done, 1)
                v.tensor_tensor(if_tok[:], M[3][:, 0:TT * 2 * ML_H].rearrange("p (t c) -> p t c", t=TT),
                                b_if[:].unsqueeze(1).to_broadcast([P, TT, 2 * ML_H]), ALU.add).then_inc(if_ready, 1)
            if u == U_IF + 2:
                dve.wait_ge(rows_turned, 1)
                link(v.tensor_copy(i_row[:, :], M[2][0:ML_H, 0:T]))
                v.tensor_copy(f_row[:, :], M[2][0:ML_H, T:2 * T]).then_inc(rows_ready, 1)
            if u == U_IF + 4:
                dve.wait_ge(e_ready, 1)
                link(v.scalar_tensor_tensor(out=f_row[:, :], in0=f_row[:, :], scalar=0.0, in1=e_row[:, :],
                                            op0=ALU.min, op1=ALU.subtract))
                link(v.tensor_tensor_scan(bm_row[:, :], one_row[:, :], f_row[:, :], 0.0, ALU.mult, ALU.add))
                link(v.tensor_tensor(i_row[:, :], i_row[:, :], bm_row[:, :], ALU.subtract))
                link(v.tensor_tensor_scan(negm_row[:, :], i_row[:, :], i_row[:, :], 0.0, ALU.max, ALU.max))
                link(v.tensor_tensor(bm_row[:, :], bm_row[:, :], negm_row[:, :], ALU.add))
                v.tensor_scalar(negm_row[:, :], negm_row[:, :], -1.0, None, ALU.mult).then_inc(scans_ready, 1)
            if u == U_IF + 6:
                dve.wait_ge(cols_turned, 1)
                v.tensor_copy(c_col[:].rearrange("p t h -> p (t h)"), M[2][:, 0:TT * ML_H]).then_inc(c_ready, 1)
            i = u - SB0
            if 0 <= i < SB_H:
                sb_softplus(i)
            if 2 <= i < SB_H + 2:
                sb_result(i - 2)
            i = u - ML0
            if 0 <= i < ML_H:
                ml_products(i)
            if 1 <= i <= ML_H:
                ml_result(i - 1)
            if ends and name[:3] in ("sbq", "sbk", "mlq", "mlk"):
                j = int(name[3])
                to = {"sbq": sbqT, "sbk": sbkT, "mlq": mlqT, "mlk": mlkT}[name[:3]]
                by = {"sbq": SB_D ** -0.5, "mlk": ML_D ** -0.5}.get(name[:3], 1.0)
                product_done(name)
                v.tensor_scalar(to[:, 4 * j:4 * j + 4, :].rearrange("p a b -> p (a b)"), flat, by, None,
                                ALU.mult).then_inc(read_dve, 1)
            if ends and name[:3] in ("sbv", "mlv"):
                j = int(name[3])
                product_done(name)
                v.tensor_copy((sbv if name[0] == "s" else mlv)[:, :, j * NG:(j + 1) * NG],
                              acc[:, n % 2]).then_inc(read_dve, 1)
            if ends and name[:3] == "mlo":
                j = int(name[3])
                dve.wait_ge(read_act, reads_before(n, "act"))
                s = mlo[:, :, j * NG:(j + 1) * NG]
                link(v.tensor_scalar(s, s, 1.0, None, ALU.add))
                link(v.reciprocal(s, s))
            if ends and name[:3] == "scc":
                j = int(name[3])
                product_done(name)
                v.tensor_copy(cT[:, 4 * j:4 * j + 4, :].rearrange("p a b -> p (a b)"), flat).then_inc(read_dve, 1)
            if ends and name[:3] == "scu":
                j = int(name[3])
                product_done(name)
                if j == 0:
                    link(v.memset(zT[:, :, 0:CONV_K - 1], 0.0))
                v.tensor_tensor(zT[:, 4 * j:4 * j + 4, CONV_K - 1:], flat.rearrange("p (a b) -> p a b", b=T),
                                cT[:, 4 * j:4 * j + 4, :], ALU.mult).then_inc(read_dve, 1)
                dve.wait_ge(read_dve, reads_before(n, "dve"))
                if j == 0:
                    conv_taps(0)
            if ends and name[:3] == "scb":
                j = int(name[3])
                product_done(name)
                v.tensor_tensor(conv[:].rearrange("p a b -> p (a b)"), flat,
                                conv[:].rearrange("p a b -> p (a b)"), ALU.mult).then_inc(read_dve, 1)
                dve.wait_ge(read_dve, reads_before(n, "dve"))
                dve.wait_ge(ysc_hi, j + 1)
                v.tensor_tensor(yscT_lo[:, 4 * j:4 * j + 4, :], conv[:], yscT_hi[:, 4 * j:4 * j + 4, :].bitcast(F32),
                                ALU.subtract).then_inc(ysc_lo, 1)
                if j == 0:
                    dve.wait_ge(ysc_lo, 1)
                    conv_taps(1)
            if u == TURN_SB:
                turn_split("ysb", ysbT_hi, ysbT_lo)
                dve.wait_ge(ml_rs, 1)
                y = mlo[:].rearrange("p t (h d) -> p (t h) d", d=ML_D)
                v.tensor_tensor(y, y, ml_rstd[:].rearrange("p t h -> p (t h)").unsqueeze(2).to_broadcast(
                    [P, TT * ML_H, ML_D]), ALU.mult).then_inc(yml_ready, 1)
            if u == TURN_ML:
                turn_split("yml", ymlT_hi, ymlT_lo)
            if ends and name[:3] in ("psb", "pml", "psc"):
                j = int(name[3])
                product_done(name)
                dve.wait_ge(read_act, reads_before(n - 1, "act"))
                m = tok[:, :, j * NG:(j + 1) * NG]
                if name[:3] == "psb":
                    v.tensor_tensor(m, acc[:, n % 2], gate[:], ALU.mult).then_inc(read_dve, 1)
                else:
                    link(v.tensor_tensor(gated[:], acc[:, n % 2], gate[:], ALU.mult))
                    v.tensor_tensor(m, m, gated[:], ALU.add).then_inc(read_dve, 1)
            if ends and name == "psc1":
                turn_split("merged", xT_hi, xT_lo)
            if ends and name[:3] == "out" or ends and name[:4] == "down":
                j = int(name[-1])
                product_done(name)
                x = x_tok[:, :, j * NG:(j + 1) * NG]
                v.tensor_tensor(x, acc[:, n % 2], x, ALU.add).then_inc(read_dve, 1)
            if ends and name == "out1":
                dve.wait_ge(read_dve, reads_before(n, "dve"))
                square(1, x_tok)
                scale(1, x_tok)
                turn_split("h2", xT_hi, xT_lo)
            if ends and name[:2] == "up":
                j = int(name[2:])
                dve.wait_ge(relu_ready, j + 1)
                v.scalar_tensor_tensor(out=relu2[:, j % 2, :], in0=flat, scalar=0.0, in1=relu[:, j % 2, :],
                                       op0=ALU.max, op1=ALU.mult).then_inc(read_dve, 1)
                dve.wait_ge(read_dve, reads_before(n, "dve"))
                dve.wait_ge(a_hi, j + 1)
                v.tensor_tensor(aT_lo[:, 4 * j:4 * j + 4, :].rearrange("p a b -> p (a b)"), relu2[:, j % 2, :],
                                aT_hi[:, 4 * j:4 * j + 4, :].rearrange("p a b -> p (a b)").bitcast(F32),
                                ALU.subtract).then_inc(a_lo, 1)
            if ends and name == "down1":
                dve.wait_ge(read_dve, reads_before(n, "dve"))
                square(2, x_tok)
                dve.wait_ge(rstd_ready, 3)
                dve.wait_ge(gain_in, 16)
                for t in range(TT):
                    last = v.scalar_tensor_tensor(out=x_tok[:, t, :], in0=x_tok[:, t, :], scalar=rstd[:, 2, t:t + 1],
                                                  in1=gain_a[:, :], op0=ALU.mult, op1=ALU.mult)
                last.then_inc(x_done, 1)
                dve.wait_ge(x_done, 1)
                square(3, x_tok)
                scale(3, x_tok)
                turn_split("h3", xT_hi, xT_lo)
                lru_decay()
            if ends and name in ("mq", "mk", "gqk", "mv", "gv", "gout", "lru"):
                product_done(name)
                if name in ("mq", "mk"):
                    last = v.tensor_scalar((mbq if name == "mq" else mbk)[:].rearrange("p a b -> p (a b)"), flat,
                                           MB_D ** -0.5 if name == "mq" else 1.0, None, ALU.mult)
                elif name == "gqk":
                    last = v.tensor_copy(gqk[:].rearrange("p a b -> p (a b)"), acc[:, n % 2, 0, :])
                elif name == "lru":
                    last = v.tensor_copy(lruT[:, :, LRU_TAPS - 1:], flat.rearrange("p (a b) -> p a b", b=T))
                else:
                    to = {"mv": mbv, "gv": gv, "gout": gout}[name]
                    last = v.tensor_copy(to[:], acc[:, n % 2, :, 0:width(n)])
                last.then_inc(read_dve, 1)
            i = u - MB0
            if 0 <= i < LAST_U["lru"] - MB0:
                moba_step(i)
            if ends and name == "lru":
                for i in range(LAST_U["lru"] - MB0, MB_H + 2):
                    moba_step(i)
                gla_steps()
                turn_split("gla", y2T_hi, y2T_lo, LC)
                turn_split("moba", y2T_hi, y2T_lo, LC + 2)
                dve.wait_ge(read_dve, reads_before(n, "dve"))
                lru_conv()
                lru_scan()
            if ends and name[:3] == "mix" or ends and name[:2] == "dn":
                j = int(name[-1])
                product_done(name)
                v.tensor_copy(mixed[:, :, j * NG:(j + 1) * NG], acc[:, n % 2]).then_inc(read_dve, 1)
            if ends and name == "mix1":
                dve.wait_ge(read_dve, reads_before(n, "dve"))
                square(4, mixed)
                dve.wait_ge(late_in, LATE)
                residual(4, gain_b, 1)
                dve.wait_ge(x_done, 2)
                square(5, x_tok)
                scale(5, x_tok)
                turn_split("h4", xT_hi, xT_lo)
            if ends and name[:2] == "gu":
                j = int(name[2:])
                dve.wait_ge(sig2_ready, j + 1)
                link(v.tensor_tensor(sig2[:, j % 2, :], acc[:, n % 2, 0, :], sig2[:, j % 2, :], ALU.mult))
                v.tensor_tensor(act2[:, j % 2, :], acc[:, n % 2, 1, :], sig2[:, j % 2, :],
                                ALU.mult).then_inc(read_dve, 1)
                dve.wait_ge(act2_hi, j + 1)
                v.tensor_tensor(a2T_lo[:, 2 * j:2 * j + 2, :].rearrange("p a b -> p (a b)"), act2[:, j % 2, :],
                                a2T_hi[:, 2 * j:2 * j + 2, :].rearrange("p a b -> p (a b)").bitcast(F32),
                                ALU.subtract).then_inc(act2_lo, 1)
            if ends and name == "dn1":
                dve.wait_ge(read_dve, reads_before(n, "dve"))
                square(6, mixed)
                residual(6, gain_c, 2)

    @block.gpsimd
    def _(pool):
        g = nc.gpsimd
        steps = [0]

        def link(ins):
            steps[0] += 1
            ins.then_inc(pool_step, 1)
            pool.wait_ge(pool_step, steps[0])

        signalled = {}

        def signal(ins, to):
            signalled[to] = signalled.get(to, 0) + 1
            ins.then_inc(to, 1)
            pool.wait_ge(to, signalled[to])

        def inverse_root(j):
            pool.wait_ge(sq_act, j + 1)
            pool.wait_ge(sq_dve, j + 1)
            link(g.tensor_scalar(mean_sq[:, j, :], squares[:, j, :], 1.0 / D, EPS, ALU.mult, ALU.add))
            signal(g.tensor_tensor(rstd[:, j, :], mean_sq[:, j, :], mhalf[:].to_broadcast([P, TT]),
                                   ALU.pow), rstd_ready)

        def keep(view, above):
            w = view.rearrange("p (a c) -> p a c", c=P)[:, 0:3:2, :]
            return g.affine_select(out=w, in_=w, pattern=[[0, 2], [1, P]], compare_op=above, fill=0.0, base=0,
                                   channel_multiplier=-1)

        link(g.memset(mhalf[:], -0.5))
        signal(g.memset(rel33[BUCKETS:BUCKETS + 1, :], 1.0), pool_set)
        inverse_root(0)
        for i in range(SB_H + 1):
            if i >= 1:
                pool.wait_ge(sb_a, i)
                signal(keep(sba[:, (i - 1) % 2], ALU.is_gt), sb_am)
            if i < SB_H:
                pool.wait_ge(sb_t, i + 1)
                signal(keep(sbw[:, i % 2], ALU.is_gt), sb_tm)
        for h in range(ML_H):
            pool.wait_ge(ml_w, h + 1)
            signal(keep(sba[:, h % 2], ALU.is_ge), ml_wm)
        pool.wait_ge(ml_ss, ML_H)
        link(g.tensor_scalar(ml_ms[:], ml_sq[:], 1.0 / ML_D, EPS, ALU.mult, ALU.add))
        signal(g.tensor_tensor(ml_rstd[:].rearrange("p t h -> p (t h)"), ml_ms[:].rearrange("p t h -> p (t h)"),
                               mhalf[:].to_broadcast([P, TT * ML_H]), ALU.pow), ml_rs)
        inverse_root(1)
        inverse_root(2)
        inverse_root(3)
        link(g.memset(gnew[:, :], 1.0))
        link(g.memset(gnew[:, :].rearrange("p (n c) -> p n c", c=GLA_CHUNK)[:, :, 0:1], 0.0))
        link(g.memset(lruT[:, :, 0:LRU_TAPS - 1], 0.0))
        signal(g.memset(gstate[:], 0.0), g_sets)
        pool.wait_ge(g_atc, 1)
        link(g.affine_select(out=gattn[:], in_=gattn[:], pattern=[[0, GLA_H], [0, TT], [1, P]],
                             compare_op=ALU.is_ge, fill=0.0, base=0, channel_multiplier=-1))
        signal(g.memset(gattn[0:GLA_CHUNK, :, :, GLA_CHUNK:P], 0.0), g_atm)
        pool.wait_ge(g_oss, 1)
        link(g.tensor_scalar(gss[:, 1, :], gss[:, 0, :], 1.0 / GLA_DV, EPS, ALU.mult, ALU.add))
        signal(g.tensor_tensor(gss[:, 2, :], gss[:, 1, :], mhalf[:].to_broadcast([P, TT * GLA_H]),
                               ALU.pow), g_rs)
        inverse_root(4)
        inverse_root(5)
        inverse_root(6)

    ctx.close()


INPUTS = ["x", "norm_mix_g", "w_in", "b_if", "ml_norm_g", "conv_w", "w_ml_proj", "w_sc_proj", "w_sb_proj",
          "w_out", "norm_mlp_g", "w_up", "w_down", "norm_final_g", "pre_mix_norm_2", "post_mix_norm_2",
          "pre_ffn_norm_2", "post_ffn_norm_2", "w_in_2", "w_out_2", "lru_conv_w_2", "lru_conv_b_2",
          "lru_wa_2", "lru_ba_2", "lru_wx_2", "lru_bx_2", "lru_lambda_2", "gla_gate_w2_2", "gla_gate_b_2",
          "gla_norm_2", "rel_bias_2", "w_ffn_gate_2", "w_ffn_up_2", "w_ffn_down_2"]


def constants():
    import numpy as np

    con = np.zeros((P, K_END), np.float32)
    con[:, K_ID:K_ID + P] = np.eye(P)
    con[:, K_TRI:K_TRI + P] = -np.tril(np.ones((P, P)))
    con[:, K_ONES:K_ONES + P] = -1.0
    sel = np.repeat(np.eye(ML_H), P, axis=1).astype(np.float32)
    hot = np.zeros((BUCKETS + 1, 2 * T), np.float32)
    exact = BUCKETS // 2
    for j in range(2 * T):
        n = T - 1 - j
        if n < 0:
            hot[BUCKETS, j] = MASKED
            continue
        far = exact + int(np.float32(np.log(np.float32(max(n, 1) / exact))) / np.float32(np.log(128 / exact))
                          * np.float32(BUCKETS - exact))
        hot[n if n < exact else min(far, BUCKETS - 1), j] = 1.0
    return {"con": con, "sel": sel, "hot": hot}


def kernel(**inputs):
    import numpy as np
    import concourse.bacc as bacc
    from concourse.bass_utils import run_bass_kernel_spmd

    nc = bacc.Bacc("TRN2", target_bir_lowering=False, num_devices=1)
    vector_rows = dict(VECS)
    arrays = {}
    for name in INPUTS:
        a = np.asarray(inputs[name])
        if name in vector_rows:
            a = a.reshape(vector_rows[name], P)
        elif name == "lru_wa_2" or name == "lru_wx_2":
            a = a.reshape(a.shape[1:])
        elif name != "rel_bias_2":
            a = a.reshape(-1, a.shape[-1])
        arrays[name] = np.ascontiguousarray(a)
    arrays.update(constants())
    dram = {name: nc.dram_tensor("in_" + name, a.shape, F32, kind="ExternalInput").ap() for name, a in arrays.items()}
    out = nc.dram_tensor("out", (T, D), F32, kind="ExternalOutput").ap()
    build(nc, dram, out)
    r = run_bass_kernel_spmd(nc, [{"in_" + name: a for name, a in arrays.items()}], core_ids=[0])
    return r.results[0]["out"].reshape(1, T, D)
```

```python
from contextlib import ExitStack

import concourse.bass as bass
import concourse.mybir as mybir

F32 = mybir.dt.float32
F32R = mybir.dt.float32r
ALU = mybir.AluOpType
ACT = mybir.ActivationFunctionType
AX = mybir.AxisListType

P = 128
T = 256
TT = T // P
D = 1024
KD = D // P
NG = 512
UK = 4
EPS = 1e-6
MASKED = -1e30

ML_H, ML_D = 4, 256
SB_H, SB_D = 16, 64
CONV_K = 3
D_FF = 4 * D
KF = D_FF // P
C_MLQ, C_MLK, C_MLV, C_MLO = 0, D, 2 * D, 3 * D
C_IF = 4 * D
C_SCB = C_IF + 2 * ML_H
C_SCC, C_SCU = C_SCB + D, C_SCB + 2 * D
C_SBQ, C_SBK, C_SBV = C_SCB + 3 * D, C_SCB + 4 * D, C_SCB + 5 * D
C_GML, C_GSC, C_GSB = C_SCB + 6 * D, C_SCB + 7 * D, C_SCB + 8 * D

LRU_W, LRU_TAPS, LRU_C = 256, 4, 8.0
GLA_H, GLA_DK, GLA_DV, GLA_RANK, GLA_CHUNK, GLA_TAU = 4, 32, 64, 16, 64, 16.0
MB_H, MB_D = 8, 64
D_FF2 = 2816
KF2 = D_FF2 // P
GU = 256
C2_LRU = 0
C2_GQ = 2 * LRU_W
C2_GV = C2_GQ + 2 * GLA_H * GLA_DK
C2_GOUT = C2_GV + GLA_H * GLA_DV + GLA_RANK
C2_MQ = C2_GOUT + GLA_H * GLA_DV
C2_MK, C2_MV = C2_MQ + MB_H * MB_D, C2_MQ + 2 * MB_H * MB_D
BUCKETS = 32
ROOT_FLOOR = 2.0 ** -100
GELU_C = 2.0 * (2.0 / 3.141592653589793) ** 0.5

LANDS, PARTS = 3, 3

K_ID, K_TRI, K_ONES, K_END = 0, P, 2 * P, 3 * P

VECS = [("norm_mix_g", 8), ("norm_mlp_g", 8), ("pre_mix_norm_2", 8), ("pre_ffn_norm_2", 8),
        ("ml_norm_g", 8), ("conv_w", 24), ("lru_conv_w_2", 8), ("lru_conv_b_2", 2),
        ("lru_ba_2", 2), ("lru_bx_2", 2), ("lru_lambda_2", 2), ("gla_gate_b_2", 1),
        ("gla_norm_2", 2)]
V_AT = {}
V_ROWS = 0
for _name, _rows in VECS:
    V_AT[_name] = V_ROWS
    V_ROWS += _rows


def plan_groups():
    g = []

    def halves(name, weight, col, act, form, k=KD):
        for j in range(2):
            g.append((f"{name}{j}", weight, [(col + j * NG, NG)], k, act, form))

    halves("sbq", "w_in", C_SBQ, "xT", "feat")
    halves("sbk", "w_in", C_SBK, "xT", "feat")
    halves("sbv", "w_in", C_SBV, "xT", "tok")
    halves("mlq", "w_in", C_MLQ, "xT", "feat")
    halves("mlk", "w_in", C_MLK, "xT", "feat")
    halves("mlv", "w_in", C_MLV, "xT", "tok")
    halves("mlo", "w_in", C_MLO, "xT", "tok")
    halves("scc", "w_in", C_SCC, "xT", "feat")
    halves("scu", "w_in", C_SCU, "xT", "feat")
    halves("scb", "w_in", C_SCB, "xT", "feat")
    for b, col in (("sb", C_GSB), ("ml", C_GML), ("sc", C_GSC)):
        for j in range(2):
            g.append((f"g{b}{j}", "w_in", [(col + j * NG, NG)], KD, "xT", "tok"))
            g.append((f"p{b}{j}", f"w_{b}_proj", [(j * NG, NG)], KD, f"y{b}T", "tok"))
    halves("out", "w_out", 0, "xT", "tok")
    for j in range(D_FF // NG):
        g.append((f"up{j}", "w_up", [(j * NG, NG)], KD, "xT", "feat"))
    halves("down", "w_down", 0, "aT", "tok", KF)
    w2 = "w_in_2"
    g.append(("gv", w2, [(C2_GV, GLA_H * GLA_DV + GLA_RANK)], KD, "xT", "tok"))
    g.append(("lru", w2, [(C2_LRU, 2 * LRU_W)], KD, "xT", "feat"))
    g.append(("gqk", w2, [(C2_GQ, 2 * P)], KD, "xT", "feat"))
    g.append(("gout", w2, [(C2_GOUT, GLA_H * GLA_DV)], KD, "xT", "tok"))
    g.append(("mqk0", w2, [(C2_MQ, 2 * P), (C2_MK, 2 * P)], KD, "xT", "feat"))
    g.append(("mv", w2, [(C2_MV, NG)], KD, "xT", "tok"))
    g.append(("mqk1", w2, [(C2_MQ + 2 * P, 2 * P), (C2_MK + 2 * P, 2 * P)], KD, "xT", "feat"))
    halves("mix", "w_out_2", 0, "y2T", "tok")
    for j in range(D_FF2 // GU):
        g.append((f"gu{j}", ("w_ffn_gate_2", "w_ffn_up_2"), [(j * GU, GU), (j * GU, GU)], KD, "xT", "feat"))
    halves("dn", "w_ffn_down_2", 0, "a2T", "tok", KF2)
    return g


GROUPS = plan_groups()
G_AT = {grp[0]: n for n, grp in enumerate(GROUPS)}
UNITS = [(n, k, min(UK, grp[3] - k)) for n, grp in enumerate(GROUPS) for k in range(0, grp[3], UK)]
_at = UNITS.index((G_AT["mix0"], 0, UK))
UNITS[_at:_at + 4] = [(G_AT[f"mix{j}"], k, m) for k, m in ((0, 4), (4, 2), (6, 2)) for j in range(2)]
FIRST_U, LAST_U = {}, {}
for _u, (_n, _k, _m) in enumerate(UNITS):
    FIRST_U.setdefault(GROUPS[_n][0], _u)
    LAST_U[GROUPS[_n][0]] = _u
NU = len(UNITS)


def width(n):
    return sum(w for _, w in GROUPS[n][2])


def readers(name):
    if name[:3] == "mlo" or name[0:3] in ("gsb", "gml", "gsc"):
        return ("act",)
    if name[:2] in ("up", "gu"):
        return ("dve",)
    if name == "gout":
        return ("dve",)
    return ("dve",)


def reads_before(n, eng):
    return sum(eng in readers(GROUPS[m][0]) for m in range(n + 1))


TURNS = [("x", KD, "norm_mix_g"), ("ysb", KD, None), ("yml", KD, "ml_norm_g"), ("merged", KD, None),
         ("h2", KD, "norm_mlp_g"), ("h3", KD, "pre_mix_norm_2"), ("gla", 2, "gla_norm_2"),
         ("moba0", 2, None), ("moba1", 2, None), ("h4", KD, "pre_ffn_norm_2")]
TURN_AT = {}
_b = 0
for _name, _k, _ in TURNS:
    TURN_AT[_name] = _b
    _b += _k // 2

SB0 = LAST_U["sbv1"] + 1
ML0 = SB0 + SB_H + 2
U_IF = 1
TURN_SB = ML0 + 6
TURN_ML = TURN_SB + 2
B2 = FIRST_U["gv"]
MB_AT = [(B2 + 11, 4), (B2 + 12, 2), (B2 + 12, 4), (B2 + 13, 2), (B2 + 14, 1), (B2 + 14, 3), (B2 + 15, 1),
         (B2 + 15, 2), (B2 + 15, 4), (B2 + 16, 2), (B2 + 17, 1)]
MB_TURN0, MB_TURN1 = (B2 + 15, 3), (B2 + 17, 2)


def build(nc, dram, out):
    ctx = ExitStack()

    def sb(name, shape, dt=F32, stack=None):
        return (stack or ctx).enter_context(nc.sbuf_tensor(name, shape, dt))

    def sem(name):
        return ctx.enter_context(nc.semaphore(name))

    land = sb("land", [P, LANDS, UK, NG])
    whi = sb("whi", [P, PARTS, UK, NG], F32R)
    wlo = sb("wlo", [P, PARTS, UK, NG], F32R)
    xT_hi = sb("xT_hi", [P, KD, T], F32R)
    xT_lo = sb("xT_lo", [P, KD, T], F32R)
    x_tok = sb("x_tok", [P, TT, D])
    tok = sb("tok", [P, TT, D])
    con = sb("con", [P, K_END])
    rows = sb("rows", [P, P])
    vecs = sb("vecs", [P, V_ROWS])
    squares = sb("squares", [P, 7, TT])
    mean_sq = sb("mean_sq", [P, 7, TT])
    rstd = sb("rstd", [P, 7, TT])
    mhalf = sb("mhalf", [P, 1])
    ident = con[:, K_ID:K_ID + P]
    negtri = con[:, K_TRI:K_TRI + P]
    negones = con[:, K_ONES:K_ONES + P]

    mix, area = ExitStack(), ExitStack()
    sbqT = sb("sbqT", [P, KD, T], stack=area)
    sbkT = sb("sbkT", [P, KD, T], stack=area)
    sbv = sb("sbv", [P, TT, D], stack=area)
    area.close()
    cT = sb("cT", [P, KD, T], stack=mix)
    zT = sb("zT", [P, KD, T + CONV_K - 1], stack=mix)
    conv = sb("conv", [P, 4, T], stack=mix)
    sb("pad0", [P, KD * T - KD * (CONV_K - 1) - 4 * T], stack=mix)
    mlqT = sb("mlqT", [P, KD, T], stack=area)
    mlkT = sb("mlkT", [P, KD, T], stack=area)
    mlv = sb("mlv", [P, TT, D], stack=area)
    area.close()
    ymlT_hi = sb("ymlT_hi", [P, KD, T], F32R, stack=mix)
    ymlT_lo = sb("ymlT_lo", [P, KD, T], F32R, stack=mix)
    gate = sb("gate", [P, TT, NG], stack=mix)
    gated = sb("gated", [P, TT, NG], stack=mix)
    mlo = sb("mlo", [P, TT, D], stack=mix)
    ysbT_hi = sb("ysbT_hi", [P, KD, T], F32R, stack=mix)
    ysbT_lo = sb("ysbT_lo", [P, KD, T], F32R, stack=mix)
    sel = sb("sel", [ML_H, ML_H * P], stack=area)
    i_row = sb("i_row", [ML_H, T], stack=area)
    f_row = sb("f_row", [ML_H, T], stack=area)
    e_row = sb("e_row", [ML_H, T], stack=area)
    one_row = sb("one_row", [ML_H, T], stack=area)
    negm_row = sb("negm_row", [ML_H, T], stack=area)
    bm_row = sb("bm_row", [ML_H, T], stack=area)
    hot = sb("hot", [BUCKETS + 1, 2 * T], stack=area)
    tab = sb("tab", [MB_H, 2 * T], stack=area)
    rel33 = sb("rel33", [BUCKETS + 1, MB_H], stack=area)
    w_if = sb("w_if", [P, KD, 2 * ML_H], stack=area)
    w_if_hi = sb("w_if_hi", [P, KD, 2 * ML_H], F32R, stack=area)
    w_if_lo = sb("w_if_lo", [P, KD, 2 * ML_H], F32R, stack=area)
    area.close()
    yscT_hi = sb("yscT_hi", [P, KD, T], F32R, stack=mix)
    yscT_lo = sb("yscT_lo", [P, KD, T], F32R, stack=mix)
    sbw = sb("sbw", [P, 2, 3 * P], stack=mix)
    sba = sb("sba", [P, 2, 3 * P], stack=mix)
    if_tok = sb("if_tok", [P, TT, 2 * ML_H], stack=mix)
    b_if = sb("b_if", [P, 2 * ML_H], stack=mix)
    c_col = sb("c_col", [P, TT, ML_H], stack=mix)
    floor_col = sb("floor_col", [P, TT, ML_H], stack=mix)
    ml_den = sb("ml_den", [P, 4, TT], stack=mix)
    ml_sq = sb("ml_sq", [P, TT, ML_H], stack=mix)
    ml_ms = sb("ml_ms", [P, TT, ML_H], stack=mix)
    ml_rstd = sb("ml_rstd", [P, TT, ML_H], stack=mix)
    mix.close()

    ffn = ExitStack()
    aT_hi = sb("aT_hi", [P, KF, T], F32R, stack=ffn)
    aT_lo = sb("aT_lo", [P, KF, T], F32R, stack=ffn)
    relu = sb("relu", [P, 2, 2 * NG], stack=ffn)
    relu2 = sb("relu2", [P, 2, 2 * NG], stack=ffn)
    gain_a = sb("gain_a", [P, D], stack=ffn)
    ffn.close()

    two = ExitStack()
    y2T_hi = sb("y2T_hi", [P, KD, T], F32R, stack=two)
    y2T_lo = sb("y2T_lo", [P, KD, T], F32R, stack=two)
    gain_b = sb("gain_b", [P, D], stack=two)
    a2T_hi = sb("a2T_hi", [P, KF2, T], F32R, stack=area)
    a2T_lo = sb("a2T_lo", [P, KF2, T], F32R, stack=area)
    sig2 = sb("sig2", [P, 2, 2 * T], stack=area)
    act2 = sb("act2", [P, 2, 2 * T], stack=area)
    mixed = sb("mixed", [P, TT, D], stack=area)
    area.close()
    LC = LRU_W // P
    mbqk = sb("mbqk", [P, 2, 4, T], stack=two)
    mbv = sb("mbv", [P, TT, MB_H * MB_D], stack=two)
    bias = sb("bias", [P, MB_H, 3 * P], stack=two)
    lw = sb("lw", [P, 9, LC, T], stack=two)
    mbs = sb("mbs", [P, 3, 3 * P], stack=two)
    mbp = sb("mbp", [P, 2, 3 * P], stack=two)
    mb_max = sb("mb_max", [P, MB_H, TT], stack=two)
    mb_sum = sb("mb_sum", [P, MB_H, TT], stack=two)
    mb_inv = sb("mb_inv", [P, MB_H, TT], stack=two)
    GD = GLA_H * GLA_DV
    gv = sb("gv", [P, TT, GD + GLA_RANK], stack=two)
    gqk = sb("gqk", [P, 2, T], stack=two)
    gout = sb("gout", [P, TT, GD], stack=two)
    gsig = sb("gsig", [P, TT, GD], stack=two)
    glrT = sb("glrT", [GLA_RANK, T], stack=two)
    gw2 = sb("gw2", [GLA_RANK, P], stack=two)
    gla = sb("gla", [P, 6, T], stack=two)
    gdec = sb("gdec", [P, 4], stack=two)
    gnew = lw[:, 3, 0, :]
    qd, kd, kl = gla[:, 3, :], gla[:, 4, :], gla[:, 5, :]
    kl_tok = sb("kl_tok", [P, TT, P], stack=two)
    gattn = sb("gattn", [P, GLA_H, TT, P], stack=two)
    gstate = sb("gstate", [P, 4, GD], stack=two)
    gsq = gattn[:].rearrange("p h t c -> p (h t c)")[:, 0:TT * GD].rearrange("p (a b) -> p a b", b=GLA_DV)
    gss = sb("gss", [P, 3, TT * GLA_H], stack=two)
    lruT = sb("lruT", [P, 2 * LC, T + LRU_TAPS - 1], stack=two)
    wab = sb("wab", [P, 2, LC, 64], stack=two)
    lamb = sb("lamb", [P, 8, LC], stack=two)
    two.close()

    acc = ctx.enter_context(nc.psum_tensor("acc", [P, 2, 2, NG], F32))
    M = [ctx.enter_context(nc.psum_tensor(f"m{i}", [P, NG], F32)) for i in range(4)]

    landed = [sem(f"landed{i}") for i in range(LANDS)]
    x_in, rows_in, con_in, small_in, gain_in, late_in = (
        sem(n) for n in ("x_in", "rows_in", "con_in", "small_in", "gain_in", "late_in"))
    tab_out, copies_out, bias_in, stored = (sem(n) for n in ("tab_out", "copies_out", "bias_in", "stored"))
    hi_ready, lo_ready, units_done = sem("hi_ready"), sem("lo_ready"), sem("units_done")
    read_act, read_dve = sem("read_act"), sem("read_dve")
    turned, turn_hi, turn_lo = sem("turned"), sem("turn_hi"), sem("turn_lo")
    sq_act, sq_dve, rstd_ready = sem("sq_act"), sem("sq_dve"), sem("rstd_ready")
    norm_act, norm_dve = sem("norm_act"), sem("norm_dve")
    act_step, dve_step, pool_step = sem("act_step"), sem("dve_step"), sem("pool_step")
    vecs_turned, vecs_ready, tab_done, tab_ready = (
        sem(n) for n in ("vecs_turned", "vecs_ready", "tab_done", "tab_ready"))
    pool_set = sem("pool_set")
    if_hi, if_lo, if_done, if_ready = sem("if_hi"), sem("if_lo"), sem("if_done"), sem("if_ready")
    rows_turned, rows_ready, e_ready, scans_ready = (
        sem(n) for n in ("rows_turned", "rows_ready", "e_ready", "scans_ready"))
    cols_turned, c_ready, floor_ready = sem("cols_turned"), sem("c_ready"), sem("floor_ready")
    sb_z, sb_log, sb_t, sb_tm, sb_r, sb_a, sb_am, sb_av, sb_y = (
        sem(n) for n in ("sb_z", "sb_log", "sb_t", "sb_tm", "sb_r", "sb_a", "sb_am", "sb_av", "sb_y"))
    sig_o = sem("sig_o")
    ml_s, ml_w, ml_wm, ml_p, ml_num, ml_y, ml_ss, ml_rs, yml_ready = (
        sem(n) for n in ("ml_s", "ml_w", "ml_wm", "ml_p", "ml_num", "ml_y", "ml_ss", "ml_rs", "yml_ready"))
    ysc_hi, ysc_lo = sem("ysc_hi"), sem("ysc_lo")
    relu_ready, a_hi, a_lo = sem("relu_ready"), sem("a_hi"), sem("a_lo")
    x_done = sem("x_done")
    mb_s, mb_logit, mb_max_ready, mb_e, mb_pt, mb_p, mb_av, mb_y = (
        sem(n) for n in ("mb_s", "mb_logit", "mb_max_ready", "mb_e", "mb_pt", "mb_p", "mb_av", "mb_y"))
    g_sets, glr_turned, glr_ready, g_gate, g_ln, g_min, g_cum, g_exp, g_qk, g_at, g_atc, g_atm = (
        sem(n) for n in ("g_sets", "glr_turned", "glr_ready", "g_gate", "g_ln", "g_min", "g_cum", "g_exp",
                         "g_qk", "g_at", "g_atc", "g_atm"))
    kl_turned, kl_ready, g_kv, g_state, g_o, g_osq, g_oss, g_rs, g_y, g_sig = (
        sem(n) for n in ("kl_turned", "kl_ready", "g_kv", "g_state", "g_o", "g_osq", "g_oss", "g_rs", "g_y",
                         "g_sig"))
    l_conv, l_gates, l_sig, l_exp, l_m2, l_mult, l_y, l_hi, l_lo, l_gin, l_gel, l_lam, l_sp, l_spn = (
        sem(n) for n in ("l_conv", "l_gates", "l_sig", "l_exp", "l_m2", "l_mult", "l_y", "l_hi", "l_lo",
                         "l_gin", "l_gel", "l_lam", "l_sp", "l_spn"))
    sig2_ready, act2_hi, act2_lo = sem("sig2_ready"), sem("act2_hi"), sem("act2_lo")

    weights = {n: dram[n] for n in dram}
    by_distance = nc.dram_tensor("by_distance", (1, MB_H * 2 * T), F32, kind="Internal").ap()
    by_query = nc.dram_tensor("by_query", (P, MB_H * 2 * T), F32, kind="Internal").ap()

    def land_count(u):
        return 16 * sum(len(GROUPS[UNITS[v][0]][2]) for v in range(u % LANDS, u + 1, LANDS))

    block = ctx.enter_context(nc.Block())

    @block.sync
    def _(sp):
        sp.dma_start(x_tok[:, 0, :], dram["x"][0:P, :]).then_inc(x_in, 16)
        sp.dma_start(x_tok[:, 1, :], dram["x"][P:T, :]).then_inc(x_in, 16)
        sp.dma_start(con[:], dram["con"]).then_inc(con_in, 16)
        for name, n in VECS:
            sp.dma_start(rows[V_AT[name]:V_AT[name] + n, :], dram[name]).then_inc(rows_in, 16)

        def load(u):
            n, k, m = UNITS[u]
            _, weight, segs, *_ = GROUPS[n]
            if u >= LANDS:
                sp.wait_ge(lo_ready, u - LANDS + 1)
            at = 0
            for i, (col, w) in enumerate(segs):
                src = weights[weight if isinstance(weight, str) else weight[i]]
                sp.dma_start(land[:, u % LANDS, 0:m, at:at + w],
                             src[k * P:(k + m) * P, col:col + w].rearrange("(k p) n -> p k n", p=P)
                             ).then_inc(landed[u % LANDS], 16)
                at += w

        for u in range(NU):
            load(u)
            if u == 0:
                sp.dma_start(w_if[:], dram["w_in"][:, C_IF:C_IF + 2 * ML_H].rearrange(
                    "(k p) n -> p k n", p=P)).then_inc(small_in, 16)
                sp.dma_start(b_if[:], dram["b_if"].to_broadcast([P, 2 * ML_H])).then_inc(small_in, 16)
                sp.dma_start(hot[:], dram["hot"]).then_inc(small_in, 16)
                sp.dma_start(sel[:], dram["sel"]).then_inc(small_in, 16)
                sp.dma_start(rel33[0:BUCKETS, :], dram["rel_bias_2"]).then_inc(small_in, 16)
            if u == 2:
                sp.wait_ge(tab_ready, 1)
                sp.dma_start(by_distance.rearrange("a (h j) -> (a h) j", h=MB_H), tab[:]).then_inc(tab_out, 16)
            if u == SB0:
                sp.wait_ge(tab_out, 16)
                sp.dma_start(by_query, by_distance.to_broadcast([P, MB_H * 2 * T])).then_inc(copies_out, 16)
            if u == FIRST_U["up1"]:
                sp.wait_ge(turn_lo, TURN_AT["merged"] + 4)
                sp.wait_ge(turn_hi, TURN_AT["merged"] + 4)
                sp.dma_start(gain_a[:], dram["norm_final_g"].to_broadcast([P, D])).then_inc(gain_in, 16)
            if u == B2 + 1:
                sp.wait_ge(x_done, 1)
                sp.dma_start(gw2[:], dram["gla_gate_w2_2"]).then_inc(late_in, 16)
                for i, name in enumerate(("lru_wa_2", "lru_wx_2")):
                    for c in range(LC):
                        sp.dma_start(wab[:, i, c, :], dram[name][2 * c:2 * c + 2].rearrange("b i j -> (b i) j")
                                     ).then_inc(late_in, 16)
            if u == B2 + 5:
                sp.dma_start(gain_b[:], dram["post_mix_norm_2"].to_broadcast([P, D])).then_inc(gain_in, 16)
            if u == B2 + 9:
                sp.wait_ge(copies_out, 16)
                row = MB_H * 2 * T - 1
                sp.dma_start(bias[:, :, 0:P], bass.AP(by_query.tensor, T - 1, [[row, P], [2 * T, MB_H], [1, P]])
                             ).then_inc(bias_in, 16)
                sp.dma_start(bias[:, :, P:3 * P],
                             bass.AP(by_query.tensor, T - 1 - P, [[row, P], [2 * T, MB_H], [1, T]])
                             ).then_inc(bias_in, 16)
            if u == FIRST_U["dn0"]:
                sp.wait_ge(x_done, 2)
                sp.dma_start(gain_b[:], dram["post_ffn_norm_2"].to_broadcast([P, D])).then_inc(gain_in, 16)
        for t in range(TT):
            sp.wait_ge(x_done, 3 + t)
            sp.dma_start(out[t * P:(t + 1) * P, :], x_tok[:, t, :]).then_inc(stored, 16)
        sp.wait_ge(stored, 16 * TT)

    LATE = 16 * (1 + 2 * LC)

    @block.tensor
    def _(pe):
        mm = nc.tensor.matmul

        def lhs_of(act):
            return {"xT": (xT_hi, xT_lo), "ysbT": (ysbT_hi, ysbT_lo), "ymlT": (ymlT_hi, ymlT_lo),
                    "yscT": (yscT_hi, yscT_lo), "aT": (aT_hi, aT_lo), "y2T": (y2T_hi, y2T_lo),
                    "a2T": (a2T_hi, a2T_lo)}[act]

        def turned_ready(stage, tiles):
            pe.wait_ge(turn_hi, TURN_AT[stage] + (tiles + 1) // 2)
            pe.wait_ge(turn_lo, TURN_AT[stage] + (tiles + 1) // 2)

        def wait_operand(name, act, k1):
            if act == "xT":
                turned_ready("merged" if name[:3] == "out" else "h2" if name[:2] == "up" else
                             "h4" if name[:2] == "gu" else
                             "h3" if B2 <= FIRST_U[name] < FIRST_U["mix0"] else "x", k1)
            elif act == "ysbT":
                turned_ready("ysb", k1)
            elif act == "ymlT":
                turned_ready("yml", k1)
            elif act == "yscT":
                pe.wait_ge(ysc_hi, (k1 + 3) // 4)
                pe.wait_ge(ysc_lo, (k1 + 3) // 4)
            elif act == "aT":
                pe.wait_ge(a_hi, (k1 + 3) // 4)
                pe.wait_ge(a_lo, (k1 + 3) // 4)
            elif act == "a2T":
                pe.wait_ge(act2_hi, k1 // 2)
                pe.wait_ge(act2_lo, k1 // 2)
            elif k1 <= 2 * LC:
                pe.wait_ge(l_hi, 1)
                pe.wait_ge(l_lo, 1)
                turned_ready("gla", 2)
            else:
                turned_ready("moba0" if k1 <= 6 else "moba1", 2)

        def product(u, between):
            n, k0, m = UNITS[u]
            name, _, _, kk, act, form = GROUPS[n]
            xh, xl = lhs_of(act)
            w, s = width(n), u % PARTS
            if k0 == 0 and n >= 2:
                for eng, seen in (("act", read_act), ("dve", read_dve)):
                    if eng in readers(GROUPS[n - 2][0]):
                        pe.wait_ge(seen, reads_before(n - 2, eng))
            pe.wait_ge(hi_ready, u + 1)
            pe.wait_ge(lo_ready, u + 1)
            for k in range(m):
                first, end = k0 + k == 0, k0 + k == kk - 1
                if k > 0:
                    between(u, k)
                if k % 2 == 0:
                    wait_operand(name, act, k0 + k + 2)
                if form == "tok":
                    for t in range(TT):
                        to = acc[:, n % 2, t, 0:w]
                        ts = slice(t * P, (t + 1) * P)
                        mm(to, xh[:, k0 + k, ts], whi[:, s, k, 0:w], start=first, stop=False)
                        mm(to, xh[:, k0 + k, ts], wlo[:, s, k, 0:w], start=False, stop=False)
                        last = mm(to, xl[:, k0 + k, ts], whi[:, s, k, 0:w], start=False, stop=end)
                else:
                    for c in range(w // P):
                        to = acc[:, n % 2, c // 2, (c % 2) * T:(c % 2 + 1) * T]
                        cs = slice(c * P, (c + 1) * P)
                        mm(to, whi[:, s, k, cs], xh[:, k0 + k, :], start=first and c % 2 == 0, stop=False,
                           skip_group_check=True)
                        mm(to, whi[:, s, k, cs], xl[:, k0 + k, :], start=False, stop=False,
                           skip_group_check=True)
                        last = mm(to, wlo[:, s, k, cs], xh[:, k0 + k, :], start=False, stop=end,
                                  skip_group_check=True)
            last.then_inc(units_done, 1)

        def turn(stage, src, col0=0, bank=0):
            _, kk, _ = [s for s in TURNS if s[0] == stage][0]
            if TURN_AT[stage]:
                pe.wait_ge(turn_hi, TURN_AT[stage])
                pe.wait_ge(turn_lo, TURN_AT[stage])
            for b in range(kk // 2):
                for i in range(2):
                    for t in range(TT):
                        k = 2 * b + i
                        last = nc.tensor.transpose(M[bank + b][:, (i * TT + t) * P:(i * TT + t + 1) * P],
                                                   src[:, t, col0 + k * P:col0 + (k + 1) * P], ident)
                last.then_inc(turned, 1)

        def norm_turn(stage, count):
            pe.wait_ge(norm_act, count)
            pe.wait_ge(norm_dve, count)
            turn(stage, tok)

        def sb_scores(h):
            if h == 0:
                pe.wait_ge(read_dve, reads_before(G_AT["sbv1"], "dve"))
            if h >= 2:
                pe.wait_ge(sb_a, h - 1)
            c, o = h // 2, SB_D * (h % 2)
            z = M[h % 2]
            mm(z[:, 0:T], sbkT[o:o + SB_D, c, 0:P], sbqT[o:o + SB_D, c, :], start=True, stop=True)
            mm(z[:, T:T + P], sbkT[o:o + SB_D, c, P:T], sbqT[o:o + SB_D, c, P:T], start=False, stop=True,
               skip_group_check=True).then_inc(sb_z, 1)

        def sb_remain(h):
            pe.wait_ge(sb_tm, h + 1)
            z, w = M[h % 2], sbw[:, h % 2]
            mm(z[:, 0:T], negtri, w[:, 0:T], start=False, stop=True, skip_group_check=True)
            mm(z[:, T:T + P], negtri, w[:, T:T + P], start=False, stop=True, skip_group_check=True)
            mm(z[:, P:T], negones, w[:, T:T + P], start=False, stop=True,
               skip_group_check=True).then_inc(sb_r, 1)

        def sb_values(h):
            pe.wait_ge(sb_am, h + 1)
            if h < 2:
                pe.wait_ge(c_ready, 1)
                pe.wait_ge(floor_ready, 1)
                pe.wait_ge(if_ready, 1)
            else:
                pe.wait_ge(sb_y, h - 1)
            o, a = M[2 + h % 2], sba[:, h % 2]
            v = slice(h * SB_D, (h + 1) * SB_D)
            mm(o[:, 0:SB_D], a[:, 0:P], sbv[:, 0, v], start=True, stop=True)
            mm(o[:, SB_D:2 * SB_D], a[:, P:T], sbv[:, 0, v], start=True, stop=False)
            mm(o[:, SB_D:2 * SB_D], a[:, T:T + P], sbv[:, 1, v], start=False, stop=True).then_inc(sb_av, 1)

        def if_gates():
            pe.wait_ge(if_hi, 1)
            pe.wait_ge(if_lo, 1)
            for t in range(TT):
                to, ts = M[3][:, t * 8:(t + 1) * 8], slice(t * P, (t + 1) * P)
                for k in range(KD):
                    mm(to, xT_hi[:, k, ts], w_if_hi[:, k, :], start=k == 0, stop=False)
                    mm(to, xT_hi[:, k, ts], w_if_lo[:, k, :], start=False, stop=False)
                    last = mm(to, xT_lo[:, k, ts], w_if_hi[:, k, :], start=False, stop=k == KD - 1)
            last.then_inc(if_done, 1)

        def if_rows():
            pe.wait_ge(if_ready, 1)
            for i in range(2):
                for t in range(TT):
                    last = nc.tensor.transpose(M[2][0:ML_H, (i * TT + t) * P:(i * TT + t + 1) * P],
                                               if_tok[:, t, i * ML_H:(i + 1) * ML_H], ident)
            last.then_inc(rows_turned, 1)

        def if_cols():
            pe.wait_ge(scans_ready, 1)
            for i, row in enumerate((i_row, bm_row)):
                for t in range(TT):
                    at = (i * TT + t) * ML_H
                    last = nc.tensor.transpose(M[2][:, at:at + ML_H], row[:, t * P:(t + 1) * P],
                                               ident[0:ML_H, 0:ML_H])
            last.then_inc(cols_turned, 1)

        def ml_scores(h):
            s, b = M[2 * (h % 2)], M[2 * (h % 2) + 1]
            if h < 2:
                pe.wait_ge(sb_a, SB_H)
                pe.wait_ge(sb_y, SB_H)
                pe.wait_ge(read_dve, reads_before(G_AT["mlv1"], "dve"))
            else:
                pe.wait_ge(ml_y, h - 1)
            for i in range(2):
                c = 2 * h + i
                mm(s[:, 0:T], mlkT[:, c, 0:P], mlqT[:, c, :], start=i == 0, stop=i == 1, skip_group_check=True)
                mm(s[:, T:T + P], mlkT[:, c, P:T], mlqT[:, c, P:T], start=False, stop=i == 1,
                   skip_group_check=True)
            mm(b[:, 0:T], sel[:, h * P:(h + 1) * P], negm_row[:, :], start=True, stop=True).then_inc(ml_s, 1)

        def ml_values(h):
            pe.wait_ge(ml_p, h + 1)
            o, b, w = M[2 * (h % 2)], M[2 * (h % 2) + 1], sba[:, h % 2]
            v = slice(h * ML_D, (h + 1) * ML_D)
            ones = con[:, K_ONES:K_ONES + 1]
            mm(o[:, 0:ML_D], w[:, 0:P], mlv[:, 0, v], start=True, stop=True)
            mm(o[:, ML_D:], w[:, P:T], mlv[:, 0, v], start=True, stop=False)
            mm(o[:, ML_D:], w[:, T:T + P], mlv[:, 1, v], start=False, stop=True)
            mm(b[:, T:T + 1], w[:, 0:P], ones, start=True, stop=True)
            mm(b[:, T + 1:T + 2], w[:, P:T], ones, start=True, stop=False)
            mm(b[:, T + 1:T + 2], w[:, T:T + P], ones, start=False, stop=True).then_inc(ml_num, 1)

        def mb_scores(h):
            pe.wait_ge(read_dve, reads_before(G_AT[f"mqk{h // 4}"], "dve"))
            if h >= 2:
                pe.wait_ge(mb_max_ready, h - 1)
            half, c, o = h // 4, h % 4 // 2, MB_D * (h % 2)
            q, k = mbqk[o:o + MB_D, half, c, :], mbqk[o:o + MB_D, half, 2 + c, :]
            s = M[h % 2]
            mm(s[:, 0:P], q[:, 0:P], k[:, 0:P], start=True, stop=True)
            mm(s[:, P:3 * P], q[:, P:T], k, start=True, stop=True).then_inc(mb_s, 1)

        def mb_turn(h):
            pe.wait_ge(mb_e, h + 1)
            if h >= 1:
                pe.wait_ge(mb_p, h)
            for i in range(3):
                last = nc.tensor.transpose(M[2][:, i * P:(i + 1) * P], mbs[:, h % 3, i * P:(i + 1) * P],
                                           ident)
            last.then_inc(mb_pt, 1)

        def mb_values(h):
            pe.wait_ge(mb_p, h + 1)
            if h == 0:
                pe.wait_ge(read_dve, reads_before(G_AT["mv"], "dve"))
                pe.wait_ge(turn_hi, TURN_AT["gla"] + 1)
                pe.wait_ge(turn_lo, TURN_AT["gla"] + 1)
            else:
                pe.wait_ge(mb_y, h)
            o, p = M[3], mbp[:, h % 2]
            v = slice(h * MB_D, (h + 1) * MB_D)
            mm(o[:, 0:MB_D], p[:, 0:P], mbv[:, 0, v], start=True, stop=True)
            mm(o[:, MB_D:2 * MB_D], p[:, P:T], mbv[:, 0, v], start=True, stop=False)
            mm(o[:, MB_D:2 * MB_D], p[:, T:3 * P], mbv[:, 1, v], start=False, stop=True).then_inc(mb_av, 1)

        def gla_rank():
            pe.wait_ge(read_dve, reads_before(G_AT["gv"], "dve"))
            pe.wait_ge(turn_hi, TURN_AT["gla"])
            pe.wait_ge(turn_lo, TURN_AT["gla"])
            for t in range(TT):
                last = nc.tensor.transpose(M[0][0:GLA_RANK, t * P:(t + 1) * P], gv[:, t, GD:GD + GLA_RANK], ident)
            last.then_inc(glr_turned, 1)

        def gla_gate():
            pe.wait_ge(late_in, LATE)
            pe.wait_ge(glr_ready, 1)
            mm(M[1][:, 0:T], gw2[:, :], glrT[:, :], start=True, stop=True).then_inc(g_gate, 1)

        def gla_scores():
            pe.wait_ge(g_qk, 3)
            pe.wait_ge(l_sig, 1)
            for t in range(TT):
                ts = slice(t * P, (t + 1) * P)
                for h in range(GLA_H):
                    hs = slice(h * GLA_DK, (h + 1) * GLA_DK)
                    last = mm(M[h][:, ts], kd[hs, ts], qd[hs, ts], start=True, stop=True)
            last.then_inc(g_at, 1)

        def gla_keys():
            pe.wait_ge(g_atc, 1)
            for t in range(TT):
                last = nc.tensor.transpose(M[3][:, t * P:(t + 1) * P], kl[:, t * P:(t + 1) * P], ident)
            last.then_inc(kl_turned, 1)

        def gla_additions():
            pe.wait_ge(kl_ready, 1)
            for n in range(3):
                o, t = GLA_CHUNK * (n % 2), n // 2
                last = mm(M[n][:, 0:GD], kl_tok[o:o + GLA_CHUNK, t, :], gv[o:o + GLA_CHUNK, t, 0:GD],
                          start=True, stop=True)
            last.then_inc(g_kv, 1)

        def gla_values():
            pe.wait_ge(g_state, 1)
            pe.wait_ge(g_atm, 1)
            for t in range(TT):
                to = M[3][:, t * GD:(t + 1) * GD]
                for i in range(2):
                    n = 2 * t + i
                    o = GLA_CHUNK * i
                    mm(to[o:o + GLA_CHUNK, :], qd[:, n * GLA_CHUNK:(n + 1) * GLA_CHUNK], gstate[:, n, :],
                       start=True, stop=False, skip_group_check=True)
                for h in range(GLA_H):
                    hs = slice(h * GLA_DV, (h + 1) * GLA_DV)
                    last = mm(to[:, hs], gattn[:, h, t, :], gv[:, t, hs], start=False, stop=True,
                              skip_group_check=True)
            last.then_inc(g_o, 1)

        def lru_gates():
            pe.wait_ge(l_conv, 1)
            pe.wait_ge(g_cum, 1)
            for i in range(2):
                for c in range(LC):
                    for b in range(2):
                        bs = slice(64 * b, 64 * b + 64)
                        last = mm(M[2 * i + b][bs, c * T:(c + 1) * T], wab[bs, i, c, :], lw[bs, 0, c, :],
                                  start=True, stop=True)
            last.then_inc(l_gates, 1)

        pe.wait_ge(con_in, 16)
        pe.wait_ge(rows_in, 16 * len(VECS))
        nc.tensor.transpose(M[0][:, 0:V_ROWS], rows[0:V_ROWS, :], ident[0:V_ROWS, 0:V_ROWS]).then_inc(vecs_turned, 1)
        pe.wait_ge(small_in, 80)
        pe.wait_ge(pool_set, 1)
        mm(M[1][0:MB_H, :], rel33[:, :], hot[:, :], start=True, stop=True).then_inc(tab_done, 1)
        pe.wait_ge(vecs_ready, 1)
        pe.wait_ge(tab_ready, 1)
        norm_turn("x", 1)

        def moba_step(i):
            if 3 <= i < MB_H + 3:
                mb_values(i - 3)
            if 2 <= i < MB_H + 2:
                mb_turn(i - 2)
            if 0 <= i < MB_H:
                mb_scores(i)

        def between(u, k):
            if (u, k) == (B2 + 2, 2):
                gla_rank()
            if (u, k) == (B2 + 8, 2):
                gla_keys()
            if (u, k) in MB_AT:
                moba_step(MB_AT.index((u, k)))
            if (u, k) == MB_TURN0:
                pe.wait_ge(mb_y, 4)
                pe.wait_ge(mb_max_ready, 7)
                turn("moba0", tok, 2 * P, 0)
            if (u, k) == MB_TURN1:
                pe.wait_ge(mb_y, MB_H)
                turn("moba1", tok, 4 * P, 1)

        for u in range(NU):
            name = GROUPS[UNITS[u][0]][0]
            first_k = UNITS[u][1] == 0
            if name == "out0" and first_k:
                pe.wait_ge(read_dve, reads_before(G_AT["psc1"], "dve"))
                turn("merged", tok)
            if name == "up0" and first_k:
                norm_turn("h2", 2)
            if name == "gv" and first_k:
                norm_turn("h3", 3)
            if name == "gu0" and first_k:
                norm_turn("h4", 4)
            product(u, between)
            if u == U_IF:
                if_gates()
            if u == U_IF + 2:
                if_rows()
            if u == U_IF + 6:
                if_cols()
            i = u - SB0
            if 1 <= i <= SB_H:
                sb_remain(i - 1)
            if 0 <= i < SB_H:
                sb_scores(i)
            if 2 <= i < SB_H + 2:
                sb_values(i - 2)
            i = u - ML0
            if 0 <= i < ML_H:
                ml_scores(i)
            if 1 <= i <= ML_H:
                ml_values(i - 1)
            if u == TURN_SB:
                pe.wait_ge(sb_y, SB_H)
                pe.wait_ge(ml_y, ML_H)
                turn("ysb", tok)
            if u == TURN_ML:
                pe.wait_ge(yml_ready, 1)
                turn("yml", mlo)
            if u == B2 + 2:
                gla_gate()
            if u == B2 + 5:
                lru_gates()
            if u == B2 + 7:
                gla_scores()
            if u == B2 + 8:
                gla_additions()
            if u == B2 + 9:
                gla_values()
            if u == B2 + 11:
                pe.wait_ge(g_y, 1)
                turn("gla", tok, 0, 3)
            between(u, UNITS[u][2])

    @block.scalar
    def _(act):
        steps = [0]
        activate = nc.scalar.activation

        def link(ins):
            steps[0] += 1
            ins.then_inc(act_step, 1)
            act.wait_ge(act_step, steps[0])

        def split(u):
            if u >= NU:
                return
            n, k, m = UNITS[u]
            w = width(n)
            act.wait_ge(landed[u % LANDS], land_count(u))
            if u >= PARTS:
                act.wait_ge(units_done, u - PARTS + 1)
            activate(whi[:, u % PARTS, 0:m, 0:w], land[:, u % LANDS, 0:m, 0:w], ACT.Copy).then_inc(hi_ready, 1)

        def square(j, src):
            activate(tok[:, 0, :], src[:, 0, :], ACT.Square, accum_out=squares[:, j, 0:1]).then_inc(sq_act, 1)

        def scale(j, src, count):
            act.wait_ge(rstd_ready, j + 1)
            activate(tok[:, 0, :], src[:, 0, :], ACT.Copy, scale=rstd[:, j, 0:1]).then_inc(norm_act, 1)

        def turn_split(stage, hi, k_to=0, bank=0):
            _, kk, gain = [s for s in TURNS if s[0] == stage][0]
            for b in range(kk // 2):
                act.wait_ge(turned, TURN_AT[stage] + b + 1)
                if gain is None:
                    last = activate(hi[:, k_to + 2 * b:k_to + 2 * b + 2, :],
                                    M[bank + b][:, :].rearrange("p (k t) -> p k t", k=2), ACT.Copy)
                else:
                    for i in range(2):
                        g = V_AT[gain] + 2 * b + i
                        last = activate(hi[:, k_to + 2 * b + i, :], M[bank + b][:, i * T:(i + 1) * T], ACT.Copy,
                                        scale=vecs[:, g:g + 1])
                last.then_inc(turn_hi, 1)

        def product_done(name):
            act.wait_ge(units_done, LAST_U[name] + 1)

        def sb_logs(h):
            act.wait_ge(sb_z, h + 1)
            w = sbw[:, h % 2]
            if h >= 2:
                act.wait_ge(sb_r, h - 1)
            link(activate(w, M[h % 2][:, 0:3 * P], ACT.Abs))
            link(activate(w, w, ACT.Exp, scale=-1.0))
            activate(w, w, ACT.Ln, bias=1.0).then_inc(sb_log, 1)

        def sb_weights(h):
            act.wait_ge(sb_r, h + 1)
            if h >= 2:
                act.wait_ge(sb_av, h - 1)
            activate(sba[:, h % 2], M[h % 2][:, 0:3 * P], ACT.Exp).then_inc(sb_a, 1)

        def ml_weights(h):
            act.wait_ge(ml_s, h + 1)
            act.wait_ge(c_ready, 1)
            b, w = M[2 * (h % 2) + 1], sba[:, h % 2]
            activate(w[:, 0:T], b[:, 0:T], ACT.Exp, bias=c_col[:, 0, h:h + 1])
            activate(w[:, T:3 * P], b[:, P:T], ACT.Exp, bias=c_col[:, 1, h:h + 1]).then_inc(ml_w, 1)

        def ml_squares(h):
            act.wait_ge(ml_y, h + 1)
            for t in range(TT):
                last = activate(sbw[:, t, 0:T], mlo[:, t, h * ML_D:(h + 1) * ML_D], ACT.Square,
                                accum_out=ml_sq[:, t, h:h + 1])
            last.then_inc(ml_ss, 1)
            act.wait_ge(ml_ss, h + 1)

        def mb_exps(h):
            act.wait_ge(mb_max_ready, h + 1)
            s = mbs[:, h % 3]
            activate(s[:, 0:P], s[:, 0:P], ACT.Exp, bias=mb_max[:, h, 0:1], accum_out=mb_sum[:, h, 0:1])
            activate(s[:, P:3 * P], s[:, P:3 * P], ACT.Exp, bias=mb_max[:, h, 1:2],
                     accum_out=mb_sum[:, h, 1:2]).then_inc(mb_e, 1)

        def mb_weights(h):
            act.wait_ge(mb_pt, h + 1)
            if h >= 2:
                act.wait_ge(mb_av, h - 1)
            activate(mbp[:, h % 2], M[2][:, 0:3 * P], ACT.Copy).then_inc(mb_p, 1)

        def gla_logs():
            b = vecs[:, V_AT["gla_gate_b_2"]:V_AT["gla_gate_b_2"] + 1]
            act.wait_ge(g_gate, 1)
            link(activate(gla[:, 0], M[1][:, 0:T], ACT.Abs, bias=b))
            link(activate(gla[:, 0], gla[:, 0], ACT.Exp, scale=-1.0))
            activate(gla[:, 0], gla[:, 0], ACT.Ln, bias=1.0).then_inc(g_ln, 1)

        def gla_exps():
            act.wait_ge(g_cum, 1)
            activate(gla[:, 3], gla[:, 1], ACT.Exp).then_inc(g_exp, 1)
            activate(gla[:, 4], gla[:, 1], ACT.Exp, scale=-1.0).then_inc(g_exp, 1)
            activate(gla[:, 5], gla[:, 2], ACT.Exp).then_inc(g_exp, 1)
            last = gla[:, 1].rearrange("p (n c) -> p n c", c=GLA_CHUNK)[:, :, GLA_CHUNK - 1]
            activate(gdec[:, :], last, ACT.Exp).then_inc(g_exp, 1)

        def gla_copies():
            act.wait_ge(g_at, 1)
            for h in range(GLA_H):
                last = activate(gattn[:, h].rearrange("p t c -> p (t c)"), M[h][:, 0:T], ACT.Copy)
            last.then_inc(g_atc, 1)

        def gla_squares():
            act.wait_ge(g_o, 1)
            activate(gsq.rearrange("p a b -> p (a b)"), M[3][:, :], ACT.Square).then_inc(g_osq, 1)

        def lru_log():
            lam = vecs[:, V_AT["lru_lambda_2"]:V_AT["lru_lambda_2"] + LC]
            link(activate(lamb[:, 0], lam, ACT.Abs))
            activate(lamb[:, 1], lamb[:, 0], ACT.Exp, scale=-1.0).then_inc(l_lam, 1)

        def lru_sigmoids():
            act.wait_ge(l_gates, 1)
            for i, (at, name) in enumerate(((1, "lru_ba_2"), (2, "lru_bx_2"))):
                for c in range(LC):
                    for b in range(2):
                        bs = slice(64 * b, 64 * b + 64)
                        last = activate(lw[bs, at, c, :], M[2 * i + b][bs, c * T:(c + 1) * T], ACT.Sigmoid,
                                        bias=vecs[bs, V_AT[name] + c:V_AT[name] + c + 1])
            last.then_inc(l_sig, 1)
            act.wait_ge(l_gin, 1)
            activate(lw[:, 8], lw[:, 6], ACT.Sigmoid, scale=GELU_C).then_inc(l_gel, 1)

        def lru_decays():
            act.wait_ge(l_spn, 1)
            act.wait_ge(l_sig, 1)
            for c in range(LC):
                activate(lw[:, 3, c, :], lw[:, 1, c, :], ACT.Exp, scale=lamb[:, 6, c:c + 1])
            for c in range(LC):
                last = activate(lw[:, 4, c, :], lw[:, 1, c, :], ACT.Tanh, scale=lamb[:, 7, c:c + 1])
            last.then_inc(l_exp, 1)

        def lru_root():
            act.wait_ge(l_m2, 1)
            activate(lw[:, 4], lw[:, 6], ACT.Sqrt).then_inc(l_mult, 1)

        def lru_result():
            act.wait_ge(l_y, 1)
            activate(y2T_hi[:, 0:LC, :], lw[:, 7], ACT.Copy).then_inc(l_hi, 1)

        def moba_steps(of):
            for at in of:
                if at in MB_AT:
                    i = MB_AT.index(at)
                    if 2 <= i < MB_H + 2:
                        mb_weights(i - 2)
                    if 0 <= i < MB_H:
                        mb_exps(i)

        act.wait_ge(x_in, 32)
        square(0, x_tok)
        act.wait_ge(small_in, 80)
        activate(w_if_hi[:], w_if[:], ACT.Copy).then_inc(if_hi, 1)
        scale(0, x_tok, 1)
        act.wait_ge(tab_done, 1)
        activate(tab[:, :], M[1][0:MB_H, :], ACT.Copy).then_inc(tab_ready, 1)
        split(0)
        act.wait_ge(vecs_ready, 1)
        turn_split("x", xT_hi)
        split(1)

        for u in range(NU):
            n = UNITS[u][0]
            name = GROUPS[n][0]
            ends = u == LAST_U[name]
            if u == B2 + 12:
                turn_split("gla", y2T_hi, LC, 3)
            moba_steps([(u - 1, UNITS[u - 1][2])])
            if u == MB_TURN1[0] + 1:
                turn_split("moba1", y2T_hi, LC + 4, 1)
            split(u + 2)
            if u == U_IF + 2:
                act.wait_ge(rows_ready, 1)
                link(activate(e_row[:, :], f_row[:, :], ACT.Abs))
                link(activate(e_row[:, :], e_row[:, :], ACT.Exp, scale=-1.0))
                activate(e_row[:, :], e_row[:, :], ACT.Ln, bias=1.0).then_inc(e_ready, 1)
            if u == U_IF + 6:
                act.wait_ge(cols_turned, 1)
                act.wait_ge(c_ready, 1)
                activate(floor_col[:].rearrange("p t h -> p (t h)"), M[2][:, TT * ML_H:2 * TT * ML_H], ACT.Exp,
                         scale=-1.0).then_inc(floor_ready, 1)
            i = u - SB0
            if 1 <= i <= SB_H:
                sb_weights(i - 1)
            if 0 <= i < SB_H:
                sb_logs(i)
            i = u - ML0
            if 0 <= i < ML_H:
                ml_weights(i)
            if 2 <= i < ML_H + 2:
                ml_squares(i - 2)
            if ends and name[:3] == "mlo":
                j = int(name[3])
                product_done(name)
                activate(mlo[:, :, j * NG:(j + 1) * NG], acc[:, n % 2], ACT.Exp, scale=-1.0).then_inc(read_act, 1)
            if ends and name[:3] in ("gsb", "gml", "gsc"):
                product_done(name)
                if name != "gsb0":
                    act.wait_ge(read_dve, reads_before(n - 1, "dve"))
                activate(gate[:], acc[:, n % 2], ACT.Sigmoid).then_inc(read_act, 1)
            if u == TURN_SB:
                turn_split("ysb", ysbT_hi)
            if u == TURN_ML:
                turn_split("yml", ymlT_hi)
            if ends and name[:3] == "scb":
                j = int(name[3])
                act.wait_ge(read_dve, reads_before(n, "dve"))
                activate(yscT_hi[:, 4 * j:4 * j + 4, :], conv[:], ACT.Copy).then_inc(ysc_hi, 1)
            if ends and name == "psc1":
                turn_split("merged", xT_hi)
            if ends and name == "out1":
                act.wait_ge(read_dve, reads_before(n, "dve"))
                square(1, x_tok)
                scale(1, x_tok, 2)
                turn_split("h2", xT_hi)
            if ends and name[:2] == "up":
                j = int(name[2:])
                product_done(name)
                activate(relu[:, j % 2, :], acc[:, n % 2].rearrange("p a b -> p (a b)"),
                         ACT.Relu).then_inc(relu_ready, 1)
                act.wait_ge(relu_ready, j + 1)
                activate(aT_hi[:, 4 * j:4 * j + 4, :].rearrange("p a b -> p (a b)"), relu[:, j % 2, :],
                         ACT.Square).then_inc(a_hi, 1)
            if ends and name == "down1":
                act.wait_ge(read_dve, reads_before(n, "dve"))
                square(2, x_tok)
                act.wait_ge(x_done, 1)
                square(3, x_tok)
                scale(3, x_tok, 3)
                turn_split("h3", xT_hi)
            if u == B2 + 1:
                lru_log()
            if u == B2 + 3:
                gla_logs()
                gla_exps()
            if u == B2 + 6:
                lru_sigmoids()
            if u == B2 + 7:
                lru_decays()
            if u == B2 + 8:
                gla_copies()
                act.wait_ge(read_dve, reads_before(G_AT["gout"], "dve"))
                activate(gsig[:], gout[:], ACT.Sigmoid).then_inc(g_sig, 1)
            if u == B2 + 9:
                lru_root()
            if u == B2 + 10:
                gla_squares()
            if u == B2 + 12:
                lru_result()
            moba_steps([(u, k) for k in range(1, UNITS[u][2])])
            if u == MB_TURN0[0]:
                turn_split("moba0", y2T_hi, LC + 2, 0)
            if ends and name == "mix1":
                act.wait_ge(read_dve, reads_before(n, "dve"))
                square(4, mixed)
                act.wait_ge(x_done, 2)
                square(5, x_tok)
                scale(5, x_tok, 4)
                turn_split("h4", xT_hi)
            if ends and name[:2] == "gu":
                j = int(name[2:])
                product_done(name)
                activate(sig2[:, j % 2, :], acc[:, n % 2, 0, :], ACT.Sigmoid).then_inc(sig2_ready, 1)
                act.wait_ge(read_dve, reads_before(n, "dve"))
                activate(a2T_hi[:, 2 * j:2 * j + 2, :].rearrange("p a b -> p (a b)"), act2[:, j % 2, :],
                         ACT.Copy).then_inc(act2_hi, 1)
            if ends and name == "dn1":
                act.wait_ge(read_dve, reads_before(n, "dve"))
                square(6, mixed)

    @block.vector
    def _(dve):
        v = nc.vector
        steps = [0]

        def link(ins):
            steps[0] += 1
            ins.then_inc(dve_step, 1)
            dve.wait_ge(dve_step, steps[0])

        def split(u):
            if u >= NU:
                return
            n, k, m = UNITS[u]
            w = width(n)
            dve.wait_ge(hi_ready, u + 1)
            dve.wait_ge(landed[u % LANDS], land_count(u))
            v.tensor_tensor(wlo[:, u % PARTS, 0:m, 0:w], land[:, u % LANDS, 0:m, 0:w],
                            whi[:, u % PARTS, 0:m, 0:w].bitcast(F32), ALU.subtract).then_inc(lo_ready, 1)

        def square(j, src):
            v.tensor_tensor_reduce(tok[:, 1, :], src[:, 1, :], src[:, 1, :], 1.0, 0.0, ALU.mult, ALU.add,
                                   squares[:, j, 1:2]).then_inc(sq_dve, 1)

        def scale(j, src):
            dve.wait_ge(rstd_ready, j + 1)
            v.tensor_scalar(tok[:, 1, :], src[:, 1, :], rstd[:, j, 1:2], None, ALU.mult).then_inc(norm_dve, 1)

        def turn_split(stage, hi, lo, k_to=0, bank=0):
            _, kk, gain = [s for s in TURNS if s[0] == stage][0]
            for b in range(kk // 2):
                dve.wait_ge(turn_hi, TURN_AT[stage] + b + 1)
                ks = slice(k_to + 2 * b, k_to + 2 * b + 2)
                if gain is None:
                    last = v.tensor_tensor(lo[:, ks, :], M[bank + b][:, :].rearrange("p (k t) -> p k t", k=2),
                                           hi[:, ks, :].bitcast(F32), ALU.subtract)
                else:
                    for i in range(2):
                        g, k = V_AT[gain] + 2 * b + i, k_to + 2 * b + i
                        last = v.scalar_tensor_tensor(out=lo[:, k, :], in0=M[bank + b][:, i * T:(i + 1) * T],
                                                      scalar=vecs[:, g:g + 1], in1=hi[:, k, :].bitcast(F32),
                                                      op0=ALU.mult, op1=ALU.subtract)
                last.then_inc(turn_lo, 1)

        def product_done(name):
            dve.wait_ge(units_done, LAST_U[name] + 1)

        def sb_softplus(h):
            dve.wait_ge(sb_log, h + 1)
            w = sbw[:, h % 2]
            v.scalar_tensor_tensor(out=w, in0=M[h % 2][:, 0:3 * P], scalar=0.0, in1=w, op0=ALU.max,
                                   op1=ALU.add).then_inc(sb_t, 1)

        def sb_result(h):
            dve.wait_ge(sb_av, h + 1)
            v.tensor_copy(tok[:, :, h * SB_D:(h + 1) * SB_D],
                          M[2 + h % 2][:, 0:2 * SB_D].rearrange("p (t d) -> p t d", t=TT)).then_inc(sb_y, 1)

        def ml_products(h):
            dve.wait_ge(ml_wm, h + 1)
            w = sba[:, h % 2]
            v.tensor_tensor(w, M[2 * (h % 2)][:, 0:3 * P], w, ALU.mult).then_inc(ml_p, 1)

        def ml_result(h):
            dve.wait_ge(ml_num, h + 1)
            if h == 0:
                dve.wait_ge(floor_ready, 1)
            o, b = M[2 * (h % 2)], M[2 * (h % 2) + 1]
            link(v.tensor_copy(ml_den[:, 0], b[:, T:T + TT]))
            link(v.scalar_tensor_tensor(out=ml_den[:, 1], in0=ml_den[:, 0], scalar=-1.0, in1=ml_den[:, 0],
                                        op0=ALU.mult, op1=ALU.max))
            link(v.tensor_tensor(ml_den[:, 2], ml_den[:, 1], floor_col[:, :, h], ALU.max))
            link(v.reciprocal(ml_den[:, 3], ml_den[:, 2]))
            for t in range(TT):
                y = mlo[:, t, h * ML_D:(h + 1) * ML_D]
                last = v.scalar_tensor_tensor(out=y, in0=o[:, t * ML_D:(t + 1) * ML_D],
                                              scalar=ml_den[:, 3, t:t + 1], in1=y, op0=ALU.mult, op1=ALU.mult)
            last.then_inc(ml_y, 1)

        def conv_taps(j):
            for tap in reversed(range(CONV_K)):
                for i in range(4):
                    k = 4 * j + i
                    w = vecs[:, V_AT["conv_w"] + tap * KD + k:V_AT["conv_w"] + tap * KD + k + 1]
                    z = zT[:, k, tap:tap + T]
                    if tap == CONV_K - 1:
                        last = v.tensor_scalar(conv[:, i, :], z, w, None, ALU.mult)
                    else:
                        last = v.scalar_tensor_tensor(out=conv[:, i, :], in0=z, scalar=w, in1=conv[:, i, :],
                                                      op0=ALU.mult, op1=ALU.add)
                link(last)

        def mb_logits(h):
            dve.wait_ge(mb_s, h + 1)
            if h == 0:
                dve.wait_ge(bias_in, 32)
            if h >= 3:
                dve.wait_ge(mb_pt, h - 2)
            s = mbs[:, h % 3]
            link(v.tensor_tensor(s, M[h % 2][:, 0:3 * P], bias[:, h, :], ALU.add))
            v.tensor_reduce(mb_max[:, h, 0:1], s[:, 0:P], AX.X, ALU.max)
            link(v.tensor_reduce(mb_max[:, h, 1:2], s[:, P:3 * P], AX.X, ALU.max))
            v.tensor_scalar(mb_max[:, h, :], mb_max[:, h, :], -1.0, None, ALU.mult).then_inc(mb_max_ready, 1)

        def mb_result(h):
            dve.wait_ge(mb_av, h + 1)
            link(v.reciprocal(mb_inv[:, h, :], mb_sum[:, h, :]))
            for t in range(TT):
                last = v.tensor_scalar(tok[:, t, 2 * P + h * MB_D:2 * P + (h + 1) * MB_D],
                                       M[3][:, t * MB_D:(t + 1) * MB_D], mb_inv[:, h, t:t + 1], None, ALU.mult)
            last.then_inc(mb_y, 1)

        def gla_rank():
            dve.wait_ge(glr_turned, 1)
            v.tensor_copy(glrT[:, :], M[0][0:GLA_RANK, 0:T]).then_inc(glr_ready, 1)

        def gla_cumulative():
            b = vecs[:, V_AT["gla_gate_b_2"]:V_AT["gla_gate_b_2"] + 1]
            dve.wait_ge(g_ln, 1)
            link(v.tensor_scalar(gla[:, 1], M[1][:, 0:T], b, 0.0, ALU.add, ALU.min))
            link(v.tensor_tensor(gla[:, 1], gla[:, 1], gla[:, 0], ALU.subtract))
            link(v.tensor_scalar(gla[:, 2], gla[:, 1], 1.0 / GLA_TAU, None, ALU.mult))
            dve.wait_ge(g_sets, 1)
            link(v.tensor_tensor_scan(gla[:, 1], gnew, gla[:, 2], 0.0, ALU.mult, ALU.add))
            cum = gla[:, 1].rearrange("p (n c) -> p n c", c=GLA_CHUNK)
            last = cum[:, :, GLA_CHUNK - 1:GLA_CHUNK].to_broadcast([P, T // GLA_CHUNK, GLA_CHUNK])
            v.tensor_tensor(gla[:, 2].rearrange("p (n c) -> p n c", c=GLA_CHUNK), last, cum,
                            ALU.subtract).then_inc(g_cum, 1)

        def gla_scaled():
            dve.wait_ge(g_exp, 4)
            dve.wait_ge(read_dve, reads_before(G_AT["gqk"], "dve"))
            v.scalar_tensor_tensor(out=qd, in0=gqk[:, 0, :], scalar=float(GLA_DK) ** -0.5, in1=gla[:, 3],
                                   op0=ALU.mult, op1=ALU.mult).then_inc(g_qk, 1)
            v.tensor_tensor(kd, gqk[:, 1, :], gla[:, 4], ALU.mult).then_inc(g_qk, 1)
            v.tensor_tensor(kl, gqk[:, 1, :], gla[:, 5], ALU.mult).then_inc(g_qk, 1)

        def gla_keys():
            dve.wait_ge(kl_turned, 1)
            v.tensor_copy(kl_tok[:].rearrange("p t c -> p (t c)"), M[3][:, 0:T]).then_inc(kl_ready, 1)

        def gla_states():
            dve.wait_ge(g_kv, 1)
            for n in range(3):
                for h in range(GLA_H):
                    ps = slice(h * GLA_DK, (h + 1) * GLA_DK)
                    vs = slice(h * GLA_DV, (h + 1) * GLA_DV)
                    last = v.scalar_tensor_tensor(out=gstate[ps, n + 1, vs], in0=gstate[ps, n, vs],
                                                  scalar=gdec[ps, n:n + 1], in1=M[n][ps, vs], op0=ALU.mult,
                                                  op1=ALU.add)
                if n < 2:
                    link(last)
                else:
                    last.then_inc(g_state, 1)

        def gla_result():
            dve.wait_ge(g_sig, 1)
            link(v.tensor_tensor(gsig[:], gsig[:], gout[:], ALU.mult))
            dve.wait_ge(g_osq, 1)
            v.tensor_reduce(gss[:, 0, :], gsq, AX.X, ALU.add).then_inc(g_oss, 1)
            dve.wait_ge(g_rs, 1)
            link(v.tensor_tensor(gsq, M[3][:, :].rearrange("p (a b) -> p a b", b=GLA_DV),
                                 gss[:, 2, :].unsqueeze(2).to_broadcast([P, TT * GLA_H, GLA_DV]), ALU.mult))
            v.tensor_tensor(tok[:, :, 0:GD], gsq.rearrange("p (t h) b -> p t (h b)", t=TT), gsig[:],
                            ALU.mult).then_inc(g_y, 1)

        def lru_decay():
            dve.wait_ge(l_lam, 1)
            e, w, w2, s = lamb[:, 1], lamb[:, 2], lamb[:, 3], lamb[:, 4]
            link(v.tensor_scalar(w, e, 2.0, None, ALU.add))
            link(v.reciprocal(w2, w))
            link(v.tensor_tensor(w, e, w2, ALU.mult))
            link(v.tensor_tensor(w2, w, w, ALU.mult))
            link(v.tensor_scalar(s, w2, 1.0 / 17, 1.0 / 15, ALU.mult, ALU.add))
            for odd in (13, 11, 9, 7, 5, 3, 1):
                link(v.tensor_tensor(s, s, w2, ALU.mult))
                link(v.tensor_scalar(s, s, 1.0 / odd, None, ALU.add))
            link(v.tensor_tensor(s, s, w, ALU.mult))
            lam = vecs[:, V_AT["lru_lambda_2"]:V_AT["lru_lambda_2"] + LC]
            link(v.tensor_scalar(lamb[:, 5], lam, -1.0, 0.0, ALU.mult, ALU.max))
            link(v.scalar_tensor_tensor(out=s, in0=s, scalar=2.0, in1=lamb[:, 5], op0=ALU.mult, op1=ALU.add))
            v.tensor_scalar(lamb[:, 6], s, -LRU_C, None, ALU.mult)
            v.tensor_scalar(lamb[:, 7], s, LRU_C, None, ALU.mult).then_inc(l_spn, 1)

        def lru_conv():
            dve.wait_ge(g_sets, 1)
            dve.wait_ge(read_dve, reads_before(G_AT["lru"], "dve"))
            for tap in reversed(range(LRU_TAPS)):
                for c in range(LC):
                    r = V_AT["lru_conv_w_2"] + tap * LC + c
                    w, x = vecs[:, r:r + 1], lruT[:, c, tap:tap + T]
                    if tap == LRU_TAPS - 1:
                        last = v.tensor_scalar(lw[:, 0, c, :], x, w, None, ALU.mult)
                    else:
                        last = v.scalar_tensor_tensor(out=lw[:, 0, c, :], in0=x, scalar=w, in1=lw[:, 0, c, :],
                                                      op0=ALU.mult, op1=ALU.add)
                link(last)
            for c in range(LC):
                r = V_AT["lru_conv_b_2"] + c
                last = v.tensor_scalar(lw[:, 0, c, :], lw[:, 0, c, :], vecs[:, r:r + 1], None, ALU.add)
            last.then_inc(l_conv, 1)
            g = lruT[:, LC:2 * LC, LRU_TAPS - 1:]
            link(v.tensor_tensor(lw[:, 6], g, g, ALU.mult))
            link(v.tensor_scalar(lw[:, 6], lw[:, 6], 0.044715, 1.0, ALU.mult, ALU.add))
            v.tensor_tensor(lw[:, 6], lw[:, 6], g, ALU.mult).then_inc(l_gin, 1)

        def lru_scan():
            dve.wait_ge(l_exp, 1)
            p, q, m2 = lw[:, 4], lw[:, 5], lw[:, 6]
            link(v.tensor_scalar(q, p, 1.0, None, ALU.add))
            link(v.reciprocal(q, q))
            link(v.scalar_tensor_tensor(out=m2, in0=p, scalar=2.0, in1=q, op0=ALU.mult, op1=ALU.mult))
            v.tensor_scalar(m2, m2, ROOT_FLOOR, None, ALU.max).then_inc(l_m2, 1)

        def lru_result():
            link(v.tensor_tensor(lw[:, 7], lw[:, 2], lw[:, 0], ALU.mult))
            link(v.tensor_tensor(lw[:, 8], lw[:, 8], lruT[:, LC:2 * LC, LRU_TAPS - 1:], ALU.mult))
            dve.wait_ge(l_mult, 1)
            link(v.memset(lw[:, 4, :, 0:1], 1.0))
            link(v.tensor_tensor(lw[:, 5], lw[:, 7], lw[:, 4], ALU.mult))
            for c in range(LC):
                last = v.tensor_tensor_scan(lw[:, 6, c, :], lw[:, 3, c, :], lw[:, 5, c, :], 0.0, ALU.mult, ALU.add)
            link(last)
            v.tensor_tensor(lw[:, 7], lw[:, 6], lw[:, 8], ALU.mult).then_inc(l_y, 1)

        def lru_rest():
            dve.wait_ge(l_hi, 1)
            v.tensor_tensor(y2T_lo[:, 0:LC, :], lw[:, 7], y2T_hi[:, 0:LC, :].bitcast(F32),
                            ALU.subtract).then_inc(l_lo, 1)

        def moba_steps(of):
            for at in of:
                if at in MB_AT:
                    i = MB_AT.index(at)
                    if 3 <= i < MB_H + 3:
                        mb_result(i - 3)
                    if 0 <= i < MB_H:
                        mb_logits(i)

        def residual(j, gain, done):
            dve.wait_ge(rstd_ready, j + 1)
            for t in range(TT):
                link(v.scalar_tensor_tensor(out=mixed[:, t, :], in0=mixed[:, t, :], scalar=rstd[:, j, t:t + 1],
                                            in1=gain[:, :], op0=ALU.mult, op1=ALU.mult))
                last = v.tensor_tensor(x_tok[:, t, :], x_tok[:, t, :], mixed[:, t, :], ALU.add)
                if done > 1 or t == TT - 1:
                    last.then_inc(x_done, 1)

        dve.wait_ge(x_in, 32)
        square(0, x_tok)
        link(v.memset(one_row[:, :], 1.0))
        dve.wait_ge(vecs_turned, 1)
        v.tensor_copy(vecs[:, :], M[0][:, 0:V_ROWS]).then_inc(vecs_ready, 1)
        scale(0, x_tok)
        dve.wait_ge(if_hi, 1)
        v.tensor_tensor(w_if_lo[:], w_if[:], w_if_hi[:].bitcast(F32), ALU.subtract).then_inc(if_lo, 1)
        split(0)
        dve.wait_ge(vecs_ready, 1)
        turn_split("x", xT_hi, xT_lo)
        split(1)

        for u in range(NU):
            n = UNITS[u][0]
            name = GROUPS[n][0]
            ends = u == LAST_U[name]
            flat = acc[:, n % 2].rearrange("p a b -> p (a b)")
            if u == B2 + 12:
                turn_split("gla", y2T_hi, y2T_lo, LC, 3)
            moba_steps([(u - 1, UNITS[u - 1][2])])
            if u == MB_TURN1[0] + 1:
                turn_split("moba1", y2T_hi, y2T_lo, LC + 4, 1)
            split(u + 2)
            if u == U_IF:
                dve.wait_ge(if_done, 1)
                v.tensor_tensor(if_tok[:], M[3][:, 0:TT * 2 * ML_H].rearrange("p (t c) -> p t c", t=TT),
                                b_if[:].unsqueeze(1).to_broadcast([P, TT, 2 * ML_H]), ALU.add).then_inc(if_ready, 1)
            if u == U_IF + 2:
                dve.wait_ge(rows_turned, 1)
                link(v.tensor_copy(i_row[:, :], M[2][0:ML_H, 0:T]))
                v.tensor_copy(f_row[:, :], M[2][0:ML_H, T:2 * T]).then_inc(rows_ready, 1)
            if u == U_IF + 4:
                dve.wait_ge(e_ready, 1)
                link(v.scalar_tensor_tensor(out=f_row[:, :], in0=f_row[:, :], scalar=0.0, in1=e_row[:, :],
                                            op0=ALU.min, op1=ALU.subtract))
                link(v.tensor_tensor_scan(bm_row[:, :], one_row[:, :], f_row[:, :], 0.0, ALU.mult, ALU.add))
                link(v.tensor_tensor(i_row[:, :], i_row[:, :], bm_row[:, :], ALU.subtract))
                link(v.tensor_tensor_scan(negm_row[:, :], i_row[:, :], i_row[:, :], 0.0, ALU.max, ALU.max))
                link(v.tensor_tensor(bm_row[:, :], bm_row[:, :], negm_row[:, :], ALU.add))
                v.tensor_scalar(negm_row[:, :], negm_row[:, :], -1.0, None, ALU.mult).then_inc(scans_ready, 1)
            if u == U_IF + 6:
                dve.wait_ge(cols_turned, 1)
                v.tensor_copy(c_col[:].rearrange("p t h -> p (t h)"), M[2][:, 0:TT * ML_H]).then_inc(c_ready, 1)
            i = u - SB0
            if 0 <= i < SB_H:
                sb_softplus(i)
            if 2 <= i < SB_H + 2:
                sb_result(i - 2)
            i = u - ML0
            if 0 <= i < ML_H:
                ml_products(i)
            if 1 <= i <= ML_H:
                ml_result(i - 1)
            if ends and name[:3] in ("sbq", "sbk", "mlq", "mlk"):
                j = int(name[3])
                to = {"sbq": sbqT, "sbk": sbkT, "mlq": mlqT, "mlk": mlkT}[name[:3]]
                by = {"sbq": SB_D ** -0.5, "mlk": ML_D ** -0.5}.get(name[:3], 1.0)
                product_done(name)
                v.tensor_scalar(to[:, 4 * j:4 * j + 4, :].rearrange("p a b -> p (a b)"), flat, by, None,
                                ALU.mult).then_inc(read_dve, 1)
            if ends and name[:3] in ("sbv", "mlv"):
                j = int(name[3])
                product_done(name)
                v.tensor_copy((sbv if name[0] == "s" else mlv)[:, :, j * NG:(j + 1) * NG],
                              acc[:, n % 2]).then_inc(read_dve, 1)
            if ends and name[:3] == "mlo":
                j = int(name[3])
                dve.wait_ge(read_act, reads_before(n, "act"))
                s = mlo[:, :, j * NG:(j + 1) * NG]
                link(v.tensor_scalar(s, s, 1.0, None, ALU.add))
                link(v.reciprocal(s, s))
            if ends and name[:3] == "scc":
                j = int(name[3])
                product_done(name)
                v.tensor_copy(cT[:, 4 * j:4 * j + 4, :].rearrange("p a b -> p (a b)"), flat).then_inc(read_dve, 1)
            if ends and name[:3] == "scu":
                j = int(name[3])
                product_done(name)
                if j == 0:
                    link(v.memset(zT[:, :, 0:CONV_K - 1], 0.0))
                v.tensor_tensor(zT[:, 4 * j:4 * j + 4, CONV_K - 1:], flat.rearrange("p (a b) -> p a b", b=T),
                                cT[:, 4 * j:4 * j + 4, :], ALU.mult).then_inc(read_dve, 1)
                dve.wait_ge(read_dve, reads_before(n, "dve"))
                if j == 0:
                    conv_taps(0)
            if ends and name[:3] == "scb":
                j = int(name[3])
                product_done(name)
                v.tensor_tensor(conv[:].rearrange("p a b -> p (a b)"), flat,
                                conv[:].rearrange("p a b -> p (a b)"), ALU.mult).then_inc(read_dve, 1)
                dve.wait_ge(read_dve, reads_before(n, "dve"))
                dve.wait_ge(ysc_hi, j + 1)
                v.tensor_tensor(yscT_lo[:, 4 * j:4 * j + 4, :], conv[:], yscT_hi[:, 4 * j:4 * j + 4, :].bitcast(F32),
                                ALU.subtract).then_inc(ysc_lo, 1)
                if j == 0:
                    dve.wait_ge(ysc_lo, 1)
                    conv_taps(1)
            if u == TURN_SB:
                turn_split("ysb", ysbT_hi, ysbT_lo)
                dve.wait_ge(ml_rs, 1)
                y = mlo[:].rearrange("p t (h d) -> p (t h) d", d=ML_D)
                v.tensor_tensor(y, y, ml_rstd[:].rearrange("p t h -> p (t h)").unsqueeze(2).to_broadcast(
                    [P, TT * ML_H, ML_D]), ALU.mult).then_inc(yml_ready, 1)
            if u == TURN_ML:
                turn_split("yml", ymlT_hi, ymlT_lo)
            if ends and name[:3] in ("psb", "pml", "psc"):
                j = int(name[3])
                product_done(name)
                dve.wait_ge(read_act, reads_before(n - 1, "act"))
                m = tok[:, :, j * NG:(j + 1) * NG]
                if name[:3] == "psb":
                    v.tensor_tensor(m, acc[:, n % 2], gate[:], ALU.mult).then_inc(read_dve, 1)
                else:
                    link(v.tensor_tensor(gated[:], acc[:, n % 2], gate[:], ALU.mult))
                    v.tensor_tensor(m, m, gated[:], ALU.add).then_inc(read_dve, 1)
            if ends and name == "psc1":
                turn_split("merged", xT_hi, xT_lo)
            if ends and name[:3] == "out" or ends and name[:4] == "down":
                j = int(name[-1])
                product_done(name)
                x = x_tok[:, :, j * NG:(j + 1) * NG]
                v.tensor_tensor(x, acc[:, n % 2], x, ALU.add).then_inc(read_dve, 1)
            if ends and name == "out1":
                dve.wait_ge(read_dve, reads_before(n, "dve"))
                square(1, x_tok)
                scale(1, x_tok)
                turn_split("h2", xT_hi, xT_lo)
            if ends and name[:2] == "up":
                j = int(name[2:])
                dve.wait_ge(relu_ready, j + 1)
                v.scalar_tensor_tensor(out=relu2[:, j % 2, :], in0=flat, scalar=0.0, in1=relu[:, j % 2, :],
                                       op0=ALU.max, op1=ALU.mult).then_inc(read_dve, 1)
                dve.wait_ge(read_dve, reads_before(n, "dve"))
                dve.wait_ge(a_hi, j + 1)
                v.tensor_tensor(aT_lo[:, 4 * j:4 * j + 4, :].rearrange("p a b -> p (a b)"), relu2[:, j % 2, :],
                                aT_hi[:, 4 * j:4 * j + 4, :].rearrange("p a b -> p (a b)").bitcast(F32),
                                ALU.subtract).then_inc(a_lo, 1)
            if ends and name == "down1":
                dve.wait_ge(read_dve, reads_before(n, "dve"))
                square(2, x_tok)
                dve.wait_ge(rstd_ready, 3)
                dve.wait_ge(gain_in, 16)
                for t in range(TT):
                    last = v.scalar_tensor_tensor(out=x_tok[:, t, :], in0=x_tok[:, t, :], scalar=rstd[:, 2, t:t + 1],
                                                  in1=gain_a[:, :], op0=ALU.mult, op1=ALU.mult)
                last.then_inc(x_done, 1)
                dve.wait_ge(x_done, 1)
                square(3, x_tok)
                scale(3, x_tok)
                turn_split("h3", xT_hi, xT_lo)
            if u == B2 + 2:
                gla_rank()
                lru_decay()
            if u == B2 + 3:
                gla_cumulative()
            if u == B2 + 4:
                lru_conv()
            if u == B2 + 6:
                gla_scaled()
            if u == B2 + 8:
                gla_keys()
                lru_scan()
            if u == B2 + 9:
                gla_states()
            if u == B2 + 10:
                gla_result()
            if u == B2 + 11:
                lru_result()
            if u == B2 + 12:
                lru_rest()
            moba_steps([(u, k) for k in range(1, UNITS[u][2])])
            if u == MB_TURN0[0]:
                turn_split("moba0", y2T_hi, y2T_lo, LC + 2, 0)
            if ends and name in ("mqk0", "mqk1", "gqk", "mv", "gv", "gout", "lru"):
                product_done(name)
                if name[:3] == "mqk":
                    qk = mbqk[:, int(name[3])].rearrange("p c t -> p (c t)")
                    v.tensor_scalar(qk[:, 0:NG], acc[:, n % 2, 0, :], MB_D ** -0.5, None, ALU.mult)
                    last = v.tensor_copy(qk[:, NG:], acc[:, n % 2, 1, :])
                elif name == "gqk":
                    last = v.tensor_copy(gqk[:].rearrange("p a b -> p (a b)"), acc[:, n % 2, 0, :])
                elif name == "lru":
                    last = v.tensor_copy(lruT[:, :, LRU_TAPS - 1:], flat.rearrange("p (a b) -> p a b", b=T))
                else:
                    to = {"mv": mbv, "gv": gv, "gout": gout}[name]
                    last = v.tensor_copy(to[:], acc[:, n % 2, :, 0:width(n)])
                last.then_inc(read_dve, 1)
            if ends and name[:3] == "mix" or ends and name[:2] == "dn":
                j = int(name[-1])
                product_done(name)
                v.tensor_copy(mixed[:, :, j * NG:(j + 1) * NG], acc[:, n % 2]).then_inc(read_dve, 1)
            if ends and name == "mix1":
                dve.wait_ge(read_dve, reads_before(n, "dve"))
                square(4, mixed)
                dve.wait_ge(gain_in, 32)
                residual(4, gain_b, 1)
                dve.wait_ge(x_done, 2)
                square(5, x_tok)
                scale(5, x_tok)
                turn_split("h4", xT_hi, xT_lo)
            if ends and name[:2] == "gu":
                j = int(name[2:])
                dve.wait_ge(sig2_ready, j + 1)
                link(v.tensor_tensor(sig2[:, j % 2, :], acc[:, n % 2, 0, :], sig2[:, j % 2, :], ALU.mult))
                v.tensor_tensor(act2[:, j % 2, :], acc[:, n % 2, 1, :], sig2[:, j % 2, :],
                                ALU.mult).then_inc(read_dve, 1)
                dve.wait_ge(act2_hi, j + 1)
                v.tensor_tensor(a2T_lo[:, 2 * j:2 * j + 2, :].rearrange("p a b -> p (a b)"), act2[:, j % 2, :],
                                a2T_hi[:, 2 * j:2 * j + 2, :].rearrange("p a b -> p (a b)").bitcast(F32),
                                ALU.subtract).then_inc(act2_lo, 1)
            if ends and name == "dn1":
                dve.wait_ge(read_dve, reads_before(n, "dve"))
                square(6, mixed)
                dve.wait_ge(gain_in, 48)
                residual(6, gain_b, 2)

    @block.gpsimd
    def _(pool):
        g = nc.gpsimd
        steps = [0]

        def link(ins):
            steps[0] += 1
            ins.then_inc(pool_step, 1)
            pool.wait_ge(pool_step, steps[0])

        signalled = {}

        def signal(ins, to):
            signalled[to] = signalled.get(to, 0) + 1
            ins.then_inc(to, 1)
            pool.wait_ge(to, signalled[to])

        def inverse_root(j):
            pool.wait_ge(sq_act, j + 1)
            pool.wait_ge(sq_dve, j + 1)
            link(g.tensor_scalar(mean_sq[:, j, :], squares[:, j, :], 1.0 / D, EPS, ALU.mult, ALU.add))
            signal(g.tensor_tensor(rstd[:, j, :], mean_sq[:, j, :], mhalf[:].to_broadcast([P, TT]),
                                   ALU.pow), rstd_ready)

        def keep(view, above):
            w = view.rearrange("p (a c) -> p a c", c=P)[:, 0:3:2, :]
            return g.affine_select(out=w, in_=w, pattern=[[0, 2], [1, P]], compare_op=above, fill=0.0, base=0,
                                   channel_multiplier=-1)

        link(g.memset(mhalf[:], -0.5))
        signal(g.memset(rel33[BUCKETS:BUCKETS + 1, :], 1.0), pool_set)
        inverse_root(0)
        for i in range(SB_H + 1):
            if i >= 1:
                pool.wait_ge(sb_a, i)
                signal(keep(sba[:, (i - 1) % 2], ALU.is_gt), sb_am)
            if i < SB_H:
                pool.wait_ge(sb_t, i + 1)
                signal(keep(sbw[:, i % 2], ALU.is_gt), sb_tm)
        for h in range(ML_H):
            pool.wait_ge(ml_w, h + 1)
            signal(keep(sba[:, h % 2], ALU.is_ge), ml_wm)
        pool.wait_ge(ml_ss, ML_H)
        link(g.tensor_scalar(ml_ms[:], ml_sq[:], 1.0 / ML_D, EPS, ALU.mult, ALU.add))
        signal(g.tensor_tensor(ml_rstd[:].rearrange("p t h -> p (t h)"), ml_ms[:].rearrange("p t h -> p (t h)"),
                               mhalf[:].to_broadcast([P, TT * ML_H]), ALU.pow), ml_rs)
        inverse_root(1)
        inverse_root(2)
        inverse_root(3)
        link(g.memset(gnew, 1.0))
        link(g.memset(gnew.rearrange("p (n c) -> p n c", c=GLA_CHUNK)[:, :, 0:1], 0.0))
        link(g.memset(lruT[:, :, 0:LRU_TAPS - 1], 0.0))
        signal(g.memset(gstate[:], 0.0), g_sets)
        pool.wait_ge(g_atc, 1)
        link(g.affine_select(out=gattn[:], in_=gattn[:], pattern=[[0, GLA_H], [0, TT], [1, P]],
                             compare_op=ALU.is_ge, fill=0.0, base=0, channel_multiplier=-1))
        signal(g.memset(gattn[0:GLA_CHUNK, :, :, GLA_CHUNK:P], 0.0), g_atm)
        pool.wait_ge(g_oss, 1)
        link(g.tensor_scalar(gss[:, 1, :], gss[:, 0, :], 1.0 / GLA_DV, EPS, ALU.mult, ALU.add))
        signal(g.tensor_tensor(gss[:, 2, :], gss[:, 1, :], mhalf[:].to_broadcast([P, TT * GLA_H]),
                               ALU.pow), g_rs)
        inverse_root(4)
        inverse_root(5)
        inverse_root(6)

    ctx.close()


INPUTS = ["x", "norm_mix_g", "w_in", "b_if", "ml_norm_g", "conv_w", "w_ml_proj", "w_sc_proj", "w_sb_proj",
          "w_out", "norm_mlp_g", "w_up", "w_down", "norm_final_g", "pre_mix_norm_2", "post_mix_norm_2",
          "pre_ffn_norm_2", "post_ffn_norm_2", "w_in_2", "w_out_2", "lru_conv_w_2", "lru_conv_b_2",
          "lru_wa_2", "lru_ba_2", "lru_wx_2", "lru_bx_2", "lru_lambda_2", "gla_gate_w2_2", "gla_gate_b_2",
          "gla_norm_2", "rel_bias_2", "w_ffn_gate_2", "w_ffn_up_2", "w_ffn_down_2"]


def constants():
    import numpy as np

    con = np.zeros((P, K_END), np.float32)
    con[:, K_ID:K_ID + P] = np.eye(P)
    con[:, K_TRI:K_TRI + P] = -np.tril(np.ones((P, P)))
    con[:, K_ONES:K_ONES + P] = -1.0
    sel = np.repeat(np.eye(ML_H), P, axis=1).astype(np.float32)
    hot = np.zeros((BUCKETS + 1, 2 * T), np.float32)
    exact = BUCKETS // 2
    for j in range(2 * T):
        n = T - 1 - j
        if n < 0:
            hot[BUCKETS, j] = MASKED
            continue
        far = exact + int(np.float32(np.log(np.float32(max(n, 1) / exact))) / np.float32(np.log(128 / exact))
                          * np.float32(BUCKETS - exact))
        hot[n if n < exact else min(far, BUCKETS - 1), j] = 1.0
    return {"con": con, "sel": sel, "hot": hot}


def kernel(**inputs):
    import numpy as np
    import concourse.bacc as bacc
    from concourse.bass_utils import run_bass_kernel_spmd

    nc = bacc.Bacc("TRN2", target_bir_lowering=False, num_devices=1)
    vector_rows = dict(VECS)
    arrays = {}
    for name in INPUTS:
        a = np.asarray(inputs[name])
        if name in vector_rows:
            a = a.reshape(vector_rows[name], P)
        elif name == "lru_wa_2" or name == "lru_wx_2":
            a = a.reshape(a.shape[1:])
        elif name != "rel_bias_2":
            a = a.reshape(-1, a.shape[-1])
        arrays[name] = np.ascontiguousarray(a)
    arrays.update(constants())
    dram = {name: nc.dram_tensor("in_" + name, a.shape, F32, kind="ExternalInput").ap() for name, a in arrays.items()}
    out = nc.dram_tensor("out", (T, D), F32, kind="ExternalOutput").ap()
    build(nc, dram, out)
    r = run_bass_kernel_spmd(nc, [{"in_" + name: a for name, a in arrays.items()}], core_ids=[0])
    return r.results[0]["out"].reshape(1, T, D)
```

```python
from contextlib import ExitStack

import concourse.bass as bass
import concourse.mybir as mybir

F32 = mybir.dt.float32
F32R = mybir.dt.float32r
ALU = mybir.AluOpType
ACT = mybir.ActivationFunctionType
AX = mybir.AxisListType

P = 128
T = 256
TT = T // P
D = 1024
KD = D // P
NG = 512
UK = 4
EPS = 1e-6
MASKED = -1e30

ML_H, ML_D = 4, 256
SB_H, SB_D = 16, 64
CONV_K = 3
D_FF = 4 * D
KF = D_FF // P
C_MLQ, C_MLK, C_MLV, C_MLO = 0, D, 2 * D, 3 * D
C_IF = 4 * D
C_SCB = C_IF + 2 * ML_H
C_SCC, C_SCU = C_SCB + D, C_SCB + 2 * D
C_SBQ, C_SBK, C_SBV = C_SCB + 3 * D, C_SCB + 4 * D, C_SCB + 5 * D
C_GML, C_GSC, C_GSB = C_SCB + 6 * D, C_SCB + 7 * D, C_SCB + 8 * D

LRU_W, LRU_TAPS, LRU_C = 256, 4, 8.0
GLA_H, GLA_DK, GLA_DV, GLA_RANK, GLA_CHUNK, GLA_TAU = 4, 32, 64, 16, 64, 16.0
MB_H, MB_D = 8, 64
D_FF2 = 2816
KF2 = D_FF2 // P
GU = 256
C2_LRU = 0
C2_GQ = 2 * LRU_W
C2_GV = C2_GQ + 2 * GLA_H * GLA_DK
C2_GOUT = C2_GV + GLA_H * GLA_DV + GLA_RANK
C2_MQ = C2_GOUT + GLA_H * GLA_DV
C2_MK, C2_MV = C2_MQ + MB_H * MB_D, C2_MQ + 2 * MB_H * MB_D
BUCKETS = 32
ROOT_FLOOR = 2.0 ** -100
GELU_C = 2.0 * (2.0 / 3.141592653589793) ** 0.5

PIECES = ((0, 2 * P), (2 * P, NG), (NG, D))

LANDS, PARTS = 3, 3

K_ID, K_TRI, K_ONES, K_END = 0, P, 2 * P, 3 * P

VECS = [("norm_mix_g", 8), ("norm_mlp_g", 8), ("pre_mix_norm_2", 8), ("pre_ffn_norm_2", 8),
        ("ml_norm_g", 8), ("conv_w", 24), ("lru_conv_w_2", 8), ("lru_conv_b_2", 2),
        ("lru_ba_2", 2), ("lru_bx_2", 2), ("lru_lambda_2", 2), ("gla_gate_b_2", 1),
        ("gla_norm_2", 2)]
V_AT = {}
V_ROWS = 0
for _name, _rows in VECS:
    V_AT[_name] = V_ROWS
    V_ROWS += _rows


def plan_groups():
    g = []

    def halves(name, weight, col, act, form, k=KD):
        for j in range(2):
            g.append((f"{name}{j}", weight, [(col + j * NG, NG)], k, act, form))

    halves("sbq", "w_in", C_SBQ, "xT", "feat")
    halves("sbk", "w_in", C_SBK, "xT", "feat")
    halves("sbv", "w_in", C_SBV, "xT", "tok")
    halves("mlq", "w_in", C_MLQ, "xT", "feat")
    halves("mlk", "w_in", C_MLK, "xT", "feat")
    halves("mlv", "w_in", C_MLV, "xT", "tok")
    halves("mlo", "w_in", C_MLO, "xT", "tok")
    halves("scc", "w_in", C_SCC, "xT", "feat")
    halves("scu", "w_in", C_SCU, "xT", "feat")
    halves("scb", "w_in", C_SCB, "xT", "feat")
    for b, col in (("sb", C_GSB), ("ml", C_GML), ("sc", C_GSC)):
        for j in range(2):
            g.append((f"g{b}{j}", "w_in", [(col + j * NG, NG)], KD, "xT", "tok"))
            g.append((f"p{b}{j}", f"w_{b}_proj", [(j * NG, NG)], KD, f"y{b}T", "tok"))
    halves("out", "w_out", 0, "mT", "tok")
    for j in range(D_FF // NG):
        g.append((f"up{j}", "w_up", [(j * NG, NG)], KD, "xT", "feat"))
    halves("down", "w_down", 0, "aT", "tok", KF)
    w2 = "w_in_2"
    g.append(("lru", w2, [(C2_LRU, 2 * LRU_W)], KD, "xT", "feat"))
    g.append(("gv", w2, [(C2_GV, GLA_H * GLA_DV + GLA_RANK)], KD, "xT", "tok"))
    g.append(("mqk0", w2, [(C2_MQ, 2 * P), (C2_MK, 2 * P)], KD, "xT", "feat"))
    g.append(("gqk", w2, [(C2_GQ, 2 * P)], KD, "xT", "feat"))
    g.append(("gout", w2, [(C2_GOUT, GLA_H * GLA_DV)], KD, "xT", "tok"))
    g.append(("mv", w2, [(C2_MV, NG)], KD, "xT", "tok"))
    g.append(("mqk1", w2, [(C2_MQ + 2 * P, 2 * P), (C2_MK + 2 * P, 2 * P)], KD, "xT", "feat"))
    halves("mix", "w_out_2", 0, "y2T", "tok")
    for j in range(D_FF2 // GU):
        g.append((f"gu{j}", ("w_ffn_gate_2", "w_ffn_up_2"), [(j * GU, GU), (j * GU, GU)], KD, "xT", "feat"))
    halves("dn", "w_ffn_down_2", 0, "a2T", "tok", KF2)
    return g


GROUPS = plan_groups()
G_AT = {grp[0]: n for n, grp in enumerate(GROUPS)}
UNITS = [(n, k, min(UK, grp[3] - k)) for n, grp in enumerate(GROUPS) for k in range(0, grp[3], UK)]
_at = UNITS.index((G_AT["mix0"], 0, UK))
UNITS[_at:_at + 4] = [(G_AT[f"mix{j}"], k, m) for k, m in ((0, 4), (4, 2), (6, 2)) for j in range(2)]
FIRST_U, LAST_U = {}, {}
for _u, (_n, _k, _m) in enumerate(UNITS):
    FIRST_U.setdefault(GROUPS[_n][0], _u)
    LAST_U[GROUPS[_n][0]] = _u
NU = len(UNITS)


def width(n):
    return sum(w for _, w in GROUPS[n][2])


def readers(name):
    if name[:3] in ("mlo", "gsb", "gml", "gsc", "mix") or name[:2] in ("mv", "dn"):
        return ("act",)
    return ("dve",)


def reads_before(n, eng):
    return sum(eng in readers(GROUPS[m][0]) for m in range(n + 1))


TURNS = [("x", KD, "norm_mix_g"), ("ysb", KD, None), ("yml", KD, "ml_norm_g"), ("merged", KD, None),
         ("h2", KD, "norm_mlp_g"), ("h3", KD, "pre_mix_norm_2"), ("gla", 2, "gla_norm_2"),
         ("moba0", 2, None), ("moba1", 2, None), ("h4", KD, "pre_ffn_norm_2")]
TURN_AT = {}
_b = 0
for _name, _k, _ in TURNS:
    TURN_AT[_name] = _b
    _b += _k // 2

SB0 = LAST_U["sbv1"] + 1
ML0 = SB0 + SB_H + 2
GATE0 = SB0 + SB_H
U_IF = 1
TURN_SB = ML0 + 6
TURN_ML = TURN_SB + 2
B2 = FIRST_U["lru"]
MB_AT = [(B2 + 11, 4), (B2 + 12, 2), (B2 + 12, 4), (B2 + 13, 2), (B2 + 14, 1), (B2 + 14, 3), (B2 + 15, 1),
         (B2 + 15, 2), (B2 + 15, 4), (B2 + 16, 1), (B2 + 16, 2)]
MB_TURN0, MB_TURN1 = (B2 + 15, 3), (B2 + 17, 1)


def build(nc, dram, out):
    ctx = ExitStack()

    def sb(name, shape, dt=F32, stack=None):
        return (stack or ctx).enter_context(nc.sbuf_tensor(name, shape, dt))

    def sem(name):
        return ctx.enter_context(nc.semaphore(name))

    land = sb("land", [P, LANDS, UK, NG])
    whi = sb("whi", [P, PARTS, UK, NG], F32R)
    wlo = sb("wlo", [P, PARTS, UK, NG], F32R)
    xT_hi = sb("xT_hi", [P, KD, T], F32R)
    xT_lo = sb("xT_lo", [P, KD, T], F32R)
    x_tok = sb("x_tok", [P, TT, D])
    tok = sb("tok", [P, TT, D])
    con = sb("con", [P, K_END])
    diag = sb("diag", [P, TT, P])
    rows = diag[:, 0, :]
    row = sb("row", [P, T])
    vecs = sb("vecs", [P, V_ROWS])
    squares = sb("squares", [P, 7, 2, TT])
    mean_sq = sb("mean_sq", [P, 7, TT])
    rstd = sb("rstd", [P, 7, TT])
    factor3 = sb("factor3", [P, TT])
    mhalf = sb("mhalf", [P, 1])
    LC = LRU_W // P
    lamb = sb("lamb", [P, 8, LC])
    ident = con[:, K_ID:K_ID + P]
    negones = con[:, K_ONES:K_ONES + P]

    mix, area = ExitStack(), ExitStack()
    sbqT = sb("sbqT", [P, KD, T], stack=area)
    sbkT = sb("sbkT", [P, KD, T], stack=area)
    sbv = sb("sbv", [P, TT, D], stack=area)
    area.close()
    cT = sb("cT", [P, KD, T], stack=mix)
    zT = sb("zT", [P, KD, T + CONV_K - 1], stack=mix)
    conv = sb("conv", [P, 4, T], stack=mix)
    sb("pad0", [P, KD * T - KD * (CONV_K - 1) - 4 * T], stack=mix)
    mlqT = sb("mlqT", [P, KD, T], stack=area)
    mlkT = sb("mlkT", [P, KD, T], stack=area)
    mlv = sb("mlv", [P, TT, D], stack=area)
    area.close()
    ymlT_hi = sb("ymlT_hi", [P, KD, T], F32R, stack=mix)
    ymlT_lo = sb("ymlT_lo", [P, KD, T], F32R, stack=mix)
    gate = sb("gate", [P, TT, NG], stack=mix)
    gated = sb("gated", [P, TT, NG], stack=mix)
    mlo = sb("mlo", [P, TT, D], stack=mix)
    ysbT_hi = sb("ysbT_hi", [P, KD, T], F32R, stack=mix)
    ysbT_lo = sb("ysbT_lo", [P, KD, T], F32R, stack=mix)
    sel = sb("sel", [ML_H, ML_H * P], stack=area)
    i_row = sb("i_row", [ML_H, T], stack=area)
    f_row = sb("f_row", [ML_H, T], stack=area)
    e_row = sb("e_row", [ML_H, T], stack=area)
    one_row = sb("one_row", [ML_H, T], stack=area)
    negm_row = sb("negm_row", [ML_H, T], stack=area)
    bm_row = sb("bm_row", [ML_H, T], stack=area)
    early = ExitStack()
    hot = sb("hot", [BUCKETS + 1, 2 * T], stack=early)
    tab = sb("tab", [MB_H, 2 * T], stack=early)
    rel33 = sb("rel33", [BUCKETS + 1, MB_H], stack=early)
    w_if = sb("w_if", [P, KD, 2 * ML_H], stack=early)
    w_if_hi = sb("w_if_hi", [P, KD, 2, 8, ML_H], F32R, stack=early)
    w_if_lo = sb("w_if_lo", [P, KD, 2, 8, ML_H], F32R, stack=early)
    early.close()
    sbw_hi = sb("sbw_hi", [P, 2, 3 * P], F32R, stack=area)
    sbw_lo = sb("sbw_lo", [P, 2, 3 * P], F32R, stack=area)
    sums_r = sb("sums_r", [P, 2 * P], F32R, stack=area)
    area.close()
    yscT_hi = sb("yscT_hi", [P, KD, T], F32R, stack=mix)
    yscT_lo = sb("yscT_lo", [P, KD, T], F32R, stack=mix)
    sbw = sb("sbw", [P, 2, 3 * P], stack=mix)
    sba = sb("sba", [P, 2, 3 * P], stack=mix)
    b_if = sb("b_if", [ML_H, 2], stack=mix)
    c_col = sb("c_col", [P, TT, ML_H], stack=mix)
    floor_col = sb("floor_col", [P, TT, ML_H], stack=mix)
    ml_den = sb("ml_den", [P, 4, TT], stack=mix)
    ml_sq = sb("ml_sq", [P, TT, ML_H], stack=mix)
    ml_ms = sb("ml_ms", [P, TT, ML_H], stack=mix)
    ml_rstd = sb("ml_rstd", [P, TT, ML_H], stack=mix)
    mix.close()

    ffn = ExitStack()
    aT_hi = sb("aT_hi", [P, KF, T], F32R, stack=ffn)
    aT_lo = sb("aT_lo", [P, KF, T], F32R, stack=ffn)
    relu = sb("relu", [P, 2, 2 * NG], stack=ffn)
    relu2 = sb("relu2", [P, 2, 2 * NG], stack=ffn)
    gain_a = sb("gain_a", [P, D], stack=ffn)
    ffn.close()

    two = ExitStack()
    y2T_hi = sb("y2T_hi", [P, KD, T], F32R, stack=two)
    y2T_lo = sb("y2T_lo", [P, KD, T], F32R, stack=two)
    gain_b = sb("gain_b", [P, D], stack=two)
    a2T_hi = sb("a2T_hi", [P, KF2, T], F32R, stack=area)
    a2T_lo = sb("a2T_lo", [P, KF2, T], F32R, stack=area)
    sig2 = sb("sig2", [P, 2, 2 * T], stack=area)
    act2 = sb("act2", [P, 2, 2 * T], stack=area)
    up2 = sb("up2", [P, 2, 2 * T], stack=area)
    mixed = sb("mixed", [P, TT, D], stack=area)
    area.close()
    mbqk = sb("mbqk", [P, 2, 4, T], stack=two)
    mbv = sb("mbv", [P, TT, MB_H * MB_D], stack=two)
    bias = sb("bias", [P, MB_H, 3 * P], stack=two)
    lw = sb("lw", [P, 9, LC, T], stack=two)
    mbs = sb("mbs", [P, 3, 3 * P], stack=two)
    mbp = sb("mbp", [P, 2, 3 * P], stack=two)
    mb_max = sb("mb_max", [P, MB_H, TT], stack=two)
    mb_sum = sb("mb_sum", [P, MB_H, TT], stack=two)
    mb_inv = sb("mb_inv", [P, MB_H, TT], stack=two)
    GD = GLA_H * GLA_DV
    gv = sb("gv", [P, TT, GD + GLA_RANK], stack=two)
    gqk = sb("gqk", [P, 2, T], stack=two)
    gout = sb("gout", [P, TT, GD], stack=two)
    gsig = sb("gsig", [P, TT, GD], stack=two)
    glrT = sb("glrT", [GLA_RANK, T], stack=two)
    gw2 = sb("gw2", [GLA_RANK, P], stack=two)
    gla = sb("gla", [P, 6, T], stack=two)
    gdec = sb("gdec", [P, 4], stack=two)
    gnew = lw[:, 7, 0, :]
    qd, kd, kl = gla[:, 3, :], gla[:, 4, :], gla[:, 5, :]
    kl_tok = sb("kl_tok", [P, TT, P], stack=two)
    gattn = sb("gattn", [P, GLA_H, TT, P], stack=two)
    gstate = sb("gstate", [P, 4, GD], stack=two)
    gsq = gattn[:].rearrange("p h t c -> p (h t c)")[:, 0:TT * GD].rearrange("p (a b) -> p a b", b=GLA_DV)
    gss = sb("gss", [P, 3, TT * GLA_H], stack=two)
    lruT = sb("lruT", [P, 2 * LC, T + LRU_TAPS - 1], stack=two)
    wab = sb("wab", [P, 2, LC, 64], stack=two)
    two.close()

    acc = ctx.enter_context(nc.psum_tensor("acc", [P, 2, 2, NG], F32))
    M = [ctx.enter_context(nc.psum_tensor(f"m{i}", [P, NG], F32)) for i in range(4)]

    landed = [sem(f"landed{i}") for i in range(LANDS)]
    x_in = [sem(f"x_in{t}") for t in range(TT)]
    rows_in, con_in, small_in, gain_in, late_in = (
        sem(n) for n in ("rows_in", "con_in", "small_in", "gain_in", "late_in"))
    tab_out, copies_out, bias_in, stored = (sem(n) for n in ("tab_out", "copies_out", "bias_in", "stored"))
    half_hi, half_lo = sem("half_hi"), sem("half_lo")
    hi_ready, lo_ready, units_done = sem("hi_ready"), sem("lo_ready"), sem("units_done")
    read_act, read_dve = sem("read_act"), sem("read_dve")
    turned, turn_hi, turn_lo = sem("turned"), sem("turn_hi"), sem("turn_lo")
    sq_act, rstd_ready, factor_ready = sem("sq_act"), sem("rstd_ready"), sem("factor_ready")
    diag_ready, row_made, row_ready = sem("diag_ready"), sem("row_made"), sem("row_ready")
    bank_squared = sem("bank_squared")
    xg_ready, gained, x_part = sem("xg_ready"), sem("gained"), sem("x_part")
    norm_act, norm_dve = sem("norm_act"), sem("norm_dve")
    act_step, dve_step, pool_step = sem("act_step"), sem("dve_step"), sem("pool_step")
    vecs_turned, vecs_ready, tab_done, tab_ready = (
        sem(n) for n in ("vecs_turned", "vecs_ready", "tab_done", "tab_ready"))
    pool_set = sem("pool_set")
    if_hi, if_lo, if_done = sem("if_hi"), sem("if_lo"), sem("if_done")
    rows_ready, e_ready, scans_ready = (
        sem(n) for n in ("rows_ready", "e_ready", "scans_ready"))
    cols_turned, c_ready, floor_ready = sem("cols_turned"), sem("c_ready"), sem("floor_ready")
    sums_ready, sb_hi, sb_lo = sem("sums_ready"), sem("sb_hi"), sem("sb_lo")
    sb_z, sb_log, sb_t, sb_tm, sb_r, sb_a, sb_am, sb_av, sb_y = (
        sem(n) for n in ("sb_z", "sb_log", "sb_t", "sb_tm", "sb_r", "sb_a", "sb_am", "sb_av", "sb_y"))
    sig_o = sem("sig_o")
    ml_s, ml_w, ml_wm, ml_p, ml_num, ml_y, ml_ss, ml_rs, yml_ready = (
        sem(n) for n in ("ml_s", "ml_w", "ml_wm", "ml_p", "ml_num", "ml_y", "ml_ss", "ml_rs", "yml_ready"))
    ysc_hi, ysc_lo = sem("ysc_hi"), sem("ysc_lo")
    a_hi, a_lo = sem("a_hi"), sem("a_lo")
    mb_s, mb_logit, mb_max_ready, mb_e, mb_pt, mb_p, mb_av, mb_y = (
        sem(n) for n in ("mb_s", "mb_logit", "mb_max_ready", "mb_e", "mb_pt", "mb_p", "mb_av", "mb_y"))
    g_sets, glr_turned, glr_ready, g_gate, g_ln, g_min, g_cum, g_exp, g_qk, g_at, g_atc, g_atm = (
        sem(n) for n in ("g_sets", "glr_turned", "glr_ready", "g_gate", "g_ln", "g_min", "g_cum", "g_exp",
                         "g_qk", "g_at", "g_atc", "g_atm"))
    kl_turned, kl_ready, g_kv, g_state, g_o, g_osq, g_oss, g_rs, g_y, g_sig = (
        sem(n) for n in ("kl_turned", "kl_ready", "g_kv", "g_state", "g_o", "g_osq", "g_oss", "g_rs", "g_y",
                         "g_sig"))
    l_conv, l_gates, l_sig, l_exp, l_m2, l_mult, l_y, l_hi, l_lo, l_gin, l_gel, l_lam, l_sp, l_spn = (
        sem(n) for n in ("l_conv", "l_gates", "l_sig", "l_exp", "l_m2", "l_mult", "l_y", "l_hi", "l_lo",
                         "l_gin", "l_gel", "l_lam", "l_sp", "l_spn"))
    gate2_ready, sig2_ready, act2_ready = sem("gate2_ready"), sem("sig2_ready"), sem("act2_ready")
    act2_hi, act2_lo = sem("act2_hi"), sem("act2_lo")

    weights = {n: dram[n] for n in dram}
    by_distance = nc.dram_tensor("by_distance", (1, MB_H * 2 * T), F32, kind="Internal").ap()
    by_query = nc.dram_tensor("by_query", (P, MB_H * 2 * T), F32, kind="Internal").ap()

    def land_count(u):
        return 16 * sum(len(GROUPS[UNITS[v][0]][2]) for v in range(u % LANDS, u + 1, LANDS))

    block = ctx.enter_context(nc.Block())

    @block.sync
    def _(sp):
        for t in range(TT):
            sp.dma_start(x_tok[:, t, :], dram["x"][t * P:(t + 1) * P, :]).then_inc(x_in[t], 16)
        sp.dma_start(con[:], dram["con"]).then_inc(con_in, 16)
        sp.dma_start(rows[0:V_ROWS, :], dram["vectors"]).then_inc(rows_in, 16)

        def load(u):
            n, k, m = UNITS[u]
            _, weight, segs, *_ = GROUPS[n]
            if u >= LANDS:
                sp.wait_ge(lo_ready, u - LANDS + 1)
            at = 0
            for i, (col, w) in enumerate(segs):
                src = weights[weight if isinstance(weight, str) else weight[i]]
                sp.dma_start(land[:, u % LANDS, 0:m, at:at + w],
                             src[k * P:(k + m) * P, col:col + w].rearrange("(k p) n -> p k n", p=P)
                             ).then_inc(landed[u % LANDS], 16)
                at += w

        for u in range(NU):
            load(u)
            if u == 1:
                sp.dma_start(w_if[:], dram["w_in"][:, C_IF:C_IF + 2 * ML_H].rearrange(
                    "(k p) n -> p k n", p=P)).then_inc(small_in, 16)
                sp.dma_start(b_if[:], dram["b_if"]).then_inc(small_in, 16)
                sp.dma_start(hot[:], dram["hot"]).then_inc(small_in, 16)
                sp.dma_start(sel[:], dram["sel"]).then_inc(small_in, 16)
                sp.dma_start(rel33[0:BUCKETS, :], dram["rel_bias_2"]).then_inc(small_in, 16)
            if u == 5:
                sp.wait_ge(tab_ready, 1)
                sp.dma_start(by_distance.rearrange("a (h j) -> (a h) j", h=MB_H), tab[:]).then_inc(tab_out, 16)
            if u == SB0:
                sp.wait_ge(tab_out, 16)
                sp.dma_start(by_query, by_distance.to_broadcast([P, MB_H * 2 * T])).then_inc(copies_out, 16)
            if u == FIRST_U["up1"]:
                sp.wait_ge(turn_lo, TURN_AT["merged"] + 4)
                sp.wait_ge(turn_hi, TURN_AT["merged"] + 4)
                sp.dma_start(gain_a[:], dram["norm_final_g"].to_broadcast([P, D])).then_inc(gain_in, 16)
            if u == B2 + 4:
                sp.wait_ge(factor_ready, 1)
                sp.dma_start(gw2[:], dram["gla_gate_w2_2"]).then_inc(late_in, 16)
                for i, name in enumerate(("lru_wa_2", "lru_wx_2")):
                    for c in range(LC):
                        sp.dma_start(wab[:, i, c, :], dram[name][2 * c:2 * c + 2].rearrange("b i j -> (b i) j")
                                     ).then_inc(late_in, 16)
            if u == B2 + 5:
                sp.dma_start(gain_b[:], dram["post_mix_norm_2"].to_broadcast([P, D])).then_inc(gain_in, 16)
            if u == B2 + 9:
                sp.wait_ge(copies_out, 16)
                row = MB_H * 2 * T - 1
                sp.dma_start(bias[:, :, 0:P], bass.AP(by_query.tensor, T - 1, [[row, P], [2 * T, MB_H], [1, P]])
                             ).then_inc(bias_in, 16)
                sp.dma_start(bias[:, :, P:3 * P],
                             bass.AP(by_query.tensor, T - 1 - P, [[row, P], [2 * T, MB_H], [1, T]])
                             ).then_inc(bias_in, 16)
            if u == FIRST_U["dn0"]:
                sp.wait_ge(gained, 4)
                sp.dma_start(gain_b[:], dram["post_ffn_norm_2"].to_broadcast([P, D])).then_inc(gain_in, 16)
        for i, (c0, c1) in enumerate(PIECES):
            for t in range(TT):
                sp.wait_ge(x_part, TT * (len(PIECES) + i) + t + 1)
                sp.dma_start(out[t * P:(t + 1) * P, c0:c1], x_tok[:, t, c0:c1]).then_inc(stored, 16)
        sp.wait_ge(stored, 16 * TT * len(PIECES))

    LATE = 16 * (1 + 2 * LC)

    @block.tensor
    def _(pe):
        mm = nc.tensor.matmul

        def lhs_of(act):
            return {"xT": (xT_hi, xT_lo), "ysbT": (ysbT_hi, ysbT_lo), "ymlT": (ymlT_hi, ymlT_lo),
                    "yscT": (yscT_hi, yscT_lo), "aT": (aT_hi, aT_lo), "y2T": (y2T_hi, y2T_lo),
                    "a2T": (a2T_hi, a2T_lo), "mT": (ysbT_hi, ysbT_lo)}[act]

        def turned_ready(stage, tiles):
            pe.wait_ge(turn_lo, TURN_AT[stage] + (tiles + 1) // 2)

        def wait_operand(name, act, k1):
            if act == "xT":
                turned_ready("h2" if name[:2] == "up" else
                             "h4" if name[:2] == "gu" else
                             "h3" if B2 <= FIRST_U[name] < FIRST_U["mix0"] else "x", k1)
            elif act == "mT":
                turned_ready("merged", k1)
            elif act == "ysbT":
                turned_ready("ysb", k1)
            elif act == "ymlT":
                turned_ready("yml", k1)
            elif act == "yscT":
                pe.wait_ge(ysc_lo, (k1 + 3) // 4)
            elif act == "aT":
                pe.wait_ge(a_lo, (k1 + 3) // 4)
            elif act == "a2T":
                pe.wait_ge(act2_lo, k1 // 2)
            elif k1 <= 2 * LC:
                pe.wait_ge(l_lo, 1)
                turned_ready("gla", 2)
            else:
                turned_ready("moba0" if k1 <= 6 else "moba1", 2)

        def product(u, between):
            n, k0, m = UNITS[u]
            name, _, _, kk, act, form = GROUPS[n]
            xh, xl = lhs_of(act)
            w, s = width(n), u % PARTS
            if k0 == 0 and n >= 2:
                for eng, seen in (("act", read_act), ("dve", read_dve)):
                    if eng in readers(GROUPS[n - 2][0]):
                        pe.wait_ge(seen, reads_before(n - 2, eng))
                if GROUPS[n - 2][0][:3] == "mix":
                    pe.wait_ge(gained, 2 * int(GROUPS[n - 2][0][3]) + 2)
            if u == 0:
                pe.wait_ge(half_lo, 1)
            for k in range(m):
                if k == (m // 2 if u == 0 else 0):
                    pe.wait_ge(lo_ready, u + 1)
                first, end = k0 + k == 0, k0 + k == kk - 1
                if k > 0:
                    between(u, k)
                if k % 2 == 0:
                    wait_operand(name, act, k0 + k + 2)
                if form == "tok":
                    for t in range(TT):
                        to = acc[:, n % 2, t, 0:w]
                        ts = slice(t * P, (t + 1) * P)
                        mm(to, xh[:, k0 + k, ts], whi[:, s, k, 0:w], start=first, stop=False)
                        mm(to, xh[:, k0 + k, ts], wlo[:, s, k, 0:w], start=False, stop=False)
                        last = mm(to, xl[:, k0 + k, ts], whi[:, s, k, 0:w], start=False, stop=end)
                else:
                    for c in range(w // P):
                        to = acc[:, n % 2, c // 2, (c % 2) * T:(c % 2 + 1) * T]
                        cs = slice(c * P, (c + 1) * P)
                        mm(to, whi[:, s, k, cs], xh[:, k0 + k, :], start=first and c % 2 == 0, stop=False,
                           skip_group_check=True)
                        mm(to, whi[:, s, k, cs], xl[:, k0 + k, :], start=False, stop=False,
                           skip_group_check=True)
                        last = mm(to, wlo[:, s, k, cs], xh[:, k0 + k, :], start=False, stop=end,
                                  skip_group_check=True)
            last.then_inc(units_done, 1)

        def turn(stage, src, col0=0, bank=0, half=None, parts=None):
            _, kk, _ = [s for s in TURNS if s[0] == stage][0]
            if TURN_AT[stage]:
                pe.wait_ge(turn_lo, TURN_AT[stage])
            for b in range(kk // 2) if half is None else (2 * half, 2 * half + 1):
                if parts:
                    pe.wait_ge(parts, TT * (b + 1))
                for i in range(2):
                    for t in range(TT):
                        k = 2 * b + i
                        last = nc.tensor.transpose(M[bank + b][:, (i * TT + t) * P:(i * TT + t + 1) * P],
                                                   src[:, t, col0 + k * P:col0 + (k + 1) * P], ident)
                last.then_inc(turned, 1)

        def spread(i, stage):
            pe.wait_ge(diag_ready, i + 1)
            pe.wait_ge(turn_lo, TURN_AT[stage] + 4)
            for t in range(TT):
                last = mm(M[0][:, t * P:(t + 1) * P], negones, diag[:, t, :], start=True, stop=True)
            last.then_inc(row_made, 1)

        def sb_scores(h):
            if h == 0:
                pe.wait_ge(read_dve, reads_before(G_AT["sbv1"], "dve"))
                pe.wait_ge(tab_ready, 1)
            if h >= 4:
                pe.wait_ge(sb_y, h - 3)
            else:
                pe.wait_ge(c_ready, 1)
                pe.wait_ge(floor_ready, 1)
                pe.wait_ge(rows_ready, 1)
            c, o = h // 2, SB_D * (h % 2)
            z = M[h % 4]
            mm(z[:, 0:T], sbkT[o:o + SB_D, c, 0:P], sbqT[o:o + SB_D, c, :], start=True, stop=True)
            mm(z[:, T:T + P], sbkT[o:o + SB_D, c, P:T], sbqT[o:o + SB_D, c, P:T], start=False, stop=True,
               skip_group_check=True).then_inc(sb_z, 1)

        def sb_remain(h):
            if h == 0:
                pe.wait_ge(sums_ready, 1)
            pe.wait_ge(sb_lo, h + 1)
            z = M[h % 4]
            for w in (sbw_hi[:, h % 2], sbw_lo[:, h % 2]):
                mm(z[:, 0:3 * P], sums_r[:, 0:P], w, start=False, stop=True, skip_group_check=True)
                last = mm(z[:, P:T], sums_r[:, P:], w[:, T:3 * P], start=False, stop=True, skip_group_check=True)
            last.then_inc(sb_r, 1)

        def sb_values(h):
            pe.wait_ge(sb_am, h + 1)
            o, a = M[h % 4][:, 3 * P:], sba[:, h % 2]
            v = slice(h * SB_D, (h + 1) * SB_D)
            for to, parts in ((o[:, 0:SB_D], ((0, 0),)), (o[:, SB_D:], ((P, 0), (T, 1)))):
                for at, t in parts:
                    last = mm(to, a[:, at:at + P], sbv[:, t, v], start=False, stop=True, skip_group_check=True)
            last.then_inc(sb_av, 1)

        def if_gates():
            pe.wait_ge(if_lo, 1)
            to = M[3][0:2 * 8 * ML_H, 0:T]
            for k in range(KD):
                hi, lo = (w[:, k].rearrange("p i r h -> p (i r h)") for w in (w_if_hi, w_if_lo))
                mm(to, hi, xT_hi[:, k, :], start=k == 0, stop=False)
                mm(to, hi, xT_lo[:, k, :], start=False, stop=False)
                last = mm(to, lo, xT_hi[:, k, :], start=False, stop=k == KD - 1)
            last.then_inc(if_done, 1)

        def if_cols():
            pe.wait_ge(scans_ready, 1)
            for i, row in enumerate((i_row, bm_row)):
                for t in range(TT):
                    at = (i * TT + t) * ML_H
                    last = nc.tensor.transpose(M[2][:, at:at + ML_H], row[:, t * P:(t + 1) * P],
                                               ident[0:ML_H, 0:ML_H])
            last.then_inc(cols_turned, 1)

        def ml_scores(h):
            s, b = M[2 * (h % 2)], M[2 * (h % 2) + 1]
            if h < 2:
                pe.wait_ge(sb_a, SB_H)
                pe.wait_ge(sb_y, SB_H)
                pe.wait_ge(read_dve, reads_before(G_AT["mlv1"], "dve"))
            else:
                pe.wait_ge(ml_y, h - 1)
            for i in range(2):
                c = 2 * h + i
                mm(s[:, 0:T], mlkT[:, c, 0:P], mlqT[:, c, :], start=i == 0, stop=i == 1, skip_group_check=True)
                mm(s[:, T:T + P], mlkT[:, c, P:T], mlqT[:, c, P:T], start=False, stop=i == 1,
                   skip_group_check=True)
            mm(b[:, 0:T], sel[:, h * P:(h + 1) * P], negm_row[:, :], start=True, stop=True).then_inc(ml_s, 1)

        def ml_values(h):
            pe.wait_ge(ml_p, h + 1)
            o, b, w = M[2 * (h % 2)], M[2 * (h % 2) + 1], sba[:, h % 2]
            v = slice(h * ML_D, (h + 1) * ML_D)
            ones = con[:, K_ONES:K_ONES + 1]
            mm(o[:, 0:ML_D], w[:, 0:P], mlv[:, 0, v], start=True, stop=True)
            mm(o[:, ML_D:], w[:, P:T], mlv[:, 0, v], start=True, stop=False)
            mm(o[:, ML_D:], w[:, T:T + P], mlv[:, 1, v], start=False, stop=True)
            mm(b[:, T:T + 1], w[:, 0:P], ones, start=True, stop=True)
            mm(b[:, T + 1:T + 2], w[:, P:T], ones, start=True, stop=False)
            mm(b[:, T + 1:T + 2], w[:, T:T + P], ones, start=False, stop=True).then_inc(ml_num, 1)

        def mb_scores(h):
            pe.wait_ge(read_dve, reads_before(G_AT[f"mqk{h // 4}"], "dve"))
            if h >= 2:
                pe.wait_ge(mb_max_ready, h - 1)
            half, c, o = h // 4, h % 4 // 2, MB_D * (h % 2)
            q, k = mbqk[o:o + MB_D, half, c, :], mbqk[o:o + MB_D, half, 2 + c, :]
            s = M[h % 2]
            mm(s[:, 0:P], q[:, 0:P], k[:, 0:P], start=True, stop=True)
            mm(s[:, P:3 * P], q[:, P:T], k, start=True, stop=True).then_inc(mb_s, 1)

        def mb_turn(h):
            pe.wait_ge(mb_e, h + 1)
            if h >= 1:
                pe.wait_ge(mb_p, h)
            for i in range(3):
                last = nc.tensor.transpose(M[2][:, i * P:(i + 1) * P], mbs[:, h % 3, i * P:(i + 1) * P],
                                           ident)
            last.then_inc(mb_pt, 1)

        def mb_values(h):
            pe.wait_ge(mb_p, h + 1)
            if h == 0:
                pe.wait_ge(read_act, reads_before(G_AT["mv"], "act"))
                pe.wait_ge(turn_lo, TURN_AT["gla"] + 1)
            else:
                pe.wait_ge(mb_y, h)
            o, p = M[3], mbp[:, h % 2]
            v = slice(h * MB_D, (h + 1) * MB_D)
            mm(o[:, 0:MB_D], p[:, 0:P], mbv[:, 0, v], start=True, stop=True)
            mm(o[:, MB_D:2 * MB_D], p[:, P:T], mbv[:, 0, v], start=True, stop=False)
            mm(o[:, MB_D:2 * MB_D], p[:, T:3 * P], mbv[:, 1, v], start=False, stop=True).then_inc(mb_av, 1)

        def gla_rank():
            pe.wait_ge(read_dve, reads_before(G_AT["gv"], "dve"))
            pe.wait_ge(l_sig, 1)
            for t in range(TT):
                last = nc.tensor.transpose(M[0][0:GLA_RANK, t * P:(t + 1) * P], gv[:, t, GD:GD + GLA_RANK], ident)
            last.then_inc(glr_turned, 1)

        def gla_gate():
            pe.wait_ge(late_in, LATE)
            pe.wait_ge(glr_ready, 1)
            mm(M[1][:, 0:T], gw2[:, :], glrT[:, :], start=True, stop=True).then_inc(g_gate, 1)

        def gla_scores():
            pe.wait_ge(g_qk, 3)
            for t in range(TT):
                ts = slice(t * P, (t + 1) * P)
                for h in range(GLA_H):
                    hs = slice(h * GLA_DK, (h + 1) * GLA_DK)
                    last = mm(M[h][:, ts], kd[hs, ts], qd[hs, ts], start=True, stop=True)
            last.then_inc(g_at, 1)

        def gla_keys():
            pe.wait_ge(g_atc, 1)
            for t in range(TT):
                last = nc.tensor.transpose(M[3][:, t * P:(t + 1) * P], kl[:, t * P:(t + 1) * P], ident)
            last.then_inc(kl_turned, 1)

        def gla_additions():
            pe.wait_ge(kl_ready, 1)
            for n in range(3):
                o, t = GLA_CHUNK * (n % 2), n // 2
                last = mm(M[n][:, 0:GD], kl_tok[o:o + GLA_CHUNK, t, :], gv[o:o + GLA_CHUNK, t, 0:GD],
                          start=True, stop=True)
            last.then_inc(g_kv, 1)

        def gla_values():
            pe.wait_ge(g_state, 1)
            pe.wait_ge(g_atm, 1)
            for t in range(TT):
                to = M[3][:, t * GD:(t + 1) * GD]
                for i in range(2):
                    n = 2 * t + i
                    o = GLA_CHUNK * i
                    mm(to[o:o + GLA_CHUNK, :], qd[:, n * GLA_CHUNK:(n + 1) * GLA_CHUNK], gstate[:, n, :],
                       start=True, stop=False, skip_group_check=True)
                for h in range(GLA_H):
                    hs = slice(h * GLA_DV, (h + 1) * GLA_DV)
                    last = mm(to[:, hs], gattn[:, h, t, :], gv[:, t, hs], start=False, stop=True,
                              skip_group_check=True)
            last.then_inc(g_o, 1)

        def lru_gates():
            pe.wait_ge(l_conv, 1)
            pe.wait_ge(late_in, LATE)
            pe.wait_ge(row_ready, 2)
            for i in range(2):
                for c in range(LC):
                    for b in range(2):
                        bs = slice(64 * b, 64 * b + 64)
                        last = mm(M[2 * i + b][bs, c * T:(c + 1) * T], wab[bs, i, c, :], lw[bs, 0, c, :],
                                  start=True, stop=True)
            last.then_inc(l_gates, 1)

        pe.wait_ge(con_in, 16)
        pe.wait_ge(rows_in, 16)
        nc.tensor.transpose(M[0][:, 0:V_ROWS], rows[0:V_ROWS, :], ident[0:V_ROWS, 0:V_ROWS]).then_inc(vecs_turned, 1)
        pe.wait_ge(norm_act, 1)
        pe.wait_ge(norm_dve, 1)
        pe.wait_ge(vecs_ready, 1)
        turn("x", tok)

        def moba_step(i):
            if 3 <= i < MB_H + 3:
                mb_values(i - 3)
            if 2 <= i < MB_H + 2:
                mb_turn(i - 2)
            if 0 <= i < MB_H:
                mb_scores(i)

        def between(u, k):
            if (u, k) == (LAST_U["psc1"], 2):
                pe.wait_ge(read_dve, reads_before(G_AT["psc0"], "dve"))
                turn("merged", tok, half=0)
            if (u, k) == (FIRST_U["out0"], 2):
                pe.wait_ge(read_dve, reads_before(G_AT["psc1"], "dve"))
                turn("merged", tok, half=1)
            if (u, k) == (LAST_U["out1"], 2):
                pe.wait_ge(read_dve, reads_before(G_AT["out0"], "dve"))
                turn("h2", x_tok, half=0)
            if (u, k) == (FIRST_U["up0"], 2):
                pe.wait_ge(read_dve, reads_before(G_AT["out1"], "dve"))
                turn("h2", x_tok, half=1)
            if (u, k) == (FIRST_U["up0"] + 1, 2):
                spread(0, "h2")
            if (u, k) == (LAST_U["down1"], 2):
                pe.wait_ge(xg_ready, 1)
                pe.wait_ge(row_ready, 1)
                turn("h3", tok, half=0)
            if (u, k) == (B2, 2):
                pe.wait_ge(xg_ready, 2)
                turn("h3", tok, half=1)
            if (u, k) == (B2 + 1, 3):
                spread(1, "h3")
            if (u, k) == (FIRST_U["gu0"], 2):
                pe.wait_ge(x_part, TT * len(PIECES))
                turn("h4", x_tok, half=1)
            if (u, k) == (FIRST_U["gu0"] + 1, 2):
                spread(2, "h4")
            if (u, k) == (B2 + 4, 3):
                gla_rank()
            if (u, k) == (B2 + 9, 2):
                gla_scores()
            if (u, k) == (B2 + 10, 2):
                gla_additions()
            if (u, k) == (B2 + 11, 2):
                gla_values()
            if (u, k) == (B2 + 12, 3):
                pe.wait_ge(g_y, 1)
                turn("gla", tok, 0, 3)
            if (u, k) in MB_AT:
                moba_step(MB_AT.index((u, k)))
            if (u, k) == MB_TURN0:
                pe.wait_ge(mb_y, 4)
                pe.wait_ge(mb_max_ready, 7)
                turn("moba0", tok, 2 * P, 0)
            if (u, k) == MB_TURN1:
                pe.wait_ge(mb_y, MB_H)
                turn("moba1", tok, 4 * P, 1)

        for u in range(NU):
            name = GROUPS[UNITS[u][0]][0]
            first_k = UNITS[u][1] == 0
            if name == "gu0" and first_k:
                turn("h4", x_tok, half=0, parts=x_part)
            product(u, between)
            if u == 0:
                pe.wait_ge(small_in, 80)
                pe.wait_ge(pool_set, 1)
                pe.wait_ge(turn_lo, KD // 2)
                mm(M[1][0:MB_H, :], rel33[:, :], hot[:, :], start=True, stop=True).then_inc(tab_done, 1)
            if u == U_IF:
                if_gates()
            if u == U_IF + 6:
                if_cols()
            i = u - SB0
            if i % 2 == 0 and 0 <= i <= SB_H:
                if i >= 2:
                    sb_remain(i - 2)
                    sb_remain(i - 1)
                if i < SB_H:
                    sb_scores(i)
                    sb_scores(i + 1)
            if i % 2 == 1 and 3 <= i <= SB_H + 1:
                sb_values(i - 3)
                sb_values(i - 2)
            i = u - ML0
            if 0 <= i < ML_H:
                ml_scores(i)
            if 1 <= i <= ML_H:
                ml_values(i - 1)
            if u == TURN_SB:
                pe.wait_ge(sb_y, SB_H)
                pe.wait_ge(ml_y, ML_H)
                turn("ysb", tok)
            if u == TURN_ML:
                pe.wait_ge(yml_ready, 1)
                turn("yml", mlo)
            if u == B2 + 3:
                lru_gates()
            if u == B2 + 4:
                gla_gate()
            if u == B2 + 9:
                gla_keys()
            between(u, UNITS[u][2])

    @block.scalar
    def _(act):
        steps = [0]
        squares_done = [0]
        activate = nc.scalar.activation

        def link(ins):
            steps[0] += 1
            ins.then_inc(act_step, 1)
            act.wait_ge(act_step, steps[0])

        def split(u):
            if u >= NU:
                return
            n, k, m = UNITS[u]
            w = width(n)
            act.wait_ge(landed[u % LANDS], land_count(u))
            if u >= PARTS:
                act.wait_ge(units_done, u - PARTS + 1)
            activate(whi[:, u % PARTS, 0:m, 0:w], land[:, u % LANDS, 0:m, 0:w], ACT.Copy).then_inc(hi_ready, 1)

        def square(j, src, junk, halves):
            for t in range(TT):
                cols = slice(halves[0] * NG, (halves[-1] + 1) * NG)
                ins = activate(junk, src[:, t, cols], ACT.Square, scale=D ** -0.5,
                               accum_out=squares[:, j, halves[0], t:t + 1])
                if t < TT - 1:
                    link(ins)
            squares_done[0] += 1
            ins.then_inc(sq_act, 1)
            act.wait_ge(sq_act, squares_done[0])

        def scale(j, src, count):
            act.wait_ge(rstd_ready, j + 1)
            activate(tok[:, 0, :], src[:, 0, :], ACT.Copy, scale=rstd[:, j, 0:1]).then_inc(norm_act, 1)

        def turn_split(stage, hi, k_to=0, bank=0, half=None):
            _, kk, gain = [s for s in TURNS if s[0] == stage][0]
            for b in range(kk // 2) if half is None else (2 * half, 2 * half + 1):
                act.wait_ge(turned, TURN_AT[stage] + b + 1)
                if gain is None:
                    last = activate(hi[:, k_to + 2 * b:k_to + 2 * b + 2, :],
                                    M[bank + b][:, :].rearrange("p (k t) -> p k t", k=2), ACT.Copy)
                else:
                    for i in range(2):
                        g = V_AT[gain] + 2 * b + i
                        last = activate(hi[:, k_to + 2 * b + i, :], M[bank + b][:, i * T:(i + 1) * T], ACT.Copy,
                                        scale=vecs[:, g:g + 1])
                last.then_inc(turn_hi, 1)

        def product_done(name):
            act.wait_ge(units_done, LAST_U[name] + 1)

        def sb_logs(h):
            for i in (h, h + 1):
                act.wait_ge(sb_z, i + 1)
                if i >= 2:
                    act.wait_ge(sb_lo, i - 1)
                link(activate(sbw[:, i % 2], M[i % 4][:, 0:3 * P], ACT.Abs))
                link(activate(sbw[:, i % 2], sbw[:, i % 2], ACT.Exp, scale=-1.0))
            for i in (h, h + 1):
                activate(sbw[:, i % 2], sbw[:, i % 2], ACT.Ln, bias=1.0).then_inc(sb_log, 1)

        def sb_leading(h):
            act.wait_ge(sb_tm, h + 1)
            if h >= 2:
                act.wait_ge(sb_r, h - 1)
            activate(sbw_hi[:, h % 2], sbw[:, h % 2], ACT.Copy).then_inc(sb_hi, 1)

        def sb_weights(h):
            act.wait_ge(sb_r, h + 1)
            if h >= 2:
                act.wait_ge(sb_av, h - 1)
            activate(sba[:, h % 2], M[h % 4][:, 0:3 * P], ACT.Exp).then_inc(sb_a, 1)

        def ml_weights(h):
            act.wait_ge(ml_s, h + 1)
            act.wait_ge(c_ready, 1)
            b, w = M[2 * (h % 2) + 1], sba[:, h % 2]
            activate(w[:, 0:T], b[:, 0:T], ACT.Exp, bias=c_col[:, 0, h:h + 1])
            activate(w[:, T:3 * P], b[:, P:T], ACT.Exp, bias=c_col[:, 1, h:h + 1]).then_inc(ml_w, 1)

        def ml_squares(h):
            act.wait_ge(ml_y, h + 1)
            for t in range(TT):
                last = activate(sbw[:, t, 0:T], mlo[:, t, h * ML_D:(h + 1) * ML_D], ACT.Square,
                                accum_out=ml_sq[:, t, h:h + 1])
            last.then_inc(ml_ss, 1)
            act.wait_ge(ml_ss, h + 1)

        def mb_exps(h):
            act.wait_ge(mb_max_ready, h + 1)
            s = mbs[:, h % 3]
            activate(s[:, 0:P], s[:, 0:P], ACT.Exp, bias=mb_max[:, h, 0:1], accum_out=mb_sum[:, h, 0:1])
            activate(s[:, P:3 * P], s[:, P:3 * P], ACT.Exp, bias=mb_max[:, h, 1:2],
                     accum_out=mb_sum[:, h, 1:2]).then_inc(mb_e, 1)

        def mb_weights(h):
            act.wait_ge(mb_pt, h + 1)
            if h >= 2:
                act.wait_ge(mb_av, h - 1)
            activate(mbp[:, h % 2], M[2][:, 0:3 * P], ACT.Copy).then_inc(mb_p, 1)

        def gla_logs():
            b = vecs[:, V_AT["gla_gate_b_2"]:V_AT["gla_gate_b_2"] + 1]
            act.wait_ge(g_gate, 1)
            link(activate(gla[:, 0], M[1][:, 0:T], ACT.Abs, bias=b))
            link(activate(gla[:, 0], gla[:, 0], ACT.Exp, scale=-1.0))
            activate(gla[:, 0], gla[:, 0], ACT.Ln, bias=1.0).then_inc(g_ln, 1)

        def gla_exps():
            act.wait_ge(g_cum, 1)
            activate(gla[:, 3], gla[:, 1], ACT.Exp).then_inc(g_exp, 1)
            activate(gla[:, 4], gla[:, 1], ACT.Exp, scale=-1.0).then_inc(g_exp, 1)
            activate(gla[:, 5], gla[:, 2], ACT.Exp).then_inc(g_exp, 1)
            last = gla[:, 1].rearrange("p (n c) -> p n c", c=GLA_CHUNK)[:, :, GLA_CHUNK - 1]
            activate(gdec[:, :], last, ACT.Exp).then_inc(g_exp, 1)

        def gla_copies():
            act.wait_ge(g_at, 1)
            for h in range(GLA_H):
                last = activate(gattn[:, h].rearrange("p t c -> p (t c)"), M[h][:, 0:T], ACT.Copy)
            last.then_inc(g_atc, 1)

        def gla_squares():
            act.wait_ge(g_o, 1)
            activate(gsq.rearrange("p a b -> p (a b)"), M[3][:, :], ACT.Square).then_inc(g_osq, 1)

        def lru_log():
            lam = vecs[:, V_AT["lru_lambda_2"]:V_AT["lru_lambda_2"] + LC]
            link(activate(lamb[:, 0], lam, ACT.Abs))
            activate(lamb[:, 1], lamb[:, 0], ACT.Exp, scale=-1.0).then_inc(l_lam, 1)

        def lru_sigmoids():
            act.wait_ge(l_gates, 1)
            for i, (at, name) in enumerate(((1, "lru_ba_2"), (2, "lru_bx_2"))):
                for c in range(LC):
                    for b in range(2):
                        bs = slice(64 * b, 64 * b + 64)
                        last = activate(lw[bs, at, c, :], M[2 * i + b][bs, c * T:(c + 1) * T], ACT.Sigmoid,
                                        bias=vecs[bs, V_AT[name] + c:V_AT[name] + c + 1])
            last.then_inc(l_sig, 1)
            act.wait_ge(l_gin, 1)
            activate(lw[:, 8], lw[:, 6], ACT.Sigmoid, scale=GELU_C).then_inc(l_gel, 1)

        def lru_decays():
            act.wait_ge(l_spn, 1)
            act.wait_ge(l_sig, 1)
            for c in range(LC):
                activate(lw[:, 3, c, :], lw[:, 1, c, :], ACT.Exp, scale=lamb[:, 6, c:c + 1])
            for c in range(LC):
                last = activate(lw[:, 4, c, :], lw[:, 1, c, :], ACT.Tanh, scale=lamb[:, 7, c:c + 1])
            last.then_inc(l_exp, 1)

        def lru_root():
            act.wait_ge(l_m2, 1)
            activate(lw[:, 4], lw[:, 6], ACT.Sqrt).then_inc(l_mult, 1)

        def lru_result():
            act.wait_ge(l_y, 1)
            activate(y2T_hi[:, 0:LC, :], lw[:, 7], ACT.Copy).then_inc(l_hi, 1)

        def moba_weights(at):
            if at in MB_AT and 2 <= MB_AT.index(at) < MB_H + 2:
                mb_weights(MB_AT.index(at) - 2)

        def moba_exps(at):
            if at in MB_AT and MB_AT.index(at) < MB_H:
                mb_exps(MB_AT.index(at))

        for t in range(TT):
            act.wait_ge(x_in[t], 16)
            square_sum = activate(tok[:, 0, :], x_tok[:, t, :], ACT.Square, scale=D ** -0.5,
                                  accum_out=squares[:, 0, 0, t:t + 1])
            if t == 0:
                link(square_sum)
        squares_done[0] += 1
        square_sum.then_inc(sq_act, 1)
        act.wait_ge(sq_act, 1)
        scale(0, x_tok, 1)
        act.wait_ge(vecs_ready, 1)
        act.wait_ge(landed[0], land_count(0))
        activate(whi[:, 0, 0:UK // 2, :], land[:, 0, 0:UK // 2, :], ACT.Copy).then_inc(half_hi, 1)
        turn_split("x", xT_hi, half=0)
        activate(whi[:, 0, UK // 2:, :], land[:, 0, UK // 2:, :], ACT.Copy).then_inc(hi_ready, 1)
        turn_split("x", xT_hi, half=1)
        split(1)

        for u in range(NU):
            n = UNITS[u][0]
            name = GROUPS[n][0]
            ends = u == LAST_U[name]
            if u == MB_TURN1[0] + 1:
                turn_split("moba1", y2T_hi, LC + 4, 1)
            if u == FIRST_U["out0"]:
                turn_split("merged", ysbT_hi, half=1)
            if u == FIRST_U["up0"]:
                turn_split("h2", xT_hi, half=1)
                square(1, x_tok, tok[:, 0, 0:NG], (1,))
            if u == B2:
                turn_split("h3", xT_hi, half=1)
                square(2, x_tok, relu[:, 0, 0:NG], (1,))
                square(3, tok, relu[:, 0, 0:NG], (1,))
            if u == FIRST_U["gu0"]:
                turn_split("h4", xT_hi, half=0)
                split(u + 1)
                act.wait_ge(x_part, TT * len(PIECES))
                square(5, x_tok, tok[:, 0, 0:NG], (0,))
                turn_split("h4", xT_hi, half=1)
                square(5, x_tok, tok[:, 0, 0:NG], (1,))
            moba_weights((u - 1, UNITS[u - 1][2]))
            if u != LAST_U["mix1"]:
                split(u + 2)
            moba_exps((u - 1, UNITS[u - 1][2]))
            if u == 0:
                act.wait_ge(small_in, 80)
                activate(w_if_hi[:].rearrange("p k i r h -> p (k i) r h"),
                         w_if[:].rearrange("p k (i h) -> p (k i) h", i=2).unsqueeze(2).to_broadcast(
                             [P, 2 * KD, 8, ML_H]), ACT.Copy).then_inc(if_hi, 1)
                act.wait_ge(tab_done, 1)
                activate(tab[:, :], M[1][0:MB_H, :], ACT.Copy).then_inc(tab_ready, 1)
            if u == LAST_U["psc1"]:
                turn_split("merged", ysbT_hi, half=0)
            if u == LAST_U["out1"]:
                act.wait_ge(read_dve, reads_before(G_AT["out0"], "dve"))
                square(1, x_tok, tok[:, 0, 0:NG], (0,))
                turn_split("h2", xT_hi, half=0)
            if u == LAST_U["down0"] + 1:
                act.wait_ge(xg_ready, 1)
                square(2, x_tok, relu[:, 0, 0:NG], (0,))
                square(3, tok, relu[:, 0, 0:NG], (0,))
            if u == LAST_U["down1"]:
                turn_split("h3", xT_hi, half=0)
            if u == U_IF + 2:
                act.wait_ge(rows_ready, 1)
                link(activate(e_row[:, :], f_row[:, :], ACT.Abs))
                link(activate(e_row[:, :], e_row[:, :], ACT.Exp, scale=-1.0))
                activate(e_row[:, :], e_row[:, :], ACT.Ln, bias=1.0).then_inc(e_ready, 1)
            if u == U_IF + 6:
                act.wait_ge(cols_turned, 1)
                act.wait_ge(c_ready, 1)
                activate(floor_col[:].rearrange("p t h -> p (t h)"), M[2][:, TT * ML_H:2 * TT * ML_H], ACT.Exp,
                         scale=-1.0).then_inc(floor_ready, 1)
            i = u - SB0
            if i == 0:
                act.wait_ge(tab_out, 16)
                activate(sums_r[:, :], con[:, K_TRI:K_TRI + 2 * P], ACT.Copy).then_inc(sums_ready, 1)
            if i % 2 == 0 and 2 <= i <= SB_H:
                sb_leading(i - 2)
                sb_leading(i - 1)
            if u - 1 in (LAST_U["mlo0"], LAST_U["mlo1"]):
                j = int(u - 1 > LAST_U["mlo0"])
                product_done(f"mlo{j}")
                activate(mlo[:, :, j * NG:(j + 1) * NG], acc[:, G_AT[f"mlo{j}"] % 2], ACT.Exp,
                         scale=-1.0).then_inc(read_act, 1)
            if i % 2 == 1 and 3 <= i <= SB_H + 1:
                sb_weights(i - 3)
                sb_weights(i - 2)
            if i % 2 == 1 and 1 <= i < SB_H:
                sb_logs(i - 1)
            i = u - ML0
            if 0 <= i < ML_H:
                ml_weights(i)
            if 2 <= i < ML_H + 2:
                ml_squares(i - 2)
            if ends and name[:3] in ("gsb", "gml", "gsc"):
                product_done(name)
                if name != "gsb0":
                    act.wait_ge(read_dve, reads_before(n - 1, "dve"))
                activate(gate[:], acc[:, n % 2], ACT.Sigmoid).then_inc(read_act, 1)
            if u == TURN_SB:
                turn_split("ysb", ysbT_hi)
            if u == TURN_ML:
                turn_split("yml", ymlT_hi)
            if ends and name[:3] == "scb":
                j = int(name[3])
                act.wait_ge(read_dve, reads_before(n, "dve"))
                activate(yscT_hi[:, 4 * j:4 * j + 4, :], conv[:], ACT.Copy).then_inc(ysc_hi, 1)
            if ends and name[:2] == "up":
                j = int(name[2:])
                act.wait_ge(read_dve, reads_before(n, "dve"))
                if j >= 2:
                    act.wait_ge(a_lo, j - 1)
                activate(relu2[:, j % 2, :], relu[:, j % 2, :], ACT.Square).then_inc(act_step, 1)
                steps[0] += 1
                act.wait_ge(act_step, steps[0])
                activate(aT_hi[:, 4 * j:4 * j + 4, :].rearrange("p a b -> p (a b)"), relu2[:, j % 2, :],
                         ACT.Copy).then_inc(a_hi, 1)
            if u == B2 - 6:
                lru_log()
            if u == B2 + 4:
                lru_sigmoids()
            if u == B2 + 5:
                gla_logs()
            if u == B2 + 6:
                lru_decays()
                gla_exps()
            if u == B2 + 9:
                gla_copies()
                lru_root()
            if u == B2 + 10:
                act.wait_ge(read_dve, reads_before(G_AT["gout"], "dve"))
                activate(gsig[:], gout[:], ACT.Sigmoid).then_inc(g_sig, 1)
            if u == B2 + 11:
                gla_squares()
            if u == B2 + 12:
                lru_result()
                turn_split("gla", y2T_hi, LC, 3)
            for k in range(1, UNITS[u][2]):
                moba_weights((u, k))
                moba_exps((u, k))
            if u == MB_TURN0[0]:
                turn_split("moba0", y2T_hi, LC + 2, 0)
            if ends and name == "mv":
                product_done(name)
                for t in range(TT):
                    last = activate(mbv[:, t, :], acc[:, n % 2, t, :], ACT.Copy, scale=factor3[:, t:t + 1])
                last.then_inc(read_act, 1)
            if ends and name[:3] == "mix" or ends and name[:2] == "dn":
                half = int(name[-1])
                first = 0 if name[:3] == "mix" else 4
                product_done(name)
                for t in reversed(range(TT)):
                    if t == 0:
                        act.wait_ge(gained, first + 2 * half + 1)
                    ins = activate(tok[:, t, 0:NG], acc[:, n % 2, t, :], ACT.Square, scale=D ** -0.5,
                                   accum_out=squares[:, 4 if first == 0 else 6, half, t:t + 1])
                    if t > 0:
                        ins.then_inc(bank_squared, 1)
                ins.then_inc(read_act, 1)
                act.wait_ge(read_act, reads_before(n, "act"))
            if ends and name[:2] == "gu":
                j = int(name[2:])
                act.wait_ge(gate2_ready, j + 1)
                activate(sig2[:, j % 2, :], act2[:, j % 2, :], ACT.Sigmoid).then_inc(sig2_ready, 1)
                act.wait_ge(act2_ready, j + 1)
                activate(a2T_hi[:, 2 * j:2 * j + 2, :].rearrange("p a b -> p (a b)"), act2[:, j % 2, :],
                         ACT.Copy).then_inc(act2_hi, 1)

    @block.vector
    def _(dve):
        v = nc.vector
        steps = [0]

        def link(ins):
            steps[0] += 1
            ins.then_inc(dve_step, 1)
            dve.wait_ge(dve_step, steps[0])

        def split(u):
            if u >= NU:
                return
            n, k, m = UNITS[u]
            w = width(n)
            dve.wait_ge(hi_ready, u + 1)
            dve.wait_ge(landed[u % LANDS], land_count(u))
            v.tensor_tensor(wlo[:, u % PARTS, 0:m, 0:w], land[:, u % LANDS, 0:m, 0:w],
                            whi[:, u % PARTS, 0:m, 0:w].bitcast(F32), ALU.subtract).then_inc(lo_ready, 1)

        def scale(j, src):
            dve.wait_ge(rstd_ready, j + 1)
            v.tensor_scalar(tok[:, 1, :], src[:, 1, :], rstd[:, j, 1:2], None, ALU.mult).then_inc(norm_dve, 1)

        def make_diag(i, stage):
            if stage == 3:
                dve.wait_ge(factor_ready, 1)
            else:
                dve.wait_ge(rstd_ready, stage + 1)
            f = factor3 if stage == 3 else rstd[:, stage, :]
            for t in range(TT):
                last = v.tensor_scalar(diag[:, t, :], ident, f[:, t:t + 1], None, ALU.mult)
            last.then_inc(diag_ready, 1)

        def take_row(i):
            dve.wait_ge(row_made, i + 1)
            v.tensor_scalar(row[:, :], M[0][:, 0:T], -1.0, None, ALU.mult).then_inc(row_ready, 1)

        def along(k):
            return row[:, :].unsqueeze(1).to_broadcast([P, k, T])

        def turn_split(stage, hi, lo, k_to=0, bank=0, half=None):
            _, kk, gain = [s for s in TURNS if s[0] == stage][0]
            for b in range(kk // 2) if half is None else (2 * half, 2 * half + 1):
                dve.wait_ge(turn_hi, TURN_AT[stage] + b + 1)
                ks = slice(k_to + 2 * b, k_to + 2 * b + 2)
                if gain is None:
                    last = v.tensor_tensor(lo[:, ks, :], M[bank + b][:, :].rearrange("p (k t) -> p k t", k=2),
                                           hi[:, ks, :].bitcast(F32), ALU.subtract)
                else:
                    for i in range(2):
                        g, k = V_AT[gain] + 2 * b + i, k_to + 2 * b + i
                        last = v.scalar_tensor_tensor(out=lo[:, k, :], in0=M[bank + b][:, i * T:(i + 1) * T],
                                                      scalar=vecs[:, g:g + 1], in1=hi[:, k, :].bitcast(F32),
                                                      op0=ALU.mult, op1=ALU.subtract)
                last.then_inc(turn_lo, 1)

        def product_done(name):
            dve.wait_ge(units_done, LAST_U[name] + 1)

        def sb_softplus(h):
            dve.wait_ge(sb_log, h + 1)
            w = sbw[:, h % 2]
            v.scalar_tensor_tensor(out=w, in0=M[h % 4][:, 0:3 * P], scalar=0.0, in1=w, op0=ALU.max,
                                   op1=ALU.add).then_inc(sb_t, 1)

        def sb_rest(h):
            dve.wait_ge(sb_hi, h + 1)
            v.tensor_tensor(sbw_lo[:, h % 2], sbw[:, h % 2], sbw_hi[:, h % 2].bitcast(F32),
                            ALU.subtract).then_inc(sb_lo, 1)

        def sb_result(h):
            dve.wait_ge(sb_av, h + 1)
            v.tensor_copy(tok[:, :, h * SB_D:(h + 1) * SB_D],
                          M[h % 4][:, 3 * P:].rearrange("p (t d) -> p t d", t=TT)).then_inc(sb_y, 1)

        def ml_products(h):
            dve.wait_ge(ml_wm, h + 1)
            w = sba[:, h % 2]
            v.tensor_tensor(w, M[2 * (h % 2)][:, 0:3 * P], w, ALU.mult).then_inc(ml_p, 1)

        def ml_result(h):
            dve.wait_ge(ml_num, h + 1)
            if h == 0:
                dve.wait_ge(floor_ready, 1)
            o, b = M[2 * (h % 2)], M[2 * (h % 2) + 1]
            link(v.tensor_copy(ml_den[:, 0], b[:, T:T + TT]))
            link(v.scalar_tensor_tensor(out=ml_den[:, 1], in0=ml_den[:, 0], scalar=-1.0, in1=ml_den[:, 0],
                                        op0=ALU.mult, op1=ALU.max))
            link(v.tensor_tensor(ml_den[:, 2], ml_den[:, 1], floor_col[:, :, h], ALU.max))
            link(v.reciprocal(ml_den[:, 3], ml_den[:, 2]))
            for t in range(TT):
                y = mlo[:, t, h * ML_D:(h + 1) * ML_D]
                last = v.scalar_tensor_tensor(out=y, in0=o[:, t * ML_D:(t + 1) * ML_D],
                                              scalar=ml_den[:, 3, t:t + 1], in1=y, op0=ALU.mult, op1=ALU.mult)
            last.then_inc(ml_y, 1)

        def output_gate(j, t):
            dve.wait_ge(read_act, reads_before(G_AT[f"mlo{j}"], "act"))
            o = mlo[:, t, j * NG:(j + 1) * NG]
            link(v.tensor_scalar(o, o, 1.0, None, ALU.add))
            link(v.reciprocal(o, o))

        def conv_taps(j):
            for tap in reversed(range(CONV_K)):
                for i in range(4):
                    k = 4 * j + i
                    w = vecs[:, V_AT["conv_w"] + tap * KD + k:V_AT["conv_w"] + tap * KD + k + 1]
                    z = zT[:, k, tap:tap + T]
                    if tap == CONV_K - 1:
                        last = v.tensor_scalar(conv[:, i, :], z, w, None, ALU.mult)
                    else:
                        last = v.scalar_tensor_tensor(out=conv[:, i, :], in0=z, scalar=w, in1=conv[:, i, :],
                                                      op0=ALU.mult, op1=ALU.add)
                link(last)

        def mb_logits(h):
            dve.wait_ge(mb_s, h + 1)
            if h == 0:
                dve.wait_ge(bias_in, 32)
            if h >= 3:
                dve.wait_ge(mb_pt, h - 2)
            s = mbs[:, h % 3]
            link(v.tensor_tensor(s, M[h % 2][:, 0:3 * P], bias[:, h, :], ALU.add))
            v.tensor_reduce(mb_max[:, h, 0:1], s[:, 0:P], AX.X, ALU.max)
            link(v.tensor_reduce(mb_max[:, h, 1:2], s[:, P:3 * P], AX.X, ALU.max))
            v.tensor_scalar(mb_max[:, h, :], mb_max[:, h, :], -1.0, None, ALU.mult).then_inc(mb_max_ready, 1)

        def mb_result(h):
            dve.wait_ge(mb_av, h + 1)
            link(v.reciprocal(mb_inv[:, h, :], mb_sum[:, h, :]))
            for t in range(TT):
                last = v.tensor_scalar(tok[:, t, 2 * P + h * MB_D:2 * P + (h + 1) * MB_D],
                                       M[3][:, t * MB_D:(t + 1) * MB_D], mb_inv[:, h, t:t + 1], None, ALU.mult)
            last.then_inc(mb_y, 1)

        def gla_rank():
            dve.wait_ge(glr_turned, 1)
            v.tensor_copy(glrT[:, :], M[0][0:GLA_RANK, 0:T]).then_inc(glr_ready, 1)

        def gla_cumulative():
            b = vecs[:, V_AT["gla_gate_b_2"]:V_AT["gla_gate_b_2"] + 1]
            dve.wait_ge(g_ln, 1)
            link(v.tensor_scalar(gla[:, 1], M[1][:, 0:T], b, 0.0, ALU.add, ALU.min))
            link(v.tensor_tensor(gla[:, 1], gla[:, 1], gla[:, 0], ALU.subtract))
            link(v.tensor_scalar(gla[:, 2], gla[:, 1], 1.0 / GLA_TAU, None, ALU.mult))
            dve.wait_ge(g_sets, 1)
            link(v.tensor_tensor_scan(gla[:, 1], gnew, gla[:, 2], 0.0, ALU.mult, ALU.add))
            cum = gla[:, 1].rearrange("p (n c) -> p n c", c=GLA_CHUNK)
            last = cum[:, :, GLA_CHUNK - 1:GLA_CHUNK].to_broadcast([P, T // GLA_CHUNK, GLA_CHUNK])
            v.tensor_tensor(gla[:, 2].rearrange("p (n c) -> p n c", c=GLA_CHUNK), last, cum,
                            ALU.subtract).then_inc(g_cum, 1)

        def gla_scaled():
            dve.wait_ge(g_exp, 4)
            dve.wait_ge(read_dve, reads_before(G_AT["gqk"], "dve"))
            v.scalar_tensor_tensor(out=qd, in0=gqk[:, 0, :], scalar=float(GLA_DK) ** -0.5, in1=gla[:, 3],
                                   op0=ALU.mult, op1=ALU.mult).then_inc(g_qk, 1)
            v.tensor_tensor(kd, gqk[:, 1, :], gla[:, 4], ALU.mult).then_inc(g_qk, 1)
            v.tensor_tensor(kl, gqk[:, 1, :], gla[:, 5], ALU.mult).then_inc(g_qk, 1)

        def gla_keys():
            dve.wait_ge(kl_turned, 1)
            v.tensor_copy(kl_tok[:].rearrange("p t c -> p (t c)"), M[3][:, 0:T]).then_inc(kl_ready, 1)

        def gla_states():
            dve.wait_ge(g_kv, 1)
            for n in range(3):
                for h in range(GLA_H):
                    ps = slice(h * GLA_DK, (h + 1) * GLA_DK)
                    vs = slice(h * GLA_DV, (h + 1) * GLA_DV)
                    last = v.scalar_tensor_tensor(out=gstate[ps, n + 1, vs], in0=gstate[ps, n, vs],
                                                  scalar=gdec[ps, n:n + 1], in1=M[n][ps, vs], op0=ALU.mult,
                                                  op1=ALU.add)
                if n < 2:
                    link(last)
                else:
                    last.then_inc(g_state, 1)

        def gla_result():
            dve.wait_ge(g_sig, 1)
            link(v.tensor_tensor(gsig[:], gsig[:], gout[:], ALU.mult))
            dve.wait_ge(g_osq, 1)
            v.tensor_reduce(gss[:, 0, :], gsq, AX.X, ALU.add).then_inc(g_oss, 1)
            dve.wait_ge(g_rs, 1)
            link(v.tensor_tensor(gsq, M[3][:, :].rearrange("p (a b) -> p a b", b=GLA_DV),
                                 gss[:, 2, :].unsqueeze(2).to_broadcast([P, TT * GLA_H, GLA_DV]), ALU.mult))
            v.tensor_tensor(tok[:, :, 0:GD], gsq.rearrange("p (t h) b -> p t (h b)", t=TT), gsig[:],
                            ALU.mult).then_inc(g_y, 1)

        def lru_decay():
            dve.wait_ge(l_lam, 1)
            e, w, w2, s = lamb[:, 1], lamb[:, 2], lamb[:, 3], lamb[:, 4]
            link(v.tensor_scalar(w, e, 2.0, None, ALU.add))
            link(v.reciprocal(w2, w))
            link(v.tensor_tensor(w, e, w2, ALU.mult))
            link(v.tensor_tensor(w2, w, w, ALU.mult))
            link(v.tensor_scalar(s, w2, 1.0 / 17, 1.0 / 15, ALU.mult, ALU.add))
            for odd in (13, 11, 9, 7, 5, 3, 1):
                link(v.tensor_tensor(s, s, w2, ALU.mult))
                link(v.tensor_scalar(s, s, 1.0 / odd, None, ALU.add))
            link(v.tensor_tensor(s, s, w, ALU.mult))
            lam = vecs[:, V_AT["lru_lambda_2"]:V_AT["lru_lambda_2"] + LC]
            link(v.tensor_scalar(lamb[:, 5], lam, -1.0, 0.0, ALU.mult, ALU.max))
            link(v.scalar_tensor_tensor(out=s, in0=s, scalar=2.0, in1=lamb[:, 5], op0=ALU.mult, op1=ALU.add))
            v.tensor_scalar(lamb[:, 6], s, -LRU_C, None, ALU.mult)
            v.tensor_scalar(lamb[:, 7], s, LRU_C, None, ALU.mult).then_inc(l_spn, 1)

        def lru_conv():
            dve.wait_ge(g_sets, 1)
            dve.wait_ge(read_dve, reads_before(G_AT["lru"], "dve"))
            for tap in reversed(range(LRU_TAPS)):
                for c in range(LC):
                    r = V_AT["lru_conv_w_2"] + tap * LC + c
                    w, x = vecs[:, r:r + 1], lruT[:, c, tap:tap + T]
                    if tap == LRU_TAPS - 1:
                        last = v.tensor_scalar(lw[:, 0, c, :], x, w, None, ALU.mult)
                    else:
                        last = v.scalar_tensor_tensor(out=lw[:, 0, c, :], in0=x, scalar=w, in1=lw[:, 0, c, :],
                                                      op0=ALU.mult, op1=ALU.add)
                link(last)
            for c in range(LC):
                r = V_AT["lru_conv_b_2"] + c
                last = v.tensor_scalar(lw[:, 0, c, :], lw[:, 0, c, :], vecs[:, r:r + 1], None, ALU.add)
            last.then_inc(l_conv, 1)

        def lru_gate_arg():
            g = lruT[:, LC:2 * LC, LRU_TAPS - 1:]
            link(v.tensor_tensor(lw[:, 6], g, g, ALU.mult))
            link(v.tensor_scalar(lw[:, 6], lw[:, 6], 0.044715, 1.0, ALU.mult, ALU.add))
            v.tensor_tensor(lw[:, 6], lw[:, 6], g, ALU.mult).then_inc(l_gin, 1)

        def lru_scan():
            dve.wait_ge(l_exp, 1)
            a, p, q, m2 = lw[:, 3], lw[:, 4], lw[:, 5], lw[:, 6]
            link(v.tensor_tensor(q, a, a, ALU.mult))
            link(v.scalar_tensor_tensor(out=m2, in0=q, scalar=1.0, in1=p, op0=ALU.add, op1=ALU.mult))
            v.tensor_scalar(m2, m2, ROOT_FLOOR, None, ALU.max).then_inc(l_m2, 1)

        def lru_result():
            link(v.tensor_tensor(lw[:, 7], lw[:, 2], lw[:, 0], ALU.mult))
            link(v.tensor_tensor(lw[:, 8], lw[:, 8], lruT[:, LC:2 * LC, LRU_TAPS - 1:], ALU.mult))
            dve.wait_ge(l_mult, 1)
            link(v.memset(lw[:, 4, :, 0:1], 1.0))
            link(v.tensor_tensor(lw[:, 5], lw[:, 7], lw[:, 4], ALU.mult))
            for c in range(LC):
                last = v.tensor_tensor_scan(lw[:, 6, c, :], lw[:, 3, c, :], lw[:, 5, c, :], 0.0, ALU.mult, ALU.add)
            link(last)
            v.tensor_tensor(lw[:, 7], lw[:, 6], lw[:, 8], ALU.mult).then_inc(l_y, 1)

        def lru_rest():
            dve.wait_ge(l_hi, 1)
            v.tensor_tensor(y2T_lo[:, 0:LC, :], lw[:, 7], y2T_hi[:, 0:LC, :].bitcast(F32),
                            ALU.subtract).then_inc(l_lo, 1)

        def moba_steps(of):
            for at in of:
                if at in MB_AT:
                    i = MB_AT.index(at)
                    if 3 <= i < MB_H + 3:
                        mb_result(i - 3)
                    if 0 <= i < MB_H:
                        mb_logits(i)

        def relu_rest(name):
            j = int(name[2:])
            dve.wait_ge(a_hi, j + 1)
            v.tensor_tensor(aT_lo[:, 4 * j:4 * j + 4, :].rearrange("p a b -> p (a b)"), relu2[:, j % 2, :],
                            aT_hi[:, 4 * j:4 * j + 4, :].rearrange("p a b -> p (a b)").bitcast(F32),
                            ALU.subtract).then_inc(a_lo, 1)

        def act2_rest(name):
            j = int(name[2:])
            dve.wait_ge(act2_hi, j + 1)
            v.tensor_tensor(a2T_lo[:, 2 * j:2 * j + 2, :].rearrange("p a b -> p (a b)"), act2[:, j % 2, :],
                            a2T_hi[:, 2 * j:2 * j + 2, :].rearrange("p a b -> p (a b)").bitcast(F32),
                            ALU.subtract).then_inc(act2_lo, 1)

        def residual(j):
            dve.wait_ge(rstd_ready, j + 1)
            dve.wait_ge(gained, 4 if j == 4 else 8)
            for c0, c1 in PIECES:
                for t in range(TT):
                    v.scalar_tensor_tensor(out=x_tok[:, t, c0:c1], in0=mixed[:, t, c0:c1], scalar=rstd[:, j, t:t + 1],
                                           in1=x_tok[:, t, c0:c1], op0=ALU.mult, op1=ALU.add).then_inc(x_part, 1)

        dve.wait_ge(x_in[1], 16)
        link(v.memset(one_row[:, :], 1.0))
        dve.wait_ge(vecs_turned, 1)
        v.tensor_copy(vecs[:, :], M[0][:, 0:V_ROWS]).then_inc(vecs_ready, 1)
        scale(0, x_tok)
        dve.wait_ge(half_hi, 1)
        dve.wait_ge(landed[0], land_count(0))
        v.tensor_tensor(wlo[:, 0, 0:UK // 2, :], land[:, 0, 0:UK // 2, :], whi[:, 0, 0:UK // 2, :].bitcast(F32),
                        ALU.subtract).then_inc(half_lo, 1)
        dve.wait_ge(vecs_ready, 1)
        turn_split("x", xT_hi, xT_lo, half=0)
        dve.wait_ge(hi_ready, 1)
        v.tensor_tensor(wlo[:, 0, UK // 2:, :], land[:, 0, UK // 2:, :], whi[:, 0, UK // 2:, :].bitcast(F32),
                        ALU.subtract).then_inc(lo_ready, 1)
        turn_split("x", xT_hi, xT_lo, half=1)
        split(1)

        for u in range(NU):
            n = UNITS[u][0]
            name = GROUPS[n][0]
            ends = u == LAST_U[name]
            flat = acc[:, n % 2].rearrange("p a b -> p (a b)")
            moba_steps([(u - 1, UNITS[u - 1][2])])
            if u == MB_TURN1[0] + 1:
                turn_split("moba1", y2T_hi, y2T_lo, LC + 4, 1)
            if u == FIRST_U["out0"]:
                turn_split("merged", ysbT_hi, ysbT_lo, half=1)
            if u == FIRST_U["up0"]:
                turn_split("h2", xT_hi, xT_lo, half=1)
                make_diag(0, 1)
            if u == B2:
                turn_split("h3", xT_hi, xT_lo, half=1)
                make_diag(1, 3)
            if u == FIRST_U["gu0"]:
                turn_split("h4", xT_hi, xT_lo, half=0)
                split(u + 1)
                turn_split("h4", xT_hi, xT_lo, half=1)
                make_diag(2, 5)
            if u - SB0 in range(4, SB_H + 3, 2):
                sb_result(u - SB0 - 4)
                sb_result(u - SB0 - 3)
            if u == B2 + 2:
                lru_conv()
            if u == B2 + 8:
                gla_scaled()
            if u == B2 + 10:
                gla_keys()
            if u != LAST_U["mix1"]:
                split(u + 2)
            if u == 0:
                dve.wait_ge(if_hi, 1)
                v.tensor_tensor(w_if_lo[:].rearrange("p k i r h -> p (k i) r h"),
                                w_if[:].rearrange("p k (i h) -> p (k i) h", i=2).unsqueeze(2).to_broadcast(
                                    [P, 2 * KD, 8, ML_H]),
                                w_if_hi[:].rearrange("p k i r h -> p (k i) r h").bitcast(F32),
                                ALU.subtract).then_inc(if_lo, 1)
            if u == LAST_U["psc1"]:
                turn_split("merged", ysbT_hi, ysbT_lo, half=0)
            if u == LAST_U["out1"]:
                turn_split("h2", xT_hi, xT_lo, half=0)
            if u == LAST_U["down1"]:
                turn_split("h3", xT_hi, xT_lo, half=0)
            if u == FIRST_U["up0"] + 1:
                take_row(0)
            if u == B2 + 1:
                take_row(1)
            if u == FIRST_U["gu0"] + 1:
                take_row(2)
            if u - 1 in [LAST_U[f"up{i}"] for i in range(D_FF // NG)]:
                relu_rest(GROUPS[UNITS[u - 1][0]][0])
            if u - 1 in [LAST_U[f"gu{i}"] for i in range(D_FF2 // GU)]:
                act2_rest(GROUPS[UNITS[u - 1][0]][0])
            if u == U_IF + 1:
                dve.wait_ge(if_done, 1)
                v.tensor_copy(i_row[:, :], M[3][0:ML_H, 0:T])
                link(v.tensor_copy(f_row[:, :], M[3][8 * ML_H:9 * ML_H, 0:T]))
                v.tensor_scalar(i_row[:, :], i_row[:, :], b_if[:, 0:1], None, ALU.add)
                v.tensor_scalar(f_row[:, :], f_row[:, :], b_if[:, 1:2], None, ALU.add).then_inc(rows_ready, 1)
            if u == U_IF + 4:
                dve.wait_ge(e_ready, 1)
                link(v.scalar_tensor_tensor(out=f_row[:, :], in0=f_row[:, :], scalar=0.0, in1=e_row[:, :],
                                            op0=ALU.min, op1=ALU.subtract))
                link(v.tensor_tensor_scan(bm_row[:, :], one_row[:, :], f_row[:, :], 0.0, ALU.mult, ALU.add))
                link(v.tensor_tensor(i_row[:, :], i_row[:, :], bm_row[:, :], ALU.subtract))
                link(v.tensor_tensor_scan(negm_row[:, :], i_row[:, :], i_row[:, :], 0.0, ALU.max, ALU.max))
                link(v.tensor_tensor(bm_row[:, :], bm_row[:, :], negm_row[:, :], ALU.add))
                v.tensor_scalar(negm_row[:, :], negm_row[:, :], -1.0, None, ALU.mult).then_inc(scans_ready, 1)
            if u == U_IF + 6:
                dve.wait_ge(cols_turned, 1)
                v.tensor_copy(c_col[:].rearrange("p t h -> p (t h)"), M[2][:, 0:TT * ML_H]).then_inc(c_ready, 1)
            i = u - SB0
            if i % 2 == 0 and 2 <= i <= SB_H:
                sb_rest(i - 2)
                sb_rest(i - 1)
            if i % 2 == 1 and 1 <= i < SB_H:
                sb_softplus(i - 1)
                sb_softplus(i)
            i = u - ML0
            if 0 <= i < ML_H:
                ml_products(i)
            if 1 <= i <= ML_H:
                ml_result(i - 1)
            if ends and name[:3] in ("sbq", "sbk", "mlq", "mlk"):
                j = int(name[3])
                to = {"sbq": sbqT, "sbk": sbkT, "mlq": mlqT, "mlk": mlkT}[name[:3]]
                by = {"sbq": SB_D ** -0.5, "mlk": ML_D ** -0.5}.get(name[:3], 1.0)
                product_done(name)
                v.tensor_scalar(to[:, 4 * j:4 * j + 4, :].rearrange("p a b -> p (a b)"), flat, by, None,
                                ALU.mult).then_inc(read_dve, 1)
            if ends and name[:3] in ("sbv", "mlv"):
                j = int(name[3])
                product_done(name)
                v.tensor_copy((sbv if name[0] == "s" else mlv)[:, :, j * NG:(j + 1) * NG],
                              acc[:, n % 2]).then_inc(read_dve, 1)
            if 0 <= u - GATE0 < 2 * TT:
                output_gate((u - GATE0) // TT, (u - GATE0) % TT)
            if ends and name[:3] == "scc":
                j = int(name[3])
                product_done(name)
                v.tensor_copy(cT[:, 4 * j:4 * j + 4, :].rearrange("p a b -> p (a b)"), flat).then_inc(read_dve, 1)
            if ends and name[:3] == "scu":
                j = int(name[3])
                product_done(name)
                if j == 0:
                    link(v.memset(zT[:, :, 0:CONV_K - 1], 0.0))
                v.tensor_tensor(zT[:, 4 * j:4 * j + 4, CONV_K - 1:], flat.rearrange("p (a b) -> p a b", b=T),
                                cT[:, 4 * j:4 * j + 4, :], ALU.mult).then_inc(read_dve, 1)
                dve.wait_ge(read_dve, reads_before(n, "dve"))
                if j == 0:
                    conv_taps(0)
            if ends and name[:3] == "scb":
                j = int(name[3])
                product_done(name)
                v.tensor_tensor(conv[:].rearrange("p a b -> p (a b)"), flat,
                                conv[:].rearrange("p a b -> p (a b)"), ALU.mult).then_inc(read_dve, 1)
                dve.wait_ge(read_dve, reads_before(n, "dve"))
                dve.wait_ge(ysc_hi, j + 1)
                v.tensor_tensor(yscT_lo[:, 4 * j:4 * j + 4, :], conv[:], yscT_hi[:, 4 * j:4 * j + 4, :].bitcast(F32),
                                ALU.subtract).then_inc(ysc_lo, 1)
                if j == 0:
                    dve.wait_ge(ysc_lo, 1)
                    conv_taps(1)
            if u == TURN_SB:
                turn_split("ysb", ysbT_hi, ysbT_lo)
                dve.wait_ge(ml_rs, 1)
                y = mlo[:].rearrange("p t (h d) -> p (t h) d", d=ML_D)
                v.tensor_tensor(y, y, ml_rstd[:].rearrange("p t h -> p (t h)").unsqueeze(2).to_broadcast(
                    [P, TT * ML_H, ML_D]), ALU.mult).then_inc(yml_ready, 1)
            if u == TURN_ML:
                turn_split("yml", ymlT_hi, ymlT_lo)
            if ends and name[:3] in ("psb", "pml", "psc"):
                j = int(name[3])
                product_done(name)
                dve.wait_ge(read_act, reads_before(n - 1, "act"))
                m = tok[:, :, j * NG:(j + 1) * NG]
                if name[:3] == "psb":
                    v.tensor_tensor(m, acc[:, n % 2], gate[:], ALU.mult).then_inc(read_dve, 1)
                else:
                    link(v.tensor_tensor(gated[:], acc[:, n % 2], gate[:], ALU.mult))
                    v.tensor_tensor(m, m, gated[:], ALU.add).then_inc(read_dve, 1)
            if ends and name[:3] == "out" or ends and name[:4] == "down":
                j = int(name[-1])
                product_done(name)
                x = x_tok[:, :, j * NG:(j + 1) * NG]
                v.tensor_tensor(x, acc[:, n % 2], x, ALU.add).then_inc(read_dve, 1)
            if ends and name[:4] == "down":
                dve.wait_ge(read_dve, reads_before(n, "dve"))
                dve.wait_ge(gain_in, 16)
                cols = slice(j * NG, (j + 1) * NG)
                v.tensor_tensor(tok[:, :, cols], x_tok[:, :, cols],
                                gain_a[:, cols].unsqueeze(1).to_broadcast([P, TT, NG]), ALU.mult).then_inc(xg_ready, 1)
            if ends and name[:2] == "up":
                j = int(name[2:])
                product_done(name)
                dve.wait_ge(row_ready, 1)
                if j >= 2:
                    dve.wait_ge(a_hi, j - 1)
                v.scalar_tensor_tensor(out=relu[:, j % 2, :].rearrange("p (a b) -> p a b", b=T),
                                       in0=flat.rearrange("p (a b) -> p a b", b=T), scalar=0.0,
                                       in1=along(4), op0=ALU.max, op1=ALU.mult).then_inc(read_dve, 1)
            if u == B2 - 5:
                lru_decay()
            if u == B2 + 4:
                lru_gate_arg()
                gla_rank()
            if u == B2 + 5:
                gla_cumulative()
            if u == B2 + 6:
                for t in range(TT):
                    ins = v.tensor_scalar(x_tok[:, t, :], tok[:, t, :], rstd[:, 2, t:t + 1], None, ALU.mult)
                link(ins)
            if u == B2 + 8:
                lru_scan()
            if u == B2 + 10:
                gla_states()
                lru_result()
            if u == B2 + 11:
                gla_result()
            if u == B2 + 12:
                lru_rest()
                turn_split("gla", y2T_hi, y2T_lo, LC, 3)
            moba_steps([(u, k) for k in range(1, UNITS[u][2])])
            if u == MB_TURN0[0]:
                turn_split("moba0", y2T_hi, y2T_lo, LC + 2, 0)
            if ends and name in ("mqk0", "mqk1", "gqk", "gv", "gout", "lru"):
                product_done(name)
                if name == "lru":
                    dve.wait_ge(row_ready, 2)
                if name[:3] == "mqk":
                    qk = mbqk[:, int(name[3])]
                    v.scalar_tensor_tensor(out=qk[:, 0:2], in0=acc[:, n % 2, 0, :].rearrange("p (a b) -> p a b", b=T),
                                           scalar=MB_D ** -0.5, in1=along(2), op0=ALU.mult, op1=ALU.mult)
                    last = v.tensor_tensor(qk[:, 2:4], acc[:, n % 2, 1, :].rearrange("p (a b) -> p a b", b=T),
                                           along(2), ALU.mult)
                elif name == "gqk":
                    last = v.tensor_tensor(gqk[:], acc[:, n % 2, 0, :].rearrange("p (a b) -> p a b", b=T), along(2),
                                           ALU.mult)
                elif name == "lru":
                    last = v.tensor_tensor(lruT[:, :, LRU_TAPS - 1:], flat.rearrange("p (a b) -> p a b", b=T),
                                           along(4), ALU.mult)
                else:
                    to = {"gv": gv, "gout": gout}[name]
                    for t in range(TT):
                        last = v.tensor_scalar(to[:, t, :], acc[:, n % 2, t, 0:width(n)], factor3[:, t:t + 1], None,
                                               ALU.mult)
                last.then_inc(read_dve, 1)
            if ends and name[:3] == "mix" or ends and name[:2] == "dn":
                j = int(name[-1])
                product_done(name)
                dve.wait_ge(gain_in, 32 if name[:3] == "mix" else 48)
                cols = slice(j * NG, (j + 1) * NG)
                for t in range(TT):
                    if t == 1:
                        dve.wait_ge(bank_squared, j + (1 if name[:3] == "mix" else 3))
                    v.tensor_tensor(mixed[:, t, cols], acc[:, n % 2, t, :], gain_b[:, cols],
                                    ALU.mult).then_inc(gained, 1)
            if ends and name == "mix1":
                residual(4)
            if ends and name == "dn1":
                residual(6)
            if ends and name[:2] == "gu":
                j = int(name[2:])
                product_done(name)
                if j == 0:
                    dve.wait_ge(row_ready, 3)
                if j >= 2:
                    dve.wait_ge(act2_lo, j - 1)
                a = act2[:, j % 2, :]
                v.tensor_tensor(a.rearrange("p (a b) -> p a b", b=T), acc[:, n % 2, 0, :].rearrange(
                    "p (a b) -> p a b", b=T), along(2), ALU.mult).then_inc(gate2_ready, 1)
                v.tensor_tensor(up2[:, j % 2, :].rearrange("p (a b) -> p a b", b=T), acc[:, n % 2, 1, :].rearrange(
                    "p (a b) -> p a b", b=T), along(2), ALU.mult).then_inc(read_dve, 1)
                dve.wait_ge(sig2_ready, j + 1)
                dve.wait_ge(read_dve, reads_before(n, "dve"))
                link(v.tensor_tensor(a, a, sig2[:, j % 2, :], ALU.mult))
                v.tensor_tensor(a, a, up2[:, j % 2, :], ALU.mult).then_inc(act2_ready, 1)

    @block.gpsimd
    def _(pool):
        g = nc.gpsimd
        steps = [0]

        def link(ins):
            steps[0] += 1
            ins.then_inc(pool_step, 1)
            pool.wait_ge(pool_step, steps[0])

        signalled = {}

        def signal(ins, to):
            signalled[to] = signalled.get(to, 0) + 1
            ins.then_inc(to, 1)
            pool.wait_ge(to, signalled[to])

        def inverse_root(j, squares_done):
            for half, (seen, count) in enumerate(squares_done):
                pool.wait_ge(seen, count)
                if half == 0:
                    link(g.tensor_scalar(mean_sq[:, j, :], squares[:, j, 0, :], EPS, None, ALU.add))
                else:
                    link(g.tensor_tensor(mean_sq[:, j, :], mean_sq[:, j, :], squares[:, j, half, :], ALU.add))
            signal(g.tensor_tensor(rstd[:, j, :], mean_sq[:, j, :], mhalf[:].to_broadcast([P, TT]),
                                   ALU.pow), rstd_ready)

        def keep(view, above):
            w = view.rearrange("p (a c) -> p a c", c=P)[:, 0:3:2, :]
            return g.affine_select(out=w, in_=w, pattern=[[0, 2], [1, P]], compare_op=above, fill=0.0, base=0,
                                   channel_multiplier=-1)

        link(g.memset(mhalf[:], -0.5))
        signal(g.memset(rel33[BUCKETS:BUCKETS + 1, :], 1.0), pool_set)
        inverse_root(0, [(sq_act, 1)])
        for i in range(0, SB_H + 2, 2):
            if i >= 2:
                for h in (i - 2, i - 1):
                    pool.wait_ge(sb_a, h + 1)
                    signal(keep(sba[:, h % 2], ALU.is_gt), sb_am)
            if i < SB_H:
                for h in (i, i + 1):
                    pool.wait_ge(sb_t, h + 1)
                    signal(keep(sbw[:, h % 2], ALU.is_gt), sb_tm)
        for h in range(ML_H):
            pool.wait_ge(ml_w, h + 1)
            signal(keep(sba[:, h % 2], ALU.is_ge), ml_wm)
        pool.wait_ge(ml_ss, ML_H)
        link(g.tensor_scalar(ml_ms[:], ml_sq[:], 1.0 / ML_D, EPS, ALU.mult, ALU.add))
        signal(g.tensor_tensor(ml_rstd[:].rearrange("p t h -> p (t h)"), ml_ms[:].rearrange("p t h -> p (t h)"),
                               mhalf[:].to_broadcast([P, TT * ML_H]), ALU.pow), ml_rs)
        inverse_root(1, [(sq_act, 2), (sq_act, 3)])
        inverse_root(2, [(sq_act, 4), (sq_act, 6)])
        pool.wait_ge(sq_act, 7)
        ms = mean_sq[:, 3, :]
        link(g.tensor_tensor(ms, squares[:, 3, 0, :], squares[:, 3, 1, :], ALU.add))
        for _ in range(2):
            link(g.tensor_tensor(ms, ms, rstd[:, 2, :], ALU.mult))
        link(g.tensor_scalar(ms, ms, EPS, None, ALU.add))
        signal(g.tensor_tensor(rstd[:, 3, :], ms, mhalf[:].to_broadcast([P, TT]), ALU.pow), rstd_ready)
        signal(g.tensor_tensor(factor3[:, :], rstd[:, 2, :], rstd[:, 3, :], ALU.mult), factor_ready)
        link(g.memset(gnew, 1.0))
        link(g.memset(gnew.rearrange("p (n c) -> p n c", c=GLA_CHUNK)[:, :, 0:1], 0.0))
        link(g.memset(lruT[:, :, 0:LRU_TAPS - 1], 0.0))
        signal(g.memset(gstate[:], 0.0), g_sets)
        pool.wait_ge(g_atc, 1)
        link(g.affine_select(out=gattn[:], in_=gattn[:], pattern=[[0, GLA_H], [0, TT], [1, P]],
                             compare_op=ALU.is_ge, fill=0.0, base=0, channel_multiplier=-1))
        signal(g.memset(gattn[0:GLA_CHUNK, :, :, GLA_CHUNK:P], 0.0), g_atm)
        pool.wait_ge(g_oss, 1)
        link(g.tensor_scalar(gss[:, 1, :], gss[:, 0, :], 1.0 / GLA_DV, EPS, ALU.mult, ALU.add))
        signal(g.tensor_tensor(gss[:, 2, :], gss[:, 1, :], mhalf[:].to_broadcast([P, TT * GLA_H]),
                               ALU.pow), g_rs)
        inverse_root(4, [(read_act, reads_before(G_AT["mix0"], "act")), (read_act, reads_before(G_AT["mix1"], "act"))])
        inverse_root(5, [(sq_act, 8), (sq_act, 9)])
        inverse_root(6, [(read_act, reads_before(G_AT["dn0"], "act")), (read_act, reads_before(G_AT["dn1"], "act"))])

    ctx.close()


INPUTS = ["x", "norm_mix_g", "w_in", "b_if", "ml_norm_g", "conv_w", "w_ml_proj", "w_sc_proj", "w_sb_proj",
          "w_out", "norm_mlp_g", "w_up", "w_down", "norm_final_g", "pre_mix_norm_2", "post_mix_norm_2",
          "pre_ffn_norm_2", "post_ffn_norm_2", "w_in_2", "w_out_2", "lru_conv_w_2", "lru_conv_b_2",
          "lru_wa_2", "lru_ba_2", "lru_wx_2", "lru_bx_2", "lru_lambda_2", "gla_gate_w2_2", "gla_gate_b_2",
          "gla_norm_2", "rel_bias_2", "w_ffn_gate_2", "w_ffn_up_2", "w_ffn_down_2"]


def constants():
    import numpy as np

    con = np.zeros((P, K_END), np.float32)
    con[:, K_ID:K_ID + P] = np.eye(P)
    con[:, K_TRI:K_TRI + P] = -np.tril(np.ones((P, P)))
    con[:, K_ONES:K_ONES + P] = -1.0
    sel = np.repeat(np.eye(ML_H), P, axis=1).astype(np.float32)
    hot = np.zeros((BUCKETS + 1, 2 * T), np.float32)
    exact = BUCKETS // 2
    for j in range(2 * T):
        n = T - 1 - j
        if n < 0:
            hot[BUCKETS, j] = MASKED
            continue
        far = exact + int(np.float32(np.log(np.float32(max(n, 1) / exact))) / np.float32(np.log(128 / exact))
                          * np.float32(BUCKETS - exact))
        hot[n if n < exact else min(far, BUCKETS - 1), j] = 1.0
    return {"con": con, "sel": sel, "hot": hot}


def kernel(**inputs):
    import numpy as np
    import concourse.bacc as bacc
    from concourse.bass_utils import run_bass_kernel_spmd

    nc = bacc.Bacc("TRN2", target_bir_lowering=False, num_devices=1)
    vector_rows = dict(VECS)
    arrays = {}
    arrays["vectors"] = np.concatenate([np.asarray(inputs[name]).reshape(n, P) for name, n in VECS])
    for name in INPUTS:
        if name in vector_rows:
            continue
        a = np.asarray(inputs[name])
        if name == "b_if":
            a = a.reshape(2, ML_H).T
        elif name == "lru_wa_2" or name == "lru_wx_2":
            a = a.reshape(a.shape[1:])
        elif name != "rel_bias_2":
            a = a.reshape(-1, a.shape[-1])
        arrays[name] = np.ascontiguousarray(a)
    arrays.update(constants())
    dram = {name: nc.dram_tensor("in_" + name, a.shape, F32, kind="ExternalInput").ap() for name, a in arrays.items()}
    out = nc.dram_tensor("out", (T, D), F32, kind="ExternalOutput").ap()
    build(nc, dram, out)
    r = run_bass_kernel_spmd(nc, [{"in_" + name: a for name, a in arrays.items()}], core_ids=[0])
    return r.results[0]["out"].reshape(1, T, D)
```
